# Optimizing a Trainium2 kernel written in Bass

```python
import jax, jax.numpy as jnp
from jax import lax
import numpy as np

D_MODEL = 1024
BATCH = 1
SEQ = 256
DEPTH = 1
DEC_BATCH = 1
DEC_SEQ = 1024
PAST_LEN = 512

GRID_W = 64
HEAD_DIM = 128
N_HEADS = D_MODEL // HEAD_DIM
N_KV_HEADS = N_HEADS // 4
Q_BLOCK = 128
ROPE_THETA = 10000.0
ATTN_W = N_HEADS * HEAD_DIM
KV_W = N_KV_HEADS * HEAD_DIM
POOL_WINDOWS = (2, 4, 8, 16)
POOL_GROUPS = len(POOL_WINDOWS)
POOL_W = D_MODEL // 2
POOL_GC = POOL_W // POOL_GROUPS
IN_W = ATTN_W + 2 * KV_W + POOL_W + 2 * D_MODEL
N_EXP_GROUPS = 4
EXP_PER_GROUP = 4
N_EXPERTS = N_EXP_GROUPS * EXP_PER_GROUP
TOP_K = 2
D_EXPERT = 256
EPS = 1e-6

kernel_name = "hybrid_diffusion_prefix_gqa_pool_hiermoe_step"

def rms_norm(x, g):
    xf = x.astype(jnp.float32)
    y = xf * lax.rsqrt(jnp.mean(xf * xf, axis=-1, keepdims=True) + EPS)
    return (y * g.astype(jnp.float32)).astype(x.dtype)

def axial_rope_tables(n_tokens):
    rows = n_tokens // GRID_W
    t = jnp.arange(rows * GRID_W)
    row = (t // GRID_W).astype(jnp.float32)
    col = (t % GRID_W).astype(jnp.float32)
    nf = HEAD_DIM // 4
    freq = ROPE_THETA ** (-jnp.arange(nf, dtype=jnp.float32) / nf)
    ang = jnp.concatenate([row[:, None] * freq, col[:, None] * freq], axis=-1)
    return jnp.cos(ang), jnp.sin(ang)

def apply_axial_rope(x, cos, sin):
    xf = x.astype(jnp.float32)
    half = HEAD_DIM // 2
    nf = half // 2
    c = cos[None, :, None, :]
    s = sin[None, :, None, :]

    def rot(xh, ch, sh):
        x1, x2 = xh[..., :nf], xh[..., nf:]
        return jnp.concatenate([x1 * ch - x2 * sh, x2 * ch + x1 * sh], axis=-1)

    xr = rot(xf[..., :half], c[..., :nf], s[..., :nf])
    xc = rot(xf[..., half:], c[..., nf:], s[..., nf:])
    return jnp.concatenate([xr, xc], axis=-1).astype(x.dtype)

def block_attention(q, k, v):
    b, lq = q.shape[0], q.shape[1]
    nb = lq // Q_BLOCK
    grp = N_HEADS // N_KV_HEADS
    qb = q.reshape(b, nb, Q_BLOCK, N_KV_HEADS, grp, HEAD_DIM).transpose(1, 0, 2, 3, 4, 5)
    scale = HEAD_DIM ** -0.5

    def one_block(qi):
        s = jnp.einsum('bqkgd,bskd->bkgqs', qi, k).astype(jnp.float32) * scale
        p = jax.nn.softmax(s, axis=-1).astype(v.dtype)
        return jnp.einsum('bkgqs,bskd->bqkgd', p, v)

    o = lax.map(one_block, qb)
    return o.transpose(1, 0, 2, 3, 4, 5).reshape(b, lq, ATTN_W)

def multiscale_pool(xp, w_pool, pool_scale):
    b, l, _ = xp.shape
    xf = xp.astype(jnp.float32)
    cs = jnp.concatenate([jnp.zeros((b, 1, POOL_W), jnp.float32), jnp.cumsum(xf, axis=1)], axis=1)
    t = jnp.arange(l)
    outs = []
    for gi, w in enumerate(POOL_WINDOWS):
        lo = jnp.clip(t - w // 2, 0, l)
        hi = jnp.clip(t + w // 2, 0, l)
        sl = slice(gi * POOL_GC, (gi + 1) * POOL_GC)
        csg = cs[:, :, sl]
        s = jnp.take(csg, hi, axis=1) - jnp.take(csg, lo, axis=1)
        cnt = (hi - lo).astype(jnp.float32)[None, :, None]
        outs.append(s / cnt - xf[:, :, sl])
    d = jnp.stack(outs, axis=2).astype(xp.dtype)
    y = jnp.einsum('blgc,gce->blge', d, w_pool).reshape(b, l, POOL_W)
    return y * pool_scale

def hierarchical_moe(h, w_rg, w_re, w_g, w_u, w_d):
    b, l, d = h.shape
    x = h.reshape(b * l, d)
    xf = x.astype(jnp.float32)
    g_logits = xf @ w_rg.astype(jnp.float32)
    p_group = jax.nn.softmax(g_logits, axis=-1)
    g_sel = jnp.argmax(g_logits, axis=-1)
    p_sel = jnp.take_along_axis(p_group, g_sel[:, None], axis=-1)
    e_logits = (xf @ w_re.astype(jnp.float32)).reshape(-1, N_EXP_GROUPS, EXP_PER_GROUP)
    e_in = jnp.take_along_axis(e_logits, g_sel[:, None, None], axis=1)[:, 0]
    top_v, top_i = lax.top_k(e_in, TOP_K)
    w_top = jax.nn.softmax(top_v, axis=-1) * p_sel
    eid = g_sel[:, None] * EXP_PER_GROUP + top_i
    gate = jnp.sum(jax.nn.one_hot(eid, N_EXPERTS, dtype=jnp.float32) * w_top[..., None], axis=1)
    hid = jax.nn.silu(jnp.einsum('td,edf->tef', x, w_g)) * jnp.einsum('td,edf->tef', x, w_u)
    hid = hid * gate[:, :, None].astype(hid.dtype)
    y = jnp.einsum('tef,efd->td', hid, w_d)
    return y.reshape(b, l, d)

def trunk_layer(x, cvec, rope, ctx_kv, lp):
    b, l, _ = x.shape
    mod = jnp.einsum('bd,de->be', jax.nn.silu(cvec), lp['w_ada']) + lp['b_ada']
    sh1, sc1, gt1, sh2, sc2, gt2 = jnp.split(mod[:, None, :], 6, axis=-1)
    h = rms_norm(x, lp['norm1_g']) * (1 + sc1) + sh1
    proj = h @ lp['w_in']
    cuts = [ATTN_W, ATTN_W + KV_W, ATTN_W + 2 * KV_W, ATTN_W + 2 * KV_W + POOL_W,
            ATTN_W + 2 * KV_W + POOL_W + D_MODEL]
    q, k, v, xp, ga, gb = jnp.split(proj, cuts, axis=-1)
    q = rms_norm(q.reshape(b, l, N_HEADS, HEAD_DIM), lp['q_norm_g'])
    k = rms_norm(k.reshape(b, l, N_KV_HEADS, HEAD_DIM), lp['k_norm_g'])
    v = v.reshape(b, l, N_KV_HEADS, HEAD_DIM)
    k_ctx_out, v_ctx_out = k, v
    if rope is not None:
        q = apply_axial_rope(q, rope[0], rope[1])
        k = apply_axial_rope(k, rope[0], rope[1])
    if ctx_kv is not None:
        k_all = jnp.concatenate([ctx_kv[0].astype(k.dtype), k], axis=1)
        v_all = jnp.concatenate([ctx_kv[1].astype(v.dtype), v], axis=1)
    else:
        k_all, v_all = k, v
    attn = block_attention(q, k_all, v_all)
    pool = multiscale_pool(xp, lp['w_pool'], lp['pool_scale'])
    merged = jax.nn.sigmoid(ga) * (attn @ lp['w_branch_a']) + jax.nn.sigmoid(gb) * (pool @ lp['w_branch_b'])
    x = x + gt1 * (merged @ lp['w_out'])
    h2 = rms_norm(x, lp['norm2_g']) * (1 + sc2) + sh2
    x = x + gt2 * hierarchical_moe(h2, lp['w_router_group'], lp['w_router_expert'],
                                   lp['w_exp_gate'], lp['w_exp_up'], lp['w_exp_down'])
    return x, k_ctx_out, v_ctx_out

def setup_inputs(seed: int = 0) -> dict:
    key = jax.random.key(seed)
    ks = jax.random.split(key, 26)
    f32 = jnp.float32
    nrm = lambda k, shape, s: jax.random.normal(k, shape, f32) * s
    return {
        'x_prompt': nrm(ks[0], (BATCH, SEQ, D_MODEL), 1.0),
        'x_sample': nrm(ks[1], (DEC_BATCH, DEC_SEQ, D_MODEL), 1.0),
        'cache_k': nrm(ks[2], (DEC_BATCH, DEPTH, PAST_LEN, N_KV_HEADS, HEAD_DIM), 1.0),
        'cache_v': nrm(ks[3], (DEC_BATCH, DEPTH, PAST_LEN, N_KV_HEADS, HEAD_DIM), 1.0),
        'c': nrm(ks[4], (DEC_BATCH, D_MODEL), 1.0),
        'c_ctx': nrm(ks[5], (D_MODEL,), 1.0),
        'norm1_g': 1.0 + nrm(ks[6], (DEPTH, D_MODEL), 0.02),
        'norm2_g': 1.0 + nrm(ks[7], (DEPTH, D_MODEL), 0.02),
        'w_ada': nrm(ks[8], (DEPTH, D_MODEL, 6 * D_MODEL), 0.5 * D_MODEL ** -0.5),
        'b_ada': nrm(ks[9], (DEPTH, 6 * D_MODEL), 0.02),
        'w_in': nrm(ks[10], (DEPTH, D_MODEL, IN_W), D_MODEL ** -0.5),
        'q_norm_g': 1.0 + nrm(ks[11], (DEPTH, HEAD_DIM), 0.02),
        'k_norm_g': 1.0 + nrm(ks[12], (DEPTH, HEAD_DIM), 0.02),
        'w_pool': nrm(ks[13], (DEPTH, POOL_GROUPS, POOL_GC, POOL_GC), POOL_GC ** -0.5),
        'pool_scale': 1.0 + nrm(ks[14], (DEPTH, POOL_W), 0.02),
        'w_branch_a': nrm(ks[15], (DEPTH, ATTN_W, D_MODEL), ATTN_W ** -0.5),
        'w_branch_b': nrm(ks[16], (DEPTH, POOL_W, D_MODEL), POOL_W ** -0.5),
        'w_out': nrm(ks[17], (DEPTH, D_MODEL, D_MODEL), D_MODEL ** -0.5),
        'w_router_group': nrm(ks[18], (DEPTH, D_MODEL, N_EXP_GROUPS), D_MODEL ** -0.5),
        'w_router_expert': nrm(ks[19], (DEPTH, D_MODEL, N_EXPERTS), D_MODEL ** -0.5),
        'w_exp_gate': nrm(ks[20], (DEPTH, N_EXPERTS, D_MODEL, D_EXPERT), D_MODEL ** -0.5),
        'w_exp_up': nrm(ks[21], (DEPTH, N_EXPERTS, D_MODEL, D_EXPERT), D_MODEL ** -0.5),
        'w_exp_down': nrm(ks[22], (DEPTH, N_EXPERTS, D_EXPERT, D_MODEL), D_EXPERT ** -0.5),
        'final_norm_g': 1.0 + nrm(ks[23], (D_MODEL,), 0.02),
    }

def reference(x_prompt, x_sample, cache_k, cache_v, c, c_ctx, norm1_g, norm2_g, w_ada, b_ada, w_in,
              q_norm_g, k_norm_g, w_pool, pool_scale, w_branch_a, w_branch_b, w_out,
              w_router_group, w_router_expert, w_exp_gate, w_exp_up, w_exp_down, final_norm_g):
    rope = axial_rope_tables(x_sample.shape[1])
    cvec_ctx = jnp.broadcast_to(c_ctx[None, :], (x_prompt.shape[0], D_MODEL))
    xp, xs = x_prompt, x_sample
    new_k, new_v = [], []
    for i in range(DEPTH):
        lp = {
            'norm1_g': norm1_g[i], 'norm2_g': norm2_g[i], 'w_ada': w_ada[i], 'b_ada': b_ada[i],
            'w_in': w_in[i], 'q_norm_g': q_norm_g[i], 'k_norm_g': k_norm_g[i],
            'w_pool': w_pool[i], 'pool_scale': pool_scale[i], 'w_branch_a': w_branch_a[i],
            'w_branch_b': w_branch_b[i], 'w_out': w_out[i], 'w_router_group': w_router_group[i],
            'w_router_expert': w_router_expert[i], 'w_exp_gate': w_exp_gate[i],
            'w_exp_up': w_exp_up[i], 'w_exp_down': w_exp_down[i],
        }
        xp, kc, vc = trunk_layer(xp, cvec_ctx, None, None, lp)
        new_k.append(kc)
        new_v.append(vc)
        xs, _, _ = trunk_layer(xs, c, rope, (cache_k[:, i], cache_v[:, i]), lp)
    y_prompt = rms_norm(xp, final_norm_g)
    y_sample = rms_norm(xs, final_norm_g)
    new_cache_k = jnp.stack(new_k, axis=1)
    new_cache_v = jnp.stack(new_v, axis=1)
    return (y_prompt, y_sample, new_cache_k, new_cache_v)


_drawn_inputs = setup_inputs


def setup_inputs(seed=0):
    import zlib

    import numpy as np

    out = dict(_drawn_inputs(seed))
    spreads = {}
    factors = {'cache_k': 8.0,
     'cache_v': 8.0,
     'norm1_g': 2.887,
     'norm2_g': 5.567,
     'q_norm_g': 8.0,
     'k_norm_g': 3.092,
     'pool_scale': 8.0,
     'final_norm_g': 2.902}
    for name, (base, spread) in spreads.items():
        noise = np.random.default_rng([zlib.crc32(name.encode()), seed]).standard_normal(out[name].shape)
        drawn = base * np.exp(spread * noise) if base else spread * noise
        out[name] = __import__('jax').numpy.asarray(drawn.astype(out[name].dtype))
    for name, factor in factors.items():
        out[name] = (out[name] * factor).astype(out[name].dtype)
    return out
```

```python
from collections import namedtuple
from contextlib import ExitStack

import numpy as np

import concourse.bass as bass
from concourse import mybir

ALU = mybir.AluOpType
ACT = mybir.ActivationFunctionType
AX = mybir.AxisListType
F32 = mybir.dt.float32
F32R = mybir.dt.float32r
I32 = mybir.dt.int32

P = 128
D = 1024
CTX, LAT, PAST = 256, 1024, 512
TOK = CTX + LAT
TILES = TOK // P
CTX_TILES = CTX // P
KC = D // P
HEADS, KV, HD = 8, 2, 128
GRP = HEADS // KV
KEYS = TOK + PAST
KEY_TILES = KEYS // P
LAT_KEYS = LAT + PAST
EG, EPG, NE, FE = 4, 4, 16, 256
NR = EG + NE
EPS = 1e-6
GRID_W, THETA = 64, 10000.0
PAIR = 2 * P
N_ADA = 6 * D // PAIR
GROUPS = [(0, 512), (512, 512), (1024, 256)]
STREAMS = [(0, CTX), (CTX, LAT)]
PADW = 8
XPW = 4 * PADW + TOK
XSEG = [(PADW, 0, CTX), (3 * PADW + CTX, CTX, LAT)]
HALF = TILES // 2
SLOTS = 36


Unit = namedtuple("Unit", "u kv tok par keys key0")


class Tally:

    def __init__(self, eng, sem):
        self.eng, self.sem, self.n, self.extra = eng, sem, 0, 0

    def step(self, ins):
        ins.then_inc(self.sem, 1)
        self.n += 1
        self.eng.wait_ge(self.sem, self.extra + self.n)

    def enter(self, i, per):
        self.start, self.per, self.extra = self.n, per, i * per

    def leave(self, count):
        assert self.n - self.start == self.per, (self.n - self.start, self.per)
        self.n, self.extra = self.start + self.per * count, 0


def build(nc, io, last_block=99):
    with ExitStack() as ctx:
        base = (nc.sbuf_base + 31) // 32 * 32

        def at(name, shape, dt, off):
            return nc.alloc_sbuf_tensor_at(name, shape, dt, offset=base + off)

        early = []
        passed = nc.alloc_semaphore("passed")

        def sem(name):
            early.append(nc.alloc_semaphore(name))
            return early[-1]

        KB = 1024
        RA, RHL, RKV, RW, RS, RC = 0, 40 * KB, 120 * KB, 176 * KB, 200 * KB, 205 * KB
        psum = ctx.enter_context(nc.psum_tensor("psum", [P, 4096], F32))

        small_at = [RC]

        def small(name, shape):
            n = 4 * int(np.prod(shape[1:]))
            small_at[0] += (n + 31) // 32 * 32
            return at(name, shape, F32, small_at[0] - (n + 31) // 32 * 32)
        ident = small("ident", [P, P])
        ones = small("ones", [P, P])
        cc = small("cc", [P, KC, 2])
        cs = small("cs", [P, KC, 2])
        vecs = small("vecs", [P, 70])
        mods = small("mods", [P, 48, 2])
        m1 = small("m1", [P, KC, 2])
        m2 = small("m2", [P, KC, 2])
        eps = small("eps", [P, 1])
        ssq = small("ssq", [P, TILES])
        rstd = small("rstd", [P, TILES])
        rt = small("rt", [P, TILES])
        nsq = small("nsq", [P, TILES])
        ntmp = small("ntmp", [P, TILES])
        rmax = small("rmax", [P, 4])
        nmax = small("nmax", [P, 2, GRP])
        esum = small("esum", [P, 2, GRP])
        gate1 = small("gate1", [P, 4])
        einv = small("einv", [P, 2, GRP])

        h_hi = at("h_hi", [P, KC, TOK], F32R, RHL)
        h_lo = at("h_lo", [P, KC, TOK], F32R, RHL + 40 * KB)
        xt = at("xt", [P, TILES, D], F32, RA)
        xnT = at("xnT", [P, KC, TOK], F32, RKV)
        ada = [at(f"ada{j}", [P, KC, PAIR], F32, RKV + (40 + 8 * j) * KB) for j in range(2)]
        ada_raw = ada + [at(f"ada_raw{j}", [P, KC, PAIR], F32, RHL + (40 + 8 * j) * KB) for j in range(4)]
        w_raw = at("w_raw", [P, KC, PAIR], F32, RW)
        w_hi = [at(f"w_hi{j}", [P, KC, P], F32R, RW + (8 + 8 * j) * KB) for j in range(2)]
        w_lo = [at(f"w_lo{j}", [P, KC, P], F32R, RW + (12 + 8 * j) * KB) for j in range(2)]
        stage = at("stage", [P, TOK], F32, RS)
        cs4 = at("cs4", [P, KC, P], F32R, RS)
        sq_junk = at("sq_junk", [P, D], F32, RHL + 32 * KB)
        ada_hi = [at(f"ada_hi{j}", [P, KC, PAIR], F32R, o) for j, o in enumerate((RHL, RHL + 8 * KB, RKV + 20 * KB))]
        ada_lo = [at(f"ada_lo{j}", [P, KC, PAIR], F32R, o) for j, o in enumerate((RHL + 16 * KB, RHL + 24 * KB, RKV + 28 * KB))]
        ada_rows = [at(f"ada_rows{j}", [P, PAIR], F32, o) for j, o in enumerate((RHL + 36 * KB, RHL + 37 * KB, RKV + 36 * KB, RKV + 37 * KB))]
        xpad = [at(f"xpad{j}", [P, XPW], F32, RA + 5376 * j) for j in range(2)]
        win = [at(f"win{j}", [P, XPW], F32, RA + 5376 * (2 + j)) for j in range(2)]
        icnt = at("icnt", [P, TOK], F32, RA + 5376 * 4)
        wpool = at("wpool", [P, 4, P], F32, RA + 27 * KB)
        gst = [at(f"gst{j}", [P, TOK], F32, RA + (30 + 5 * j) * KB) for j in range(2)]
        dpool = at("dpool", [P, 4, TOK], F32, RKV)
        qT = at("qT", [P, HEADS, TOK], F32, RA)
        cos = at("cos", [P, LAT], F32, RKV + 28 * KB)
        sin = at("sin", [P, LAT], F32, RKV + 32 * KB)
        rtmp = at("rtmp", [P, LAT], F32, RKV + 36 * KB)
        sq = [at(f"sq{j}", [P, TOK], F32, RKV + (40 + 5 * j) * KB) for j in range(2)]
        rsb = at("rsb", [P, TOK], F32, RKV + 50 * KB)
        kT_hi = at("kT_hi", [P, KV, KEYS], F32R, RKV)
        kT_lo = at("kT_lo", [P, KV, KEYS], F32R, RKV + 14 * KB)
        vals = at("vals", [P, KEY_TILES, KV * HD], F32, RKV + 28 * KB)
        kraw = [stage, at("kraw1", [P, TOK], F32, RKV + 40 * KB)]
        vraw = [stage, at("vraw1", [P, TOK], F32, RHL)]
        kc_raw = at("kc_raw", [P, KV, PAST], F32, RHL + 8 * KB)

        s = {}
        for n in ("eps_r x_ss rs_used consts rope wpool_in icnt_in x_sq x_scaled xT_ps xT_outa xT_outd c_in c_sig c_silu ada_mm0 ada_mm1 ada_hi_r0 ada_hi_r1 ada_lo_p0 ada_lo_p1 ada_lo_r0 ada_lo_r1 ada_rows0 ada_rows1 ada_turn mods_r0 mods_r1 ada_in0 ada_in1 "
                  "mods_b h_raw h_hi_r h_lo_p h_lo_d w_in0 w_hi0 w_hi1 w_lo0 w_lo1 mm0 mm1 ps_free0 ps_free1 pad0 xp_in xp_used "
                  "d_done gate_r0 gate_r1 gate_st0 gate_st1 py_ps py_out py_st sq_r0 sq_r1 ss_mm rt_sq rt_r rs_mm rs_out q_raw q_sin q_cos q_fin "
                  "k_fin k_hi k_lo kout v_raw vout v_ps v_out_a v_out_d cache_in cache_hi cache_lo dve_c").split():
            s[n] = sem("b1_" + n)
        x_in = [sem(f"x_in{t}") for t in range(TILES)]
        ada_first = [sem(f"ada_first{b}") for b in range(8)]

        XP_PAIRS, GATE_PAIRS, Q_PAIRS = 2, 8, 4
        G0, Q0, K0, V0 = 2, 10, 14, 15
        N_PAIRS = 16
        def pass_wait(pool):
            pool.sem_inc(passed, 1)
        par_sets = (0, 1536)
        AUX = (3072, 3584)
        rows_at = (3072, 2048, 3072, 3072)

        def v_chunk(n):
            j, (g, w) = n // 3, GROUPS[n % 3]
            return (vals[:, g // P:(g + w) // P, j * HD:(j + 1) * HD],
                    psum[:, AUX[n % 2]:AUX[n % 2] + w].rearrange("p (t d) -> p t d", d=P))

        with nc.Block() as block:
            @block.sync
            def _(sp):
                sp.dma_start(cc[:], io["cvec"]).then_inc(s["c_in"], 16)
                sp.dma_start(vecs[:], io["vecs"]).then_inc(s["consts"], 16)
                sp.dma_start(ident[:], io["ident"]).then_inc(s["consts"], 16)
                for t in range(TILES):
                    sp.dma_start(xt[:, t, :], io["x"][t]).then_inc(x_in[t], 16)
                for b in range(8):
                    if b >= 6:
                        sp.wait_ge(s[f"ada_lo_r{b % 2}"], 1)
                        sp.wait_ge(s[f"ada_lo_p{b % 2}"], 1)
                    sp.dma_start(ada_raw[b % 6][:], io["w_ada"][b]).then_inc(ada_first[b], 16)
                    if b == 4:
                        sp.dma_start(w_raw[:], io["w_in"][0]).then_inc(s["w_in0"], 16)

                def load_w(n):
                    sp.wait_ge(s["w_lo1"], n)
                    sp.dma_start(w_raw[:], io["w_in"][bass.ds(n, 1)].rearrange("o p k n -> p (o k) n")).then_inc(s["w_in0"], 16)
                def load_ada(n, j):
                    sp.wait_ge(s[f"ada_lo_r{j}"], n)
                    sp.dma_start(ada[j][:], io["w_ada"][bass.ds(2 * n + j, 1)].rearrange("o p k n -> p (o k) n")).then_inc(s[f"ada_in{j}"], 16)

                load_w(1)
                load_ada(4, 0)
                load_ada(4, 1)
                sp.wait_ge(s["xT_ps"], TILES)
                sp.dma_start(wpool[:], io["w_pool"]).then_inc(s["wpool_in"], 16)
                for c in range(4):
                    if c:
                        sp.wait_ge(s["xp_used"], c)
                    sp.dma_start(icnt[:], io["icnt"][c:c + 1, :].broadcast_to([P, TOK])).then_inc(s["icnt_in"], 16)
                    if c == 1:
                        load_w(2)

                def store_gate(i, j):
                    sp.wait_ge(s[f"gate_r{j}"], i + 1)
                    sp.dma_start(io["gates"][bass.ds(2 * i + j, 1)].rearrange("o p n -> p (o n)"), gst[j][:]).then_inc(s[f"gate_st{j}"], 16)
                with sp.Fori(0, GATE_PAIRS - 1) as i:
                    load_w(i + G0 + 1)
                    load_ada(i + 5, 0)
                    store_gate(i, 0)
                    load_ada(i + 5, 1)
                    store_gate(i, 1)
                load_w(Q0)
                store_gate(GATE_PAIRS - 1, 0)
                store_gate(GATE_PAIRS - 1, 1)
                for c in range(4):
                    sp.wait_ge(s["py_out"], 3 * (c + 1))
                    sp.dma_start(io["poolT"][c], sq[c % 2][:]).then_inc(s["py_st"], 16)
                    sp.wait_ge(s["py_st"], 16 * (c + 1))
                    if c == 0:
                        sp.wait_ge(s["d_done"], 4)
                        sp.dma_start(cos[:], io["cos"]).then_inc(s["rope"], 16)
                        sp.dma_start(sin[:], io["sin"]).then_inc(s["rope"], 16)
                with sp.Fori(0, Q_PAIRS) as i:
                    load_w(i + Q0 + 1)
                load_w(V0)
                for j in range(2):
                    sp.wait_ge(s["q_raw"], HEADS + j + 1)
                    sp.dma_start(io["out_k"][j], kraw[j][:, 0:CTX]).then_inc(s["kout"], 16)
                for j in range(2):
                    sp.wait_ge(s["v_raw"], j + 1)
                    if j == 1:
                        sp.dma_start(kc_raw[:], io["cache_k"]).then_inc(s["cache_in"], 16)
                        sp.wait_ge(s["k_fin"], 2)
                        sp.dma_start(vals[:, TILES:KEY_TILES, :], io["cache_v"]).then_inc(s["cache_in"], 16)
                    sp.dma_start(io["out_v"][j], vraw[j][:, 0:CTX]).then_inc(s["vout"], 16)
                sp.wait_ge(s["kout"], 32)
                sp.wait_ge(s["vout"], 32)
                for j in range(2):
                    sp.wait_ge(s[f"gate_st{j}"], 16 * GATE_PAIRS)
                sp.wait_ge(s["cache_in"], 32)

            @block.tensor
            def _(pe):
                for t in range(TILES):
                    pe.wait_ge(s["x_scaled"], t + 1)
                    if t == 0:
                        pe.wait_ge(s["consts"], 32)
                    if t >= 2:
                        pe.wait_ge(s["xT_outa"], t - 1)
                        pe.wait_ge(s["xT_outd"], t - 1)
                    for k in range(KC):
                        o = (t % 2) * 1024 + k * P
                        mm = pe.transpose(psum[:, o:o + P], xt[:, t, k * P:(k + 1) * P], ident[:])
                    mm.then_inc(s["xT_ps"], 1)

                def ada_block(n, j, buf):
                    pe.wait_ge(s[f"ada_lo_r{j}"], n + 1)
                    if buf < 2:
                        pe.wait_ge(s[f"ada_lo_p{j}"], n + 1)
                    if buf < 2:
                        pe.wait_ge(s[f"ada_rows{j}"], n)
                    else:
                        pe.wait_ge(s[f"ada_rows{1 - j}"], n + j)
                    for part in (ada_hi, ada_lo):
                        for k in range(KC):
                            mm = pe.matmul(psum[:, rows_at[buf]:rows_at[buf] + PAIR], cs4[:, k, :], part[buf][:, k, :],
                                           start=(k == 0 and part is ada_hi), stop=(k == KC - 1 and part is ada_lo))
                    mm.then_inc(s[f"ada_mm{j}"], 1)

                def ada_turn(n, j, buf):
                    pe.wait_ge(s[f"ada_rows{j}"], n + 1)
                    if j:
                        pe.wait_ge(s["mods_r0"], n + 1)
                    else:
                        pe.wait_ge(s["mods_r1"], n)
                    for m in range(2):
                        mm = pe.transpose(psum[:, AUX[1] + m * P:AUX[1] + (m + 1) * P], ada_rows[buf][:, m * P:(m + 1) * P], ident[:])
                    mm.then_inc(s["ada_turn"], 1)

                pe.wait_ge(s["c_silu"], 1)
                for b in range(9):
                    if b < 8:
                        ada_block(b // 2, b % 2, b % 2)
                    if b:
                        ada_turn((b - 1) // 2, (b - 1) % 2, (b - 1) % 2)

                def project(n, j, first=False, hooks={}):
                    pe.wait_ge(s[f"w_hi{j}"], n + 1)
                    pe.wait_ge(s[f"w_lo{j}"], n + 1)
                    pe.wait_ge(s[f"ps_free{j}"], n)
                    for k in range(KC):
                        if first:
                            pe.wait_ge(s["h_hi_r"], k + 1)
                            pe.wait_ge(s["h_lo_p"] if k % 2 else s["h_lo_d"], k // 2 + 1)
                        for a, b in ((w_hi, h_hi), (w_hi, h_lo), (w_lo, h_hi)):
                            for g, w in GROUPS:
                                mm = pe.matmul(psum[:, par_sets[j] + g:par_sets[j] + g + w], a[j][:, k, :], b[:, k, g:g + w],
                                               start=(k == 0 and a is w_hi and b is h_hi), stop=(k == KC - 1 and a is w_lo))
                        if k in hooks:
                            hooks[k]()
                    mm.then_inc(s[f"mm{j}"], 1)

                pe.wait_ge(s["xT_outa"], TILES)
                pe.wait_ge(s["xT_outd"], TILES)
                for n in range(XP_PAIRS):
                    project(n, 0, first=(n == 0))
                    project(n, 1)
                with pe.Fori(0, GATE_PAIRS) as i:
                    for j in range(2):
                        project(i + G0, j, hooks={4: lambda: ada_block(i + 4, j, 2), 7: lambda: ada_turn(i + 4, j, 2 + j)})
                pe.wait_ge(s["wpool_in"], 16)
                pe.wait_ge(s["d_done"], 4)
                pe.wait_ge(s["mods_b"], 1)
                for c in range(4):
                    for q, (g, w) in enumerate(GROUPS):
                        n = 3 * c + q
                        if n >= 2:
                            pe.wait_ge(s["py_out"], n - 1)
                        pe.matmul(psum[:, AUX[n % 2]:AUX[n % 2] + w], wpool[:, c, :], dpool[:, c, g:g + w],
                                  start=True, stop=True).then_inc(s["py_ps"], 1)
                pe.wait_ge(s["py_out"], 12)

                def sums(n, j):
                    pe.wait_ge(s[f"sq_r{j}"], n + 1)
                    for t in range(TILES):
                        a = par_sets[j] + TOK + t
                        mm = pe.matmul(psum[:, a:a + 96], sq[j][:, t * P:(t + 1) * P], ones[:, 0:96], start=True, stop=True)
                    mm.then_inc(s["ss_mm"], 1)

                def spread(n, j):
                    pe.wait_ge(s["rt_r"], 2 * n + j + 1)
                    pe.wait_ge(s["rs_out"], 2 * (2 * n + j))
                    for t in range(TILES):
                        a = par_sets[j] + TOK + t * P if t < CTX_TILES else AUX[0] + (t - CTX_TILES) * P
                        mm = pe.transpose(psum[:, a:a + P], rt[:, t:t + 1].broadcast_to([P, P]), ident[:])
                    mm.then_inc(s["rs_mm"], 1)

                def hooks(n, j):
                    return {2: lambda: sums(n, j), 5: lambda: spread(n, j)}
                project(Q0, 0)
                with pe.Fori(0, Q_PAIRS) as i:
                    project(i + Q0, 1, hooks=hooks(i, 0))
                    project(i + Q0 + 1, 0, hooks=hooks(i, 1))
                project(K0, 1, hooks=hooks(4, 0))
                project(V0, 0, hooks=hooks(4, 1))
                project(V0, 1)
                for j in range(2):
                    pe.wait_ge(s["v_raw"], j + 1)
                    for q, (g, w) in enumerate(GROUPS):
                        n = 3 * j + q
                        if n == 0:
                            pe.wait_ge(s["rs_out"], 20)
                        if n >= 2:
                            pe.wait_ge(s["v_out_d" if n % 2 else "v_out_a"], n // 2)
                        for r in range(w // P):
                            mm = pe.transpose(psum[:, AUX[n % 2] + r * P:AUX[n % 2] + (r + 1) * P],
                                              vraw[j][:, g + r * P:g + (r + 1) * P], ident[:])
                        mm.then_inc(s["v_ps"], 1)

            @block.scalar
            def _(act):
                def act_out(t):
                    act.wait_ge(s["xT_ps"], t + 1)
                    nc.scalar.copy(xnT[:, 0:4, t * P:(t + 1) * P],
                                   psum[:, (t % 2) * 1024:(t % 2) * 1024 + 512].rearrange("p (k n) -> p k n", n=P)).then_inc(s["xT_outa"], 1)

                act.wait_ge(s["c_in"], 16)
                act.wait_ge(s["eps_r"], 1)
                nc.scalar.activation(cs[:], cc[:], ACT.Sigmoid).then_inc(s["c_sig"], 1)
                for t in range(TILES):
                    act.wait_ge(x_in[t], 16)
                    if t:
                        act.wait_ge(s["x_ss"], t)
                    nc.scalar.activation(sq_junk[:], xt[:, t, :], ACT.Square, accum_out=ssq[:, t:t + 1]).then_inc(s["x_ss"], 1)
                    if t % HALF == HALF - 1:
                        act.wait_ge(s["x_ss"], t + 1)
                        h = slice(t + 1 - HALF, t + 1)
                        nc.scalar.activation(rstd[:, h], ssq[:, h], ACT.Sqrt, bias=eps[:], scale=1.0 / D).then_inc(s["x_sq"], 1)
                for t in range(TILES):
                    act_out(t)

                for b in range(8):
                    act.wait_ge(ada_first[b], 16)
                    act.wait_ge(s[f"ada_mm{b % 2}"], b // 2)
                    nc.scalar.copy(ada_hi[b % 2][:], ada_raw[b % 6][:]).then_inc(s[f"ada_hi_r{b % 2}"], 1)

                def split(n, j):
                    act.wait_ge(s["w_in0"], 16 * (n + 1))
                    act.wait_ge(s[f"mm{j}"], n)
                    nc.scalar.copy(w_hi[j][:], w_raw[:, :, j * P:(j + 1) * P]).then_inc(s[f"w_hi{j}"], 1)
                split(0, 0)
                split(0, 1)
                for k in range(KC):
                    act.wait_ge(s["h_raw"], k + 1)
                    nc.scalar.copy(h_hi[:, k, :], xnT[:, k, :]).then_inc(s["h_hi_r"], 1)
                for n in range(XP_PAIRS):
                    for j in range(2):
                        act.wait_ge(s[f"mm{j}"], n + 1)
                        act.wait_ge(s["pad0"], 6)
                        if n:
                            act.wait_ge(s["d_done"], j + 1)
                        for (o, g, w) in XSEG:
                            ins = nc.scalar.copy(xpad[j][:, o:o + w], psum[:, par_sets[j] + g:par_sets[j] + g + w])
                            ins.then_inc(s["xp_in"], 1)
                        act.wait_ge(s["xp_in"], 2 * (2 * n + j + 1))
                        act.sem_inc(s[f"ps_free{j}"], 1)
                        split(n + 1, j)
                with act.Fori(0, GATE_PAIRS) as i:
                    for j in range(2):
                        act.wait_ge(s[f"mm{j}"], i + G0 + 1)
                        act.wait_ge(s[f"gate_st{j}"], 16 * i)
                        nc.scalar.activation(gst[j][:], psum[:, par_sets[j]:par_sets[j] + TOK], ACT.Sigmoid).then_inc(s[f"gate_r{j}"], 1)
                        act.wait_ge(s[f"gate_r{j}"], i + 1)
                        act.sem_inc(s[f"ps_free{j}"], 1)
                        split(i + G0 + 1, j)
                for c in range(4):
                    for q, (g, w) in enumerate(GROUPS):
                        n = 3 * c + q
                        act.wait_ge(s["py_ps"], n + 1)
                        if c >= 2:
                            act.wait_ge(s["py_st"], 16 * (c - 1))
                        nc.scalar.mul(sq[c % 2][:, g:g + w], psum[:, AUX[n % 2]:AUX[n % 2] + w],
                                      vecs[:, 66 + c:67 + c]).then_inc(s["py_out"], 1)

                def square(n, j):
                    act.wait_ge(s[f"mm{j}"], n + Q0 + 1)
                    if j == 0:
                        act.wait_ge(s["ss_mm"], 2 * n)
                    else:
                        act.wait_ge(s["ss_mm"], 2 * n + 1)
                    nc.scalar.activation(sq[j][:], psum[:, par_sets[j]:par_sets[j] + TOK], ACT.Square).then_inc(s[f"sq_r{j}"], 1)

                def root(n, j):
                    act.wait_ge(s["ss_mm"], 2 * n + j + 1)
                    act.wait_ge(s["rs_mm"], 2 * n + j)
                    nc.scalar.activation(rt[:], psum[:, par_sets[j] + TOK:par_sets[j] + TOK + TILES], ACT.Sqrt,
                                         bias=eps[:], scale=1.0 / HD).then_inc(s["rt_sq"], 1)
                    act.wait_ge(s["rs_mm"], 2 * n + j + 1)
                    act.wait_ge(s["rs_used"], 2 * n + j)
                    nc.scalar.copy(rsb[:, 0:CTX], psum[:, par_sets[j] + TOK:par_sets[j] + TOK + CTX]).then_inc(s["rs_out"], 1)
                    nc.scalar.copy(rsb[:, CTX:TOK], psum[:, AUX[0]:AUX[0] + LAT]).then_inc(s["rs_out"], 1)
                act.wait_ge(s["py_st"], 64)
                with act.Fori(0, Q_PAIRS) as i:
                    for j in range(2):
                        square(i, j)
                        split(i + Q0 + 1, j)
                        root(i, j)
                for j in range(2):
                    square(4, j)
                    split(V0, j)
                    root(4, j)
                for j in range(2):
                    act.wait_ge(s["k_fin"], j + 1)
                    nc.scalar.copy(kT_hi[:, j, 0:TOK], kraw[j][:]).then_inc(s["k_hi"], 1)
                act.wait_ge(s["k_lo"], 2)
                act.wait_ge(s["kout"], 32)
                for j in range(2):
                    act.wait_ge(s[f"mm{j}"], V0 + 1)
                    if j == 1:
                        act.wait_ge(s["mm1"], V0 + 1)
                    nc.scalar.copy(vraw[j][:], psum[:, par_sets[j]:par_sets[j] + TOK]).then_inc(s["v_raw"], 1)
                act.wait_ge(s["q_fin"], HEADS)
                act.wait_ge(s["k_fin"], 2)
                for n in range(0, 6, 2):
                    act.wait_ge(s["v_ps"], n + 1)
                    nc.scalar.copy(*v_chunk(n)).then_inc(s["v_out_a"], 1)
                act.wait_ge(s["cache_in"], 32)
                nc.scalar.copy(kT_hi[:, :, TOK:KEYS], kc_raw[:]).then_inc(s["cache_hi"], 1)

            @block.gpsimd
            def _(pool):
                for b in range(8):
                    j = b % 2
                    pool.wait_ge(s[f"ada_hi_r{j}"], b // 2 + 1)
                    pool.wait_ge(s[f"ada_mm{j}"], b // 2)
                    nc.gpsimd.tensor_tensor(ada_lo[j][:, 6:8, :], ada_raw[b % 6][:, 6:8, :], ada_hi[j][:, 6:8, :], ALU.subtract).then_inc(s[f"ada_lo_p{j}"], 1)

                def split(n, j):
                    pool.wait_ge(s[f"w_hi{j}"], n + 1)
                    nc.gpsimd.tensor_tensor(w_lo[j][:], w_raw[:, :, j * P:(j + 1) * P], w_hi[j][:], ALU.subtract).then_inc(s[f"w_lo{j}"], 1)
                split(0, 0)
                split(0, 1)
                for k in range(1, KC, 2):
                    pool.wait_ge(s["h_hi_r"], k + 1)
                    nc.gpsimd.tensor_tensor(h_lo[:, k, :], xnT[:, k, :], h_hi[:, k, :], ALU.subtract).then_inc(s["h_lo_p"], 1)
                for n in range(1, G0 + 1):
                    split(n, 0)
                    split(n, 1)
                with pool.Fori(0, GATE_PAIRS) as i:
                    split(i + G0 + 1, 0)
                    split(i + G0 + 1, 1)
                with pool.Fori(0, Q_PAIRS) as i:
                    for j in range(2):
                        split(i + Q0 + 1, j)
                        pool.wait_ge(s["q_sin"], 2 * i + j + 1)
                        q_lat = qT[:, bass.ds(2 * i + j, 1), CTX:TOK].rearrange("p o n -> p (o n)")
                        nc.gpsimd.tensor_tensor(q_lat, q_lat, cos[:], ALU.mult).then_inc(s["q_cos"], 1)
                for j in range(2):
                    split(V0, j)
                    pool.wait_ge(s["q_sin"], HEADS + j + 1)
                    nc.gpsimd.tensor_tensor(kraw[j][:, CTX:TOK], kraw[j][:, CTX:TOK], cos[:], ALU.mult).then_inc(s["q_cos"], 1)
                for j in range(2):
                    pool.wait_ge(s["k_hi"], j + 1)
                    nc.gpsimd.tensor_tensor(kT_lo[:, j, 0:TOK], kraw[j][:], kT_hi[:, j, 0:TOK], ALU.subtract).then_inc(s["k_lo"], 1)
                pool.wait_ge(s["cache_hi"], 1)
                nc.gpsimd.tensor_tensor(kT_lo[:, :, TOK:KEYS], kc_raw[:], kT_hi[:, :, TOK:KEYS], ALU.subtract).then_inc(s["cache_lo"], 1)

            @block.vector
            def _(dve):
                own = Tally(dve, s["dve_c"])

                def inverse(r, a, t):
                    own.step(nc.vector.reciprocal(r, r))
                    own.step(nc.vector.tensor_tensor(t, r, r, ALU.mult))
                    own.step(nc.vector.tensor_tensor(t, t, a, ALU.mult))
                    own.step(nc.vector.tensor_scalar(t, t, -0.5, 1.5, ALU.mult, ALU.add))
                    own.step(nc.vector.tensor_tensor(r, r, t, ALU.mult))
                own.step(nc.vector.memset(eps[:], EPS))
                dve.sem_inc(s["eps_r"], 1)
                own.step(nc.vector.memset(ones[:], 1.0))
                dve.wait_ge(s["c_sig"], 1)
                own.step(nc.vector.tensor_tensor(cs[:], cs[:], cc[:], ALU.mult))
                parts = cs4[:].rearrange("p k (r q z) -> p k r q z", q=2, z=2)
                silu = cs[:].unsqueeze(2).broadcast_to([P, KC, P // 4, 2])
                own.step(nc.vector.tensor_copy(parts[:, :, :, 0, :], silu))
                own.step(nc.vector.tensor_tensor(parts[:, :, :, 1, :], silu, parts[:, :, :, 0, :], ALU.subtract))
                dve.sem_inc(s["c_silu"], 1)
                dve.wait_ge(s["consts"], 32)

                def dve_out(t):
                    dve.wait_ge(s["xT_ps"], t + 1)
                    nc.vector.tensor_copy(xnT[:, 4:8, t * P:(t + 1) * P],
                                          psum[:, (t % 2) * 1024 + 512:(t % 2) * 1024 + 1024].rearrange("p (k n) -> p k n", n=P)).then_inc(s["xT_outd"], 1)
                for t in range(TILES):
                    if t % HALF == 0:
                        h = slice(t, t + HALF)
                        dve.wait_ge(s["x_sq"], t // HALF + 1)
                        own.step(nc.vector.tensor_scalar(nsq[:, h], ssq[:, h], 1.0 / D, EPS, ALU.mult, ALU.add))
                        inverse(rstd[:, h], nsq[:, h], ntmp[:, h])
                    r = rstd[:, t:t + 1]
                    nc.vector.tensor_scalar(xt[:, t, :], xt[:, t, :], r, None, ALU.mult).then_inc(s["x_scaled"], 1)
                    if t:
                        dve_out(t - 1)
                dve_out(TILES - 1)

                def rows_out(n, j, buf):
                    dve.wait_ge(s[f"ada_mm{j}"], n + 1)
                    nc.vector.tensor_copy(ada_rows[buf][:], psum[:, rows_at[buf]:rows_at[buf] + PAIR]).then_inc(s[f"ada_rows{j}"], 1)

                def take_mods(n, j):
                    dve.wait_ge(s["ada_turn"], 2 * n + j + 1)
                    turned = psum[:, AUX[1]:AUX[1] + PAIR].rearrange("p (m r) -> p m r", m=2)
                    m = mods[:, bass.ds(4 * n + 2 * j, 2), :]
                    own.step(nc.vector.tensor_tensor(m, turned[:, :, 2:4], vecs[:, bass.ds(4 * n + 2 * j, 2)].unsqueeze(2).broadcast_to([P, 2, 2]), ALU.add))
                    own.step(nc.vector.tensor_tensor(m, m, turned[:, :, 0:2], ALU.add))
                    dve.sem_inc(s[f"mods_r{j}"], 1)

                def norm_gain(m, a, g):
                    own.step(nc.vector.tensor_scalar(m[:], mods[:, a:a + KC, :], 1.0, None, ALU.add))
                    own.step(nc.vector.tensor_tensor(m[:], m[:], vecs[:, g:g + KC].unsqueeze(2).broadcast_to([P, KC, 2]), ALU.mult))
                for b in range(10):
                    if b < 8:
                        j = b % 2
                        dve.wait_ge(s[f"ada_hi_r{j}"], b // 2 + 1)
                        dve.wait_ge(s[f"ada_mm{j}"], b // 2)
                        nc.vector.tensor_tensor(ada_lo[j][:, 0:6, :], ada_raw[b % 6][:, 0:6, :], ada_hi[j][:, 0:6, :], ALU.subtract).then_inc(s[f"ada_lo_r{j}"], 1)
                    if 1 <= b < 9:
                        rows_out((b - 1) // 2, (b - 1) % 2, (b - 1) % 2)
                    if b >= 2:
                        take_mods((b - 2) // 2, b % 2)
                norm_gain(m1, KC, 48)
                dve.wait_ge(s["xT_outa"], TILES)
                dve.wait_ge(s["xT_outd"], TILES)
                for k in range(KC + 1):
                    if k < KC:
                        for q, (g, w) in enumerate(STREAMS):
                            v = xnT[:, k, g:g + w]
                            ins = nc.vector.tensor_scalar(v, v, m1[:, k, q:q + 1], mods[:, k, q:q + 1], ALU.mult, ALU.add)
                            if q == 0:
                                own.step(ins)
                        ins.then_inc(s["h_raw"], 1)
                    if k % 2:
                        dve.wait_ge(s["h_hi_r"], k)
                        nc.vector.tensor_tensor(h_lo[:, k - 1, :], xnT[:, k - 1, :], h_hi[:, k - 1, :], ALU.subtract).then_inc(s["h_lo_d"], 1)
                dve.wait_ge(s["xT_ps"], TILES)
                for j in range(2):
                    for a, b in ((0, PADW), (PADW + CTX, 3 * PADW + CTX), (XPW - PADW, XPW)):
                        nc.vector.memset(xpad[j][:, a:b], 0.0).then_inc(s["pad0"], 1)
                dve.wait_ge(s["pad0"], 6)
                dve.wait_ge(s["h_lo_p"], 4)

                def ada_split(n, j):
                    dve.wait_ge(s[f"ada_in{j}"], 16 * (n - 3))
                    dve.wait_ge(s[f"ada_mm{1 - j}"], n + j)
                    own.step(nc.vector.tensor_copy(ada_hi[2][:], ada[j][:]))
                    nc.vector.tensor_tensor(ada_lo[2][:], ada[j][:], ada_hi[2][:], ALU.subtract).then_inc(s[f"ada_lo_r{j}"], 1)
                ada_split(4, 0)
                for c in range(4):
                    j = c % 2
                    dve.wait_ge(s["xp_in"], 2 * (c + 1))
                    src = xpad[j]
                    lo, hi = 1, XPW
                    own.step(nc.vector.tensor_tensor(win[0][:, 1:XPW], src[:, 0:XPW - 1], src[:, 1:XPW], ALU.add))
                    src, sh = win[0], 1
                    for d in range(c):
                        dst = win[(d + 1) % 2]
                        lo, hi = lo + sh, hi - sh
                        own.step(nc.vector.tensor_tensor(dst[:, lo:hi], src[:, lo - sh:hi - sh], src[:, lo + sh:hi + sh], ALU.add))
                        src, sh = dst, 2 * sh
                    dve.wait_ge(s["icnt_in"], 16 * (c + 1))
                    for (o, g, w) in XSEG:
                        ins = nc.vector.tensor_tensor(dpool[:, c, g:g + w], src[:, o:o + w], icnt[:, g:g + w], ALU.mult)
                        ins.then_inc(own.sem, 1)
                        own.n += 1
                    dve.wait_ge(own.sem, own.n)
                    dve.sem_inc(s["xp_used"], 1)
                    for (o, g, w) in XSEG:
                        ins = nc.vector.tensor_tensor(dpool[:, c, g:g + w], dpool[:, c, g:g + w], xpad[j][:, o:o + w], ALU.subtract)
                        own.step(ins)
                    dve.sem_inc(s["d_done"], 1)
                with dve.Fori(0, GATE_PAIRS - 1) as i:
                    own.enter(i, 6)
                    for j in range(2):
                        rows_out(i + 4, j, 2 + j)
                        take_mods(i + 4, j)
                        ada_split(i + 4 + j, 1 - j)
                    own.leave(GATE_PAIRS - 1)
                rows_out(11, 0, 2)
                take_mods(11, 0)
                ada_split(11, 1)
                rows_out(11, 1, 3)
                take_mods(11, 1)
                norm_gain(m2, 4 * KC, 56)
                dve.sem_inc(s["mods_b"], 1)

                def norm_rope(n, j, dst_all, dst_parts):
                    dve.wait_ge(s["rt_sq"], 2 * n + j + 1)
                    own.step(nc.vector.tensor_scalar(nsq[:], psum[:, par_sets[j] + TOK:par_sets[j] + TOK + TILES], 1.0 / HD, EPS,
                                                     ALU.mult, ALU.add))
                    inverse(rt[:], nsq[:], ntmp[:])
                    dve.sem_inc(s["rt_r"], 1)
                    dve.wait_ge(s["rs_out"], 2 * (2 * n + j + 1))
                    is_k = isinstance(n, int)
                    own.step(nc.vector.scalar_tensor_tensor(out=dst_all, in0=psum[:, par_sets[j]:par_sets[j] + TOK],
                                                            scalar=vecs[:, 64 + int(is_k):65 + int(is_k)], in1=rsb[:], op0=ALU.mult, op1=ALU.mult))
                    dve.sem_inc(s[f"ps_free{j}"], 1)
                    dve.sem_inc(s["rs_used"], 1)
                    dve.sem_inc(s["q_raw"], 1)
                    for a in range(0, P, 32):
                        b = a ^ 32
                        own.step(nc.vector.tensor_tensor(rtmp[a:a + 32, :], dst_parts(b, b + 32), sin[b:b + 32, :], ALU.mult))
                    dve.sem_inc(s["q_sin"], 1)
                    dve.wait_ge(s["q_cos"], 2 * n + j + 1)
                    own.step(nc.vector.tensor_tensor(dst_parts(0, P), dst_parts(0, P), rtmp[:], ALU.add))

                dve.wait_ge(s["rope"], 32)
                dve.wait_ge(s["py_ps"], 12)
                for j in range(2):
                    dve.wait_ge(s[f"gate_st{j}"], 16 * GATE_PAIRS)
                with dve.Fori(0, Q_PAIRS) as i:
                    own.enter(i, 24)
                    for j in range(2):
                        h = bass.ds(2 * i + j, 1)
                        norm_rope(i, j, qT[:, h, :].rearrange("p o n -> p (o n)"),
                                  lambda a, b: qT[a:b, h, CTX:TOK].rearrange("p o n -> p (o n)"))
                        dve.sem_inc(s["q_fin"], 1)
                    own.leave(Q_PAIRS)
                for j in range(2):
                    norm_rope(4, j, kraw[j][:], lambda a, b: kraw[j][a:b, CTX:TOK])
                    dve.sem_inc(s["k_fin"], 1)
                for n in range(1, 6, 2):
                    dve.wait_ge(s["v_ps"], n + 1)
                    nc.vector.tensor_copy(*v_chunk(n)).then_inc(s["v_out_d"], 1)
        if last_block == 1:
            return dict(vals=vals, qT=qT, kT_hi=kT_hi, kT_lo=kT_lo, mods=mods)

        prob = [at(f"prob{j}", [P, GRP, LAT_KEYS], F32, RHL + 24 * j * KB) for j in range(2)]
        probT = [[at(f"probT{b}_{j}", [P, GRP * P], F32, RHL + (48 + 4 * b + 2 * j) * KB) for j in range(2)] for b in range(3)]
        q_hi = [at(f"q_hi{j}", [P, GRP, P], F32R, RHL + (60 + 4 * j) * KB) for j in range(2)]
        q_lo = [at(f"q_lo{j}", [P, GRP, P], F32R, RHL + (62 + 4 * j) * KB) for j in range(2)]
        SC, TP, PV = 0, 1536, 3072
        SCALE = HD ** -0.5
        for n in ("q_hi_r q_lo_r scored neg_max exped normed turned0 turned1 turned2 t_out0 t_out1 t_out2 "
                  "pv0 pv1 pv2 pv_unit pv_out dve_c").split():
            s["a_" + n] = sem("b2_" + n)

        def latent(u, kv):
            qt = u - 8 * kv
            return Unit(u, kv, (qt + CTX_TILES) * P, None, LAT_KEYS, CTX)

        units = [latent(u, u // 8) for u in range(16)] + [Unit(16 + z, z // 2, z % 2 * P, None, CTX, 0) for z in range(4)]
        units = [x._replace(par=n % 2) for n, x in enumerate(units)]

        def uses(x, g):
            return 4 * x.u + g if x.keys == LAT_KEYS else 64 + x.u - 16

        def banks_scored(x, g):
            return 12 * x.u + 3 * g if x.keys == LAT_KEYS else 192 + 4 * (x.u - 16) + g

        def score_banks(x):
            return [(b, min(512, x.keys)) for b in range((x.keys + 511) // 512)]

        def chunks(x, g):
            return range(3 * g, 3 * g + 3) if x.keys == LAT_KEYS else range(g, g + 1) if g < 2 else range(0)

        def over_units(eng, head, block_, after, tail, own=None, per=0):
            def step(w, x, n):
                for g in range(GRP):
                    block_(w, g)
                    after(x, g)
                    if g < GRP - 1:
                        head(x, g + 1)
                if n is not None:
                    head(n, 0)
                tail(w)

            for g in range(GRP):
                head(units[0], g)
                if g < GRP - 1:
                    after(units[0], g)
            after(units[0], GRP - 1)
            head(units[1], 0)
            for kv in range(KV):
                with eng.Fori(0, 3) as i:
                    if own:
                        own.enter(i, per)
                    for r in (1, 2):
                        w, x, n = (latent(2 * i + 8 * kv + r + d, kv)._replace(par=(r + d) % 2) for d in (-1, 0, 1))
                        step(w, x, n)
                    if own:
                        own.leave(3)
                for u in ((7, 8) if kv == 0 else range(15, 20)):
                    step(units[u - 1], units[u], units[u + 1] if u < 19 else None)
            for g in range(GRP):
                block_(units[19], g)
            tail(units[19])

        def turned_out(eng, copy, x, g, b, m):
            eng.wait_ge(s[f"a_turned{b}"], m + 1)
            copy(probT[b][g % 2 if x.keys == LAT_KEYS else 0][:], psum[:, TP + 512 * b:TP + 512 * b + 512]).then_inc(s[f"a_t_out{b}"], 1)

        with nc.Block() as block:
            @block.tensor
            def _(pe):
                def head(x, g):
                    if g == 0:
                        pe.wait_ge(s["a_q_lo_r"], x.u + 1)
                    pe.wait_ge(s["a_exped"], 4 * x.u + g)
                    for b, w in score_banks(x):
                        o = psum[:, SC + 512 * b:SC + 512 * b + w]
                        k = slice(x.key0 + 512 * b, x.key0 + 512 * b + w)
                        pe.matmul(o, q_hi[x.par][:, g, :], kT_hi[:, x.kv, k], start=True, stop=False)
                        pe.matmul(o, q_hi[x.par][:, g, :], kT_lo[:, x.kv, k], start=False, stop=False)
                        pe.matmul(o, q_lo[x.par][:, g, :], kT_hi[:, x.kv, k], start=False, stop=True).then_inc(s["a_scored"], 1)

                def values(x, c):
                    b, g = c % 3, c // 3
                    m = uses(x, g)
                    pe.wait_ge(s[f"a_t_out{b}"], m + 1)
                    mm = pe.matmul(psum[:, PV + 512 * x.par:PV + 512 * x.par + 512], vals[:, x.key0 // P + c, x.kv * HD:(x.kv + 1) * HD],
                                   probT[b][g % 2][:], start=(c == 0), stop=(c == x.keys // P - 1))
                    mm.then_inc(s[f"a_pv{b}"], 1)
                    if c == x.keys // P - 1:
                        pe.wait_ge(s[f"a_pv{b}"], m + 1)
                        pe.sem_inc(s["a_pv_unit"], 1)

                def block_(x, g):
                    if g == 0:
                        pe.wait_ge(s["a_normed"], 4 * x.u + 4)
                    for c in chunks(x, g):
                        b = c % 3
                        pe.wait_ge(s[f"a_t_out{b}"], uses(x, g))
                        for h in range(GRP):
                            o = TP + 512 * b + h * P
                            mm = pe.transpose(psum[:, o:o + P], prob[x.par][:, h, c * P:(c + 1) * P], ident[:])
                        mm.then_inc(s[f"a_turned{b}"], 1)
                        if c >= 3:
                            values(x, c - 3)

                def tail(x):
                    for c in range(x.keys // P)[-3:]:
                        values(x, c)
                over_units(pe, head, block_, lambda x, g: None, tail)

            @block.scalar
            def _(act):
                def head(x, g):
                    act.wait_ge(s["a_neg_max"], 4 * x.u + g + 1)
                    if g == 0 and (not isinstance(x.u, int) or x.u > 1):
                        last = x.u - 2
                        for b in range(2 if isinstance(last, int) and last >= 16 else 3):
                            act.wait_ge(s[f"a_turned{b}"], 4 * last + 4 if not isinstance(last, int) or last < 16 else 64 + last - 15)
                    nc.scalar.activation(prob[x.par][:, g, 0:x.keys], psum[:, SC:SC + x.keys], ACT.Exp, bias=nmax[:, x.par, g:g + 1],
                                         scale=SCALE, accum_out=esum[:, x.par, g:g + 1]).then_inc(s["a_exped"], 1)

                def block_(x, g):
                    for c in chunks(x, g):
                        b, m = c % 3, uses(x, g)
                        if b == 1:
                            continue
                        turned_out(act, nc.scalar.copy, x, g, b, m)

                def tail(x):
                    act.wait_ge(s["a_pv_unit"], x.u + 1)
                    nc.scalar.copy(qT[:, x.kv * GRP:(x.kv + 1) * GRP, bass.ds(x.tok, P)],
                                   psum[:, PV + 512 * x.par:PV + 512 * x.par + 512].rearrange("p (h n) -> p h n", n=P)).then_inc(s["a_pv_out"], 1)
                over_units(act, head, block_, lambda x, g: None, tail)

            @block.gpsimd
            def _(pool):
                def split(x):
                    if not isinstance(x.u, int) or x.u > 1:
                        last = x.u - 2
                        pool.wait_ge(s["a_scored"], 12 * last + 12 if not isinstance(last, int) or last < 16 else 192 + 4 * (last - 15))
                    q = qT[:, x.kv * GRP:(x.kv + 1) * GRP, bass.ds(x.tok, P)]
                    pass_wait(pool)
                    nc.gpsimd.tensor_copy(q_hi[x.par][:], q).then_inc(s["a_q_hi_r"], 1)
                    pool.wait_ge(s["a_q_hi_r"], x.u + 1)
                    pass_wait(pool)
                    nc.gpsimd.tensor_tensor(q_lo[x.par][:], q, q_hi[x.par][:], ALU.subtract).then_inc(s["a_q_lo_r"], 1)

                def head(x, g):
                    if g == 0:
                        split(x)

                over_units(pool, head, lambda x, g: None, lambda x, g: None, lambda x: None)

            @block.vector
            def _(dve):
                own = Tally(dve, s["a_dve_c"])

                def head(x, g):
                    for b, w in score_banks(x):
                        dve.wait_ge(s["a_scored"], banks_scored(x, g) + b + 1)
                        ins = nc.vector.reduce_max(rmax[:, b:b + 1], psum[:, SC + 512 * b:SC + 512 * b + w], AX.X)
                    own.step(ins)
                    if x.keys == LAT_KEYS:
                        own.step(nc.vector.reduce_max(rmax[:, 3:4], rmax[:, 0:3], AX.X))
                    last = rmax[:, 3:4] if x.keys == LAT_KEYS else rmax[:, 0:1]
                    nc.vector.tensor_scalar(nmax[:, x.par, g:g + 1], last, -SCALE, None, ALU.mult).then_inc(s["a_neg_max"], 1)

                def block_(x, g):
                    for c in chunks(x, g):
                        if c % 3 == 1:
                            turned_out(dve, nc.vector.tensor_copy, x, g, 1, uses(x, g))

                def after(x, g):
                    dve.wait_ge(s["a_exped"], 4 * x.u + g + 1)
                    own.step(nc.vector.reciprocal(einv[:, x.par, g:g + 1], esum[:, x.par, g:g + 1]))
                    v = prob[x.par][:, g, 0:x.keys]
                    nc.vector.tensor_scalar(v, v, einv[:, x.par, g:g + 1], None, ALU.mult).then_inc(s["a_normed"], 1)
                over_units(dve, head, block_, after, lambda x: None, own, 24)
        if last_block == 2:
            return dict(qT=qT)

        pool_hi = at("pool_hi", [P, 4, TOK], F32R, RKV)
        pool_lo = at("pool_lo", [P, 4, TOK], F32R, RKV + 20 * KB)
        pool_raw = at("pool_raw", [P, 4, TOK], F32, RKV + 20 * KB)
        KM = KC + 4
        wm_hi = [at(f"wm_hi{j}", [P, KM, P], F32R, RKV + (42 + 12 * j) * KB) for j in range(2)]
        wm_lo = [at(f"wm_lo{j}", [P, KM, P], F32R, RKV + (48 + 12 * j) * KB) for j in range(2)]
        wm_raw = at("wm_raw", [P, KM, PAIR], F32, RW + 12 * KB)
        merged = at("merged", [P, KC, TOK], F32, RA)
        wo_raw = at("wo_raw", [P, KC, PAIR], F32, RW + 12 * KB)
        wo_hi = [at(f"wo_hi{j}", [P, KC, P], F32R, RKV + (42 + 8 * j) * KB) for j in range(2)]
        wo_lo = [at("wo_lo0", [P, KC, P], F32R, RKV + 46 * KB), at("wo_lo1", [P, KC, P], F32R, RW + 20 * KB)]
        ost = [stage, at("ost1", [P, TOK], F32, RKV)]
        x1 = at("x1", [P, TILES, D], F32, RA)
        for n in ("wm_in wm_hi0 wm_hi1 wm_lo0 wm_lo1 at_hi at_lo_d at_lo_p pl_in pl_hi pl_lo ga_in0 ga_in1 gb_in mmA mmB a_out b_out merged "
                  "mg_hi mg_lo_d mg_lo_p wo_in wo_hi0 wo_hi1 wo_lo0 wo_lo1 mmO0 mmO1 ost_r0 ost_r1 o_turn o_add "
                  "x_in dve_c act_c").split():
            s["m_" + n] = sem("b3_" + n)
        H_LO_POOL = (3, 7)
        lo_before = [sum(k not in H_LO_POOL for k in range(n)) for n in range(KC + 1)]

        with nc.Block() as block:
            @block.sync
            def _(sp):
                def load_wm(n):
                    sp.wait_ge(s["m_wm_lo1"], n)
                    sp.dma_start(wm_raw[:], io["w_merge"][bass.ds(n, 1)].rearrange("o p k n -> p (o k) n")).then_inc(s["m_wm_in"], 16)

                def load_wo(n):
                    sp.wait_ge(s["m_wo_lo1"], n)
                    sp.dma_start(wo_raw[:], io["w_out"][bass.ds(n, 1)].rearrange("o p k n -> p (o k) n")).then_inc(s["m_wo_in"], 16)
                load_wm(0)
                sp.dma_start(pool_raw[:], io["poolT"].rearrange("c p n -> p c n")).then_inc(s["m_pl_in"], 16)
                sp.wait_ge(s["m_at_hi"], KC)
                sp.wait_ge(s["m_at_lo_d"], KC - len(H_LO_POOL))
                sp.wait_ge(s["m_at_lo_p"], len(H_LO_POOL))

                def load_gates(n, j):
                    sp.dma_start(merged[:, bass.ds(2 * n + j, 1), :].rearrange("p o n -> p (o n)"),
                                 io["gates"][bass.ds(2 * n + j, 1)].rearrange("o p n -> p (o n)")).then_inc(s[f"m_ga_in{j}"], 16)
                    sp.wait_ge(s["m_merged"], 2 * n + j)
                    sp.dma_start(stage[:], io["gates"][bass.ds(2 * n + j + KC, 1)].rearrange("o p n -> p (o n)")).then_inc(s["m_gb_in"], 16)
                with sp.Fori(0, 3) as i:
                    load_gates(i, 0)
                    load_wm(i + 1)
                    load_gates(i, 1)
                load_gates(3, 0)
                sp.wait_ge(s["m_wm_lo1"], 4)
                load_wo(0)
                load_gates(3, 1)
                for k in range(KC):
                    if k in H_LO_POOL:
                        sp.wait_ge(s["m_mg_lo_p"], H_LO_POOL.index(k) + 1)
                    else:
                        sp.wait_ge(s["m_mg_lo_d"], lo_before[k] + 1)
                sp.dma_start(x1[:], io["x"].rearrange("t p d -> p t d")).then_inc(s["m_x_in"], 16)
                with sp.Fori(0, 3) as i:
                    load_wo(i + 1)

            @block.tensor
            def _(pe):
                def product(o, w_h, w_l, j, a_hi, a_lo, k0, k1, sem_, ready=None, hooks={}):
                    for k in range(k0, k1):
                        if ready:
                            ready(k - k0)
                        for a, b in ((w_h, a_hi), (w_h, a_lo), (w_l, a_hi)):
                            for g, w in GROUPS:
                                mm = pe.matmul(psum[:, o + g:o + g + w], a[j][:, k, :], b[:, k - k0, g:g + w],
                                               start=(k == k0 and a is w_h and b is a_hi), stop=(k == k1 - 1 and a is w_l))
                        if k in hooks:
                            hooks[k]()
                    mm.then_inc(sem_, 1)

                def attn_ready(k):
                    pe.wait_ge(s["m_at_hi"], k + 1)
                    pe.wait_ge(s["m_at_lo_p"], H_LO_POOL.index(k) + 1) if k in H_LO_POOL else pe.wait_ge(s["m_at_lo_d"], lo_before[k] + 1)

                def pool_ready(k):
                    pe.wait_ge(s["m_pl_hi"], k + 1)
                    pe.wait_ge(s["m_pl_lo"], k + 1)

                def branches(n, j, first=False):
                    pe.wait_ge(s[f"m_wm_hi{j}"], n + 1)
                    pe.wait_ge(s[f"m_wm_lo{j}"], n + 1)
                    pe.wait_ge(s["m_a_out"], 2 * n + j)
                    product(par_sets[0], wm_hi, wm_lo, j, h_hi, h_lo, 0, KC, s["m_mmA"], attn_ready if first else None)
                    pe.wait_ge(s["m_b_out"], 2 * n + j)
                    product(par_sets[1], wm_hi, wm_lo, j, pool_hi, pool_lo, KC, KM, s["m_mmB"], pool_ready if first else None)
                branches(0, 0, True)
                branches(0, 1)
                with pe.Fori(0, 3) as i:
                    branches(i + 1, 0)
                    branches(i + 1, 1)

                def merged_ready(k):
                    pe.wait_ge(s["m_mg_hi"], k + 1)
                    pe.wait_ge(s["m_mg_lo_p"], H_LO_POOL.index(k) + 1) if k in H_LO_POOL else pe.wait_ge(s["m_mg_lo_d"], lo_before[k] + 1)

                def turn(n, j):
                    pe.wait_ge(s[f"m_ost_r{j}"], 2 * n + 2)
                    for q, (g, w) in enumerate(GROUPS):
                        m = 6 * n + 3 * j + q
                        bank = AUX[(3 * j + q) % 2]
                        pe.wait_ge(s["m_o_add"], m - 1) if not isinstance(m, int) or m > 1 else None
                        for t in range(g // P, (g + w) // P):
                            mm = pe.transpose(psum[:, bank + t * P - g:bank + (t + 1) * P - g], ost[j][:, t * P:(t + 1) * P], ident[:])
                        mm.then_inc(s["m_o_turn"], 1)

                def out(n, j, ready=None, hooks={}):
                    pe.wait_ge(s[f"m_wo_hi{j}"], n + 1)
                    pe.wait_ge(s[f"m_wo_lo{j}"], n + 1)
                    pe.wait_ge(s[f"m_ost_r{j}"], 2 * n)
                    product(par_sets[j], wo_hi, wo_lo, j, h_hi, h_lo, 0, KC, s[f"m_mmO{j}"], ready, hooks)
                pe.wait_ge(s["m_a_out"], KC)
                out(0, 0, merged_ready)
                pe.wait_ge(s["m_b_out"], KC)
                out(0, 1, hooks={3: lambda: turn(0, 0)})
                with pe.Fori(0, 3) as i:
                    out(i + 1, 0, hooks={3: lambda: turn(i, 1)})
                    out(i + 1, 1, hooks={3: lambda: turn(i + 1, 0)})
                turn(3, 1)

            @block.scalar
            def _(act):
                def split_wm(n, j):
                    act.wait_ge(s["m_wm_in"], 16 * (n + 1))
                    act.wait_ge(s["m_mmB"], 2 * n - 1 + j) if not isinstance(n, int) or n else None
                    nc.scalar.copy(wm_hi[j][:], wm_raw[:, :, j * P:(j + 1) * P]).then_inc(s[f"m_wm_hi{j}"], 1)
                split_wm(0, 0)
                for k in range(KC):
                    nc.scalar.copy(h_hi[:, k, :], qT[:, k, :]).then_inc(s["m_at_hi"], 1)
                act.wait_ge(s["m_pl_in"], 16)
                for k in range(4):
                    nc.scalar.copy(pool_hi[:, k, :], pool_raw[:, k, :]).then_inc(s["m_pl_hi"], 1)
                split_wm(0, 1)
                with act.Fori(0, 3) as i:
                    split_wm(i + 1, 0)
                    split_wm(i + 1, 1)

                def split_wo(n, j):
                    act.wait_ge(s["m_wo_in"], 16 * (n + 1))
                    act.wait_ge(s[f"m_mmO{j}"], n)
                    nc.scalar.copy(wo_hi[j][:], wo_raw[:, :, j * P:(j + 1) * P]).then_inc(s[f"m_wo_hi{j}"], 1)
                act.wait_ge(s["m_mmB"], KC - 1)
                split_wo(0, 0)
                split_wo(0, 1)
                act.wait_ge(s["m_mmA"], KC)
                for k in range(KC):
                    act.wait_ge(s["m_merged"], k + 1)
                    nc.scalar.copy(h_hi[:, k, :], merged[:, k, :]).then_inc(s["m_mg_hi"], 1)

                def out(n, j, more=True):
                    act.wait_ge(s[f"m_mmO{j}"], n + 1)
                    for q, (g, w) in enumerate(STREAMS):
                        nc.scalar.mul(ost[j][:, g:g + w], psum[:, par_sets[j] + g:par_sets[j] + g + w],
                                      gate1[:, 2 * j + q:2 * j + q + 1]).then_inc(s[f"m_ost_r{j}"], 1)
                    if more:
                        split_wo(n + 1, j)
                own = Tally(act, s["m_act_c"])
                with act.Fori(0, 3) as i:
                    own.enter(i, 1)
                    for j in range(2):
                        act.wait_ge(s[f"m_ost_r{j}"], 2 * i)
                    own.step(nc.scalar.copy(gate1[:], mods[:, bass.ds(2 * i + 2 * KC, 2), :].rearrange("p m q -> p (m q)")))
                    out(i, 0)
                    out(i, 1)
                    own.leave(3)
                for j in range(2):
                    act.wait_ge(s[f"m_ost_r{j}"], 6)
                own.step(nc.scalar.copy(gate1[:], mods[:, 3 * KC - 2:3 * KC, :].rearrange("p m q -> p (m q)")))
                out(3, 0, False)
                out(3, 1, False)

            @block.gpsimd
            def _(pool):
                def split_wm(n, j):
                    pool.wait_ge(s[f"m_wm_hi{j}"], n + 1)
                    nc.gpsimd.tensor_tensor(wm_lo[j][:], wm_raw[:, :, j * P:(j + 1) * P], wm_hi[j][:], ALU.subtract).then_inc(s[f"m_wm_lo{j}"], 1)
                split_wm(0, 0)
                for k in H_LO_POOL:
                    pool.wait_ge(s["m_at_hi"], k + 1)
                    nc.gpsimd.tensor_tensor(h_lo[:, k, :], qT[:, k, :], h_hi[:, k, :], ALU.subtract).then_inc(s["m_at_lo_p"], 1)
                split_wm(0, 1)
                with pool.Fori(0, 3) as i:
                    split_wm(i + 1, 0)
                    split_wm(i + 1, 1)

                def split_wo(n, j):
                    pool.wait_ge(s[f"m_wo_hi{j}"], n + 1)
                    nc.gpsimd.tensor_tensor(wo_lo[j][:], wo_raw[:, :, j * P:(j + 1) * P], wo_hi[j][:], ALU.subtract).then_inc(s[f"m_wo_lo{j}"], 1)
                split_wo(0, 0)
                split_wo(0, 1)
                for k in H_LO_POOL:
                    pool.wait_ge(s["m_mg_hi"], k + 1)
                    nc.gpsimd.tensor_tensor(h_lo[:, k, :], merged[:, k, :], h_hi[:, k, :], ALU.subtract).then_inc(s["m_mg_lo_p"], 1)
                with pool.Fori(0, 3) as i:
                    split_wo(i + 1, 0)
                    split_wo(i + 1, 1)

            @block.vector
            def _(dve):
                own = Tally(dve, s["m_dve_c"])
                for k in range(KC):
                    if k not in H_LO_POOL:
                        dve.wait_ge(s["m_at_hi"], k + 1)
                        nc.vector.tensor_tensor(h_lo[:, k, :], qT[:, k, :], h_hi[:, k, :], ALU.subtract).then_inc(s["m_at_lo_d"], 1)
                for k in range(4):
                    dve.wait_ge(s["m_pl_hi"], k + 1)
                    nc.vector.tensor_tensor(pool_lo[:, k, :], pool_raw[:, k, :], pool_hi[:, k, :], ALU.subtract).then_inc(s["m_pl_lo"], 1)
                with dve.Fori(0, 4) as i:
                    own.enter(i, 6)
                    for j in range(2):
                        v = merged[:, bass.ds(2 * i + j, 1), :].rearrange("p o n -> p (o n)")
                        dve.wait_ge(s[f"m_ga_in{j}"], 16 * (i + 1))
                        dve.wait_ge(s["m_mmA"], 2 * i + j + 1)
                        own.step(nc.vector.tensor_tensor(v, v, psum[:, par_sets[0]:par_sets[0] + TOK], ALU.mult))
                        dve.sem_inc(s["m_a_out"], 1)
                        dve.wait_ge(s["m_gb_in"], 32 * i + 16 * (j + 1))
                        dve.wait_ge(s["m_mmB"], 2 * i + j + 1)
                        own.step(nc.vector.tensor_tensor(stage[:], stage[:], psum[:, par_sets[1]:par_sets[1] + TOK], ALU.mult))
                        dve.sem_inc(s["m_b_out"], 1)
                        own.step(nc.vector.tensor_tensor(v, v, stage[:], ALU.add))
                        dve.sem_inc(s["m_merged"], 1)
                    own.leave(4)
                for k in range(KC):
                    if k not in H_LO_POOL:
                        dve.wait_ge(s["m_mg_hi"], k + 1)
                        nc.vector.tensor_tensor(h_lo[:, k, :], merged[:, k, :], h_hi[:, k, :], ALU.subtract).then_inc(s["m_mg_lo_d"], 1)
                dve.wait_ge(s["m_x_in"], 16)
                with dve.Fori(0, 4) as i:
                    for j in range(2):
                        for q, (g, w) in enumerate(GROUPS):
                            dve.wait_ge(s["m_o_turn"], 6 * i + 3 * j + q + 1)
                            bank = AUX[(3 * j + q) % 2]
                            v = x1[:, g // P:(g + w) // P, bass.ds((2 * i + j) * P, P)]
                            nc.vector.tensor_tensor(v, v, psum[:, bank:bank + w].rearrange("p (t n) -> p t n", n=P), ALU.add).then_inc(s["m_o_add"], 1)
        if last_block == 3:
            return dict(x1=x1)

        nc.clear_and_free_semaphores(early)
        nc.all_engine_barrier()

        h2 = at("h2", [P, TILES, D], F32, RHL)
        h2T = [at(f"h2T{j}", [P, KC, P], F32, RHL + (40 + 4 * j) * KB) for j in range(2)]
        rowb = at("rowb", [P, 6, D], F32, RHL + 48 * KB)
        route = at("route", [P, ROUTE_W], F32, RHL + 72 * KB)
        r_at = [RKV]

        def routed(name, shape, dt=F32):
            r_at[0] += (4 * int(np.prod(shape[1:])) + 31) // 32 * 32
            return at(name, shape, dt, r_at[0] - (4 * int(np.prod(shape[1:])) + 31) // 32 * 32)
        w_route = routed("w_route", [P, KC, NR])
        logits = routed("logits", [P, TILES, NR])
        gmax, psel, v1, v2, wexp = (routed(n, [P, TILES]) for n in ("gmax", "psel", "v1", "v2", "wexp"))
        rsub, geq, gsel = (routed(n, [P, TILES, EG]) for n in ("rsub", "geq", "gsel"))
        e_in, eeq, rest = (routed(n, [P, TILES, EPG]) for n in ("e_in", "eeq", "rest"))
        pick = [routed(f"pick{c}", [P, TILES, EPG]) for c in range(2)]
        by_expert = routed("by_expert", [P, TILES, EG, EPG])
        chosen = [routed(f"chosen{c}", [P, TILES, EG, EPG]) for c in range(2)]
        either = routed("either", [P, TILES, NE])
        place = routed("place", [P, TILES, NE])
        rsum = routed("rsum", [P, TILES])
        count = routed("count", [P, NE])
        fills = routed("fills", [P, NE, TILES])
        n_tiles, ends, starts = (routed(n, [P, NE]) for n in ("n_tiles", "ends", "starts"))
        sums = routed("sums", [P, NE, NE])
        past = routed("past", [P, SLOTS, NE])
        owner = routed("owner", [P, SLOTS])
        pos = routed("pos", [P, 2, TILES])
        posA, posB = (routed(n, [P, 2 * TILES]) for n in ("posA", "posB"))
        above = routed("above", [P, 2 * TILES, SLOTS])
        hotB = routed("hotB", [P, 2 * TILES, P])
        hotA = routed("hotA", [P, 2 * TILES, SLOTS])
        assert r_at[0] <= RC
        k_at = [RHL + 75 * KB]

        def kept(name, shape, dt):
            k_at[0] += (4 * int(np.prod(shape[1:])) + 31) // 32 * 32
            return at(name, shape, dt, k_at[0] - (4 * int(np.prod(shape[1:])) + 31) // 32 * 32)
        ids = kept("ids", [P, SLOTS], I32)
        wrow = kept("wrow", [P, SLOTS], I32)
        place_i = kept("place_i", [P, 2, TILES], I32)
        w_top = kept("w_top", [P, 2, TILES], F32)
        assert k_at[0] <= RKV
        o = 0
        tabs = {}
        for n, w in ROUTE_TABLES:
            tabs[n] = route[:, o:o + w]
            o += w
        for n in "sq rt rows rows_out consts wr h2_a h2_d h2_st turned out logit g_max e_sum e_dif e_w mask ranks onehot ids_ps dve_c".split():
            s["r_" + n] = sem("b4_" + n)
        ROWS = [(m2, 0, 0), (m2, 0, 1), (mods, 3 * KC, 0), (mods, 3 * KC, 1), (mods, 5 * KC, 0), (mods, 5 * KC, 1)]
        LG, RANKS, COUNTS, IDS = 6 * 512, 7 * 512, 4 * 512, 5 * 512

        with nc.Block() as block:
            @block.sync
            def _(sp):
                sp.dma_start(route[:], io["route"]).then_inc(s["r_consts"], 16)
                sp.dma_start(w_route[:], io["w_route"]).then_inc(s["r_wr"], 16)
                for t in range(TILES):
                    sp.wait_ge(s["r_h2_a"], t + 1)
                    sp.dma_start(io["h2d"][t * P:(t + 1) * P, :], h2[:, t, :]).then_inc(s["r_h2_st"], 16)
                sp.wait_ge(s["r_h2_st"], 16 * TILES)

            @block.tensor
            def _(pe):
                for r, (v, c, q) in enumerate(ROWS):
                    if r >= 3:
                        pe.wait_ge(s["r_rows_out"], r - 2)
                    for k in range(KC):
                        o = (r % 3) * 1024 + k * P
                        mm = pe.matmul(psum[:, o:o + P], v[:, c + k, q:q + 1].broadcast_to([P, P]), ident[:], start=True, stop=True)
                    mm.then_inc(s["r_rows"], 1)
                pe.wait_ge(s["r_rows_out"], len(ROWS))

                def logit(t):
                    pe.wait_ge(s["r_out"], t + 1)
                    for k in range(KC):
                        mm = pe.matmul(psum[:, LG + t * NR:LG + (t + 1) * NR], h2T[t % 2][:, k, :], w_route[:, k, :],
                                       start=(k == 0), stop=(k == KC - 1))
                    mm.then_inc(s["r_logit"], 1)
                pe.wait_ge(s["r_wr"], 16)
                for t in range(TILES):
                    pe.wait_ge(s["r_h2_a"], t + 1)
                    if t >= 2:
                        pe.wait_ge(s["r_out"], t - 1)
                    for k in range(KC):
                        o = (t % 2) * 1024 + k * P
                        mm = pe.transpose(psum[:, o:o + P], h2[:, t, k * P:(k + 1) * P], ident[:])
                    mm.then_inc(s["r_turned"], 1)
                    if t:
                        logit(t - 1)
                logit(TILES - 1)

                pe.wait_ge(s["r_mask"], 1)
                pe.wait_ge(s["r_consts"], 16)
                n = TILES * NE
                m = either[:].rearrange("p t e -> p (t e)")
                pe.matmul(psum[:, RANKS:RANKS + n], tabs["before"], m, start=True, stop=False)
                for d in range(1, TILES):
                    mm = pe.matmul(psum[:, RANKS + d * NE:RANKS + n], ones[:], m[:, 0:n - d * NE], start=False, stop=(d == TILES - 1))
                for t in range(TILES):
                    mm = pe.matmul(psum[:, COUNTS:COUNTS + NE], ones[:], either[:, t, :], start=(t == 0), stop=(t == TILES - 1))
                mm.then_inc(s["r_ranks"], 1)
                pe.wait_ge(s["r_onehot"], 1)
                for c in range(2 * TILES):
                    mm = pe.matmul(psum[:, IDS:IDS + SLOTS], hotB[:, c, :], hotA[:, c, :], start=(c == 0), stop=(c == 2 * TILES - 1))
                mm.then_inc(s["r_ids_ps"], 1)

            @block.scalar
            def _(act):
                for t in range(TILES):
                    nc.scalar.activation(h2[:, t, :], x1[:, t, :], ACT.Square, accum_out=ssq[:, t:t + 1]).then_inc(s["r_sq"], 1)
                act.wait_ge(s["r_sq"], TILES)
                nc.scalar.activation(rstd[:], ssq[:], ACT.Sqrt, bias=eps[:], scale=1.0 / D).then_inc(s["r_rt"], 1)
                for t in range(TILES):
                    act.wait_ge(s["r_turned"], t + 1)
                    if t >= 2:
                        act.wait_ge(s["r_logit"], t - 1)
                    nc.scalar.copy(h2T[t % 2][:].rearrange("p k n -> p (k n)"), psum[:, (t % 2) * 1024:(t % 2) * 1024 + 1024]).then_inc(s["r_out"], 1)
                act.wait_ge(s["r_g_max"], 1)
                nc.scalar.activation(rsub[:], rsub[:], ACT.Exp).then_inc(s["r_e_sum"], 1)
                act.wait_ge(s["r_e_dif"], 1)
                nc.scalar.activation(wexp[:], v2[:], ACT.Exp).then_inc(s["r_e_w"], 1)

            @block.gpsimd
            def _(pool):
                pool.wait_ge(s["r_rows_out"], 4)
                for t in range(TILES):
                    pool.wait_ge(s["r_h2_d"], t + 1)
                    nc.gpsimd.tensor_tensor(h2[:, t, :], h2[:, t, :], rowb[:, 2 + (t >= CTX_TILES), :], ALU.add).then_inc(s["r_h2_a"], 1)

            @block.vector
            def _(dve):
                own = Tally(dve, s["r_dve_c"])
                tt, ts = nc.vector.tensor_tensor, nc.vector.tensor_scalar
                for r in range(len(ROWS)):
                    dve.wait_ge(s["r_rows"], r + 1)
                    nc.vector.tensor_copy(rowb[:, r, :], psum[:, (r % 3) * 1024:(r % 3) * 1024 + 1024]).then_inc(s["r_rows_out"], 1)
                dve.wait_ge(s["r_rows_out"], len(ROWS))
                dve.wait_ge(s["r_rt"], 1)
                own.step(ts(nsq[:], ssq[:], 1.0 / D, EPS, ALU.mult, ALU.add))
                own.step(nc.vector.reciprocal(rstd[:], rstd[:]))
                own.step(tt(ntmp[:], rstd[:], rstd[:], ALU.mult))
                own.step(tt(ntmp[:], ntmp[:], nsq[:], ALU.mult))
                own.step(ts(ntmp[:], ntmp[:], -0.5, 1.5, ALU.mult, ALU.add))
                own.step(tt(rstd[:], rstd[:], ntmp[:], ALU.mult))
                for t in range(TILES):
                    nc.vector.scalar_tensor_tensor(h2[:, t, :], x1[:, t, :], rstd[:, t:t + 1], rowb[:, int(t >= CTX_TILES), :],
                                                   ALU.mult, ALU.mult).then_inc(s["r_h2_d"], 1)
                dve.wait_ge(s["r_logit"], TILES)
                own.step(nc.vector.tensor_copy(logits[:], psum[:, LG:LG + TILES * NR].rearrange("p (t n) -> p t n", n=NR)))
                dve.wait_ge(s["r_consts"], 16)
                g4 = [P, TILES, EG]
                desc = tabs["desc"].unsqueeze(1).broadcast_to(g4)

                def first_max(hot, eq, x, top):
                    own.step(nc.vector.reduce_max(top, x, AX.X))
                    own.step(tt(eq[:], x, top.unsqueeze(2).broadcast_to(g4), ALU.is_equal))
                    own.step(tt(eq[:], eq[:], desc, ALU.mult))
                    own.step(nc.vector.reduce_max(rsum[:], eq[:], AX.X))
                    own.step(tt(hot[:], eq[:], rsum[:].unsqueeze(2).broadcast_to(g4), ALU.is_equal))
                gl = logits[:, :, 0:EG]
                first_max(gsel, geq, gl, gmax[:])
                own.step(tt(rsub[:], gl, gmax[:].unsqueeze(2).broadcast_to(g4), ALU.subtract))
                dve.sem_inc(s["r_g_max"], 1)
                el = logits[:, :, EG:NR].rearrange("p t (g e) -> p t g e", e=EPG)
                g44 = [P, TILES, EG, EPG]
                own.step(tt(by_expert[:], el, gsel[:].unsqueeze(3).broadcast_to(g44), ALU.mult))
                own.step(nc.vector.reduce_sum(e_in[:], by_expert[:].rearrange("p t g e -> p t e g"), AX.X))
                first_max(pick[0], eeq, e_in[:], v1[:])
                own.step(ts(rest[:], pick[0][:], -1.0, 1.0, ALU.mult, ALU.add))
                own.step(tt(rest[:], rest[:], e_in[:], ALU.mult))
                own.step(ts(e_in[:], pick[0][:], -3.0e38, None, ALU.mult))
                own.step(tt(rest[:], rest[:], e_in[:], ALU.add))
                first_max(pick[1], eeq, rest[:], v2[:])
                own.step(tt(v2[:], v2[:], v1[:], ALU.subtract))
                dve.sem_inc(s["r_e_dif"], 1)
                for c in range(2):
                    own.step(tt(chosen[c][:], gsel[:].unsqueeze(3).broadcast_to(g44), pick[c][:].unsqueeze(2).broadcast_to(g44), ALU.mult))
                own.step(tt(either[:], chosen[0][:].rearrange("p t g e -> p t (g e)"), chosen[1][:].rearrange("p t g e -> p t (g e)"), ALU.add))
                dve.sem_inc(s["r_mask"], 1)
                dve.wait_ge(s["r_e_sum"], 1)
                own.step(nc.vector.reduce_sum(psel[:], rsub[:], AX.X))
                own.step(nc.vector.reciprocal(psel[:], psel[:]))
                dve.wait_ge(s["r_e_w"], 1)
                own.step(ts(v1[:], wexp[:], 1.0, None, ALU.add))
                own.step(nc.vector.reciprocal(v1[:], v1[:]))
                own.step(tt(w_top[:, 0, :], v1[:], psel[:], ALU.mult))
                own.step(tt(w_top[:, 1, :], w_top[:, 0, :], wexp[:], ALU.mult))
                dve.wait_ge(s["r_ranks"], 1)
                own.step(nc.vector.tensor_copy(count[:], psum[:, COUNTS:COUNTS + NE]))
                own.step(tt(fills[:], count[:].unsqueeze(2).broadcast_to([P, NE, TILES]),
                            tabs["tile0"].unsqueeze(1).broadcast_to([P, NE, TILES]), ALU.is_gt))
                own.step(nc.vector.reduce_sum(n_tiles[:], fills[:], AX.X))
                own.step(tt(sums[:], tabs["upto"].rearrange("p (e f) -> p e f", f=NE), n_tiles[:].unsqueeze(1).broadcast_to([P, NE, NE]), ALU.mult))
                own.step(nc.vector.reduce_sum(ends[:], sums[:], AX.X))
                own.step(tt(starts[:], ends[:], n_tiles[:], ALU.subtract))
                own.step(ts(starts[:], starts[:], float(P), None, ALU.mult))
                own.step(tt(place[:], psum[:, RANKS:RANKS + TILES * NE].rearrange("p (t e) -> p t e", e=NE),
                            starts[:].unsqueeze(1).broadcast_to([P, TILES, NE]), ALU.add))
                for c in range(2):
                    x = by_expert[:].rearrange("p t g e -> p t (g e)")
                    own.step(tt(x, place[:], chosen[c][:].rearrange("p t g e -> p t (g e)"), ALU.mult))
                    own.step(nc.vector.reduce_sum(pos[:, c, :], x, AX.X))
                flat = pos[:].rearrange("p c t -> p (c t)")
                ab = [P, 2 * TILES, SLOTS]
                own.step(tt(above[:], flat.unsqueeze(2).broadcast_to(ab), tabs["slot0"].unsqueeze(1).broadcast_to(ab), ALU.is_ge))
                own.step(nc.vector.reduce_sum(posA[:], above[:], AX.X))
                own.step(ts(posA[:], posA[:], -1.0, None, ALU.add))
                own.step(ts(posB[:], posA[:], -float(P), None, ALU.mult))
                own.step(tt(posB[:], posB[:], flat, ALU.add))
                own.step(tt(hotA[:], posA[:].unsqueeze(2).broadcast_to(ab), tabs["slot"].unsqueeze(1).broadcast_to(ab), ALU.is_equal))
                for c in range(2):
                    v = hotA[:, c * TILES:(c + 1) * TILES, :]
                    own.step(tt(v, v, tabs["token"].unsqueeze(2).broadcast_to([P, TILES, SLOTS]), ALU.mult))
                bb = [P, 2 * TILES, P]
                own.step(tt(hotB[:], posB[:].unsqueeze(2).broadcast_to(bb), tabs["col"].unsqueeze(1).broadcast_to(bb), ALU.is_equal))
                dve.sem_inc(s["r_onehot"], 1)
                own.step(tt(past[:], tabs["slot"].unsqueeze(2).broadcast_to([P, SLOTS, NE]),
                            ends[:].unsqueeze(1).broadcast_to([P, SLOTS, NE]), ALU.is_ge))
                own.step(nc.vector.reduce_sum(owner[:], past[:], AX.X))
                own.step(ts(owner[:], owner[:], float(NE - 1), float(P), ALU.min, ALU.mult))
                own.step(tt(owner[:], owner[:], tabs["row"].broadcast_to([P, SLOTS]), ALU.add))
                own.step(nc.vector.tensor_copy(wrow[:], owner[:]))
                own.step(nc.vector.tensor_copy(place_i[:], pos[:]))
                dve.wait_ge(s["r_ids_ps"], 1)
                own.step(nc.vector.tensor_copy(ids[:], psum[:, IDS:IDS + SLOTS]))
        if last_block == 4:
            return dict(h2=h2, logits=logits, ids=ids, wrow=wrow, place_i=place_i, w_top=w_top, rowb=rowb)

        wgu = [at(f"wgu{j}", [P, KC, 2 * FE], F32, RKV + 16 * j * KB) for j in range(2)]
        wdn = [at(f"wdn{j}", [P, 2, D], F32, RKV + (32 + 8 * j) * KB) for j in range(2)]
        xg = [at(f"xg{j}", [P, D], F32, RKV + (48 + 4 * j) * KB) for j in range(2)]
        xgT = [at(f"xgT{j}", [P, KC, P], F32, RHL + 4 * j * KB) for j in range(2)]
        sig = [at(f"sig{j}", [P, FE], F32, RHL + (8 + j) * KB) for j in range(2)]
        hid = [at(f"hid{j}", [P, FE], F32, RHL + (10 + j) * KB) for j in range(2)]
        hidT = [at(f"hidT{j}", [P, 2, P], F32, RHL + (12 + j) * KB) for j in range(2)]
        yst = [at(f"yst{j}", [P, D], F32, RHL + (16 + 4 * j) * KB) for j in range(2)]
        x_row, gu_row, dn_row = ([kept(f"{n}{j}", [P, 1], I32) for j in range(2)] for n in ("x_row", "gu_row", "dn_row"))
        for n in "pool_c xg0 xg1 wgu0 wgu1 wdn0 wdn1 turned xgT_a xgT_d gu sig hid_s hid hid_turned hidT down y_a y_d y_st0 y_st1".split():
            s["e_" + n] = sem("b5_" + n)
        STEPS = SLOTS - 1
        XT_PS, GU_PS, HT_PS, Y_PS = 0, (1024, 1536), 2048, 3072

        with nc.Block() as block:
            @block.gpsimd
            def _(pool):
                own = Tally(pool, s["e_pool_c"])

                def gather(dst, rows, table, index, a, j, done):
                    pass_wait(pool)
                    own.step(nc.gpsimd.tensor_copy(index[j][:], table[:, bass.ds(a, 1)]))
                    pass_wait(pool)
                    nc.gpsimd.indirect_dma_start(dst, None, rows, bass.IndirectOffsetOnAxis(index[j][:], 0)).then_inc(done, 16)

                def load_x(a, j):
                    gather(xg[j][:], io["h2d"], ids, x_row, a, j, s[f"e_xg{j}"])

                def load_gu(a, j):
                    gather(wgu[j][:].rearrange("p k n -> p (k n)"), io["w_gu"], wrow, gu_row, a, j, s[f"e_wgu{j}"])

                def load_dn(a, j):
                    gather(wdn[j][:].rearrange("p k n -> p (k n)"), io["w_dn"], wrow, dn_row, a, j, s[f"e_wdn{j}"])
                load_x(0, 0)
                load_gu(0, 0)
                load_x(1, 1)
                load_dn(0, 0)
                load_gu(1, 1)
                load_dn(1, 1)

                def step(a, j):
                    pool.wait_ge(s["e_turned"], a - 1)
                    load_x(a, j)
                    pool.wait_ge(s["e_gu"], a - 1)
                    load_gu(a, j)
                    pool.wait_ge(s["e_down"], a - 1)
                    load_dn(a, j)
                with pool.Fori(0, STEPS // 2 - 1) as i:
                    own.enter(i, 6)
                    step(2 * i + 2, 0)
                    step(2 * i + 3, 1)
                    own.leave(STEPS // 2 - 1)
                step(STEPS - 1, 0)

            @block.sync
            def _(sp):
                def store(i, j):
                    a = 2 * i + j
                    sp.wait_ge(s["e_y_a"], a + 1)
                    sp.wait_ge(s["e_y_d"], a + 1)
                    sp.dma_start(io["ybuf"][bass.ds(a * P, P), :], yst[j][:]).then_inc(s[f"e_y_st{j}"], 16)
                with sp.Fori(0, STEPS // 2) as i:
                    store(i, 0)
                    store(i, 1)
                store(STEPS // 2, 0)
                sp.wait_ge(s["e_y_st0"], 16 * (STEPS // 2 + 1))
                sp.wait_ge(s["e_y_st1"], 16 * (STEPS // 2))

            @block.tensor
            def _(pe):
                def turn(i, j):
                    a = 2 * i + j
                    pe.wait_ge(s[f"e_xg{j}"], 16 * (i + 1))
                    pe.wait_ge(s["e_xgT_a"], a)
                    pe.wait_ge(s["e_xgT_d"], a)
                    for k in range(KC):
                        mm = pe.transpose(psum[:, XT_PS + k * P:XT_PS + (k + 1) * P], xg[j][:, k * P:(k + 1) * P], ident[:])
                    mm.then_inc(s["e_turned"], 1)

                def gate_up(i, j):
                    a = 2 * i + j
                    pe.wait_ge(s[f"e_wgu{j}"], 16 * (i + 1))
                    pe.wait_ge(s["e_xgT_a"], a + 1)
                    pe.wait_ge(s["e_xgT_d"], a + 1)
                    if not isinstance(i, int) or i:
                        pe.wait_ge(s["e_hid"], a - 1)
                    for k in range(KC):
                        mm = pe.matmul(psum[:, GU_PS[j]:GU_PS[j] + 2 * FE], xgT[j][:, k, :], wgu[j][:, k, :], start=(k == 0), stop=(k == KC - 1))
                    mm.then_inc(s["e_gu"], 1)

                def turn_hidden(i, j):
                    a = 2 * i + j
                    pe.wait_ge(s["e_hid"], a + 1)
                    pe.wait_ge(s["e_hidT"], a)
                    for c in range(2):
                        mm = pe.transpose(psum[:, HT_PS + c * P:HT_PS + (c + 1) * P], hid[j][:, c * P:(c + 1) * P], ident[:])
                    mm.then_inc(s["e_hid_turned"], 1)

                def down(i, j):
                    a = 2 * i + j
                    pe.wait_ge(s[f"e_wdn{j}"], 16 * (i + 1))
                    pe.wait_ge(s["e_hidT"], a + 1)
                    for h, free in enumerate(("e_y_a", "e_y_d")):
                        pe.wait_ge(s[free], a)
                        for c in range(2):
                            mm = pe.matmul(psum[:, Y_PS + 512 * h:Y_PS + 512 * (h + 1)], hidT[j][:, c, :], wdn[j][:, c, 512 * h:512 * (h + 1)],
                                           start=(c == 0), stop=(c == 1))
                    mm.then_inc(s["e_down"], 1)

                def step(i, j, more=2):
                    if more > 0:
                        gate_up(i + (j + 1) // 2, 1 - j)
                    turn_hidden(i, j)
                    if more > 1:
                        turn(i + 1, j)
                    down(i, j)
                turn(0, 0)
                turn(0, 1)
                gate_up(0, 0)
                with pe.Fori(0, STEPS // 2 - 1) as i:
                    step(i, 0)
                    step(i, 1)
                last = STEPS // 2
                step(last - 1, 0)
                step(last - 1, 1, 1)
                step(last, 0, 0)

            @block.scalar
            def _(act):
                def x_out(i, j):
                    a = 2 * i + j
                    act.wait_ge(s["e_turned"], a + 1)
                    if not isinstance(i, int) or i:
                        act.wait_ge(s["e_gu"], a - 1)
                    nc.scalar.copy(xgT[j][:, 0:4, :].rearrange("p k n -> p (k n)"), psum[:, XT_PS:XT_PS + 512]).then_inc(s["e_xgT_a"], 1)

                def sigmoid(i, j):
                    a = 2 * i + j
                    act.wait_ge(s["e_gu"], a + 1)
                    if not isinstance(i, int) or i:
                        act.wait_ge(s["e_hid_s"], a - 1)
                    nc.scalar.activation(sig[j][:], psum[:, GU_PS[j]:GU_PS[j] + FE], ACT.Sigmoid).then_inc(s["e_sig"], 1)

                def hidden_out(i, j):
                    a = 2 * i + j
                    act.wait_ge(s["e_hid_turned"], a + 1)
                    nc.scalar.copy(hidT[j][:].rearrange("p c n -> p (c n)"), psum[:, HT_PS:HT_PS + FE]).then_inc(s["e_hidT"], 1)

                def y_out(i, j):
                    a = 2 * i + j
                    act.wait_ge(s["e_down"], a + 1)
                    act.wait_ge(s[f"e_y_st{j}"], 16 * i)
                    nc.scalar.copy(yst[j][:, 0:512], psum[:, Y_PS:Y_PS + 512]).then_inc(s["e_y_a"], 1)

                def step(i, j, more=2):
                    if more > 0:
                        sigmoid(i + (j + 1) // 2, 1 - j)
                    hidden_out(i, j)
                    if more > 1:
                        x_out(i + 1, j)
                    y_out(i, j)
                x_out(0, 0)
                x_out(0, 1)
                sigmoid(0, 0)
                with act.Fori(0, STEPS // 2 - 1) as i:
                    step(i, 0)
                    step(i, 1)
                last = STEPS // 2
                step(last - 1, 0)
                step(last - 1, 1, 1)
                step(last, 0, 0)

            @block.vector
            def _(dve):
                def x_out(i, j):
                    a = 2 * i + j
                    dve.wait_ge(s["e_turned"], a + 1)
                    if not isinstance(i, int) or i:
                        dve.wait_ge(s["e_gu"], a - 1)
                    nc.vector.tensor_copy(xgT[j][:, 4:8, :].rearrange("p k n -> p (k n)"), psum[:, XT_PS + 512:XT_PS + 1024]).then_inc(s["e_xgT_d"], 1)

                def hidden(i, j):
                    a = 2 * i + j
                    dve.wait_ge(s["e_sig"], a + 1)
                    nc.vector.tensor_tensor(sig[j][:], sig[j][:], psum[:, GU_PS[j]:GU_PS[j] + FE], ALU.mult).then_inc(s["e_hid_s"], 1)
                    dve.wait_ge(s["e_hid_s"], a + 1)
                    if not isinstance(i, int) or i:
                        dve.wait_ge(s["e_hid_turned"], a - 1)
                    nc.vector.tensor_tensor(hid[j][:], sig[j][:], psum[:, GU_PS[j] + FE:GU_PS[j] + 2 * FE], ALU.mult).then_inc(s["e_hid"], 1)

                def y_out(i, j):
                    a = 2 * i + j
                    dve.wait_ge(s["e_down"], a + 1)
                    dve.wait_ge(s[f"e_y_st{j}"], 16 * i)
                    nc.vector.tensor_copy(yst[j][:, 512:1024], psum[:, Y_PS + 512:Y_PS + 1024]).then_inc(s["e_y_d"], 1)

                def step(i, j, more=2):
                    if more > 0:
                        hidden(i + (j + 1) // 2, 1 - j)
                    if more > 1:
                        x_out(i + 1, j)
                    y_out(i, j)
                x_out(0, 0)
                x_out(0, 1)
                hidden(0, 0)
                with dve.Fori(0, STEPS // 2 - 1) as i:
                    step(i, 0)
                    step(i, 1)
                last = STEPS // 2
                step(last - 1, 0)
                step(last - 1, 1, 1)
                step(last, 0, 0)
        if last_block == 5:
            return dict(x1=x1)

        y1 = [at(f"y1_{j}", [P, D], F32, RKV + 4 * j * KB) for j in range(4)]
        y2 = [at(f"y2_{j}", [P, D], F32, RKV + (16 + 4 * j) * KB) for j in range(4)]
        final_g = at("final_g", [P, D], F32, RKV + 32 * KB)
        junk = [at(f"junk{j}", [P, D], F32, RKV + (36 + 4 * j) * KB) for j in range(2)]
        for n in "g0 g1 g2 g3 final w1 join gated sum sq rt normed st dve_c".split():
            s["f_" + n] = sem("b6_" + n)

        with nc.Block() as block:
            @block.gpsimd
            def _(pool):
                def gather(t):
                    for c, buf in enumerate((y1, y2)):
                        nc.gpsimd.indirect_dma_start(buf[t % 4][:], None, io["ybuf"], bass.IndirectOffsetOnAxis(place_i[:, c, t:t + 1], 0)).then_inc(s[f"f_g{t % 4}"], 16)
                for t in range(4):
                    gather(t)
                for t in range(TILES):
                    pool.wait_ge(s["f_gated"], t + 1)
                    nc.gpsimd.tensor_tensor(x1[:, t, :], x1[:, t, :], y2[t % 4][:], ALU.add).then_inc(s["f_sum"], 1)
                    if t + 4 < TILES:
                        pool.wait_ge(s["f_sum"], t + 1)
                        gather(t + 4)

            @block.scalar
            def _(act):
                def weigh(t):
                    act.wait_ge(s[f"f_g{t % 4}"], 32 * (t // 4 + 1))
                    nc.scalar.mul(y1[t % 4][:], y1[t % 4][:], w_top[:, 0, t:t + 1]).then_inc(s["f_w1"], 1)
                weigh(0)
                for t in range(TILES):
                    if t + 1 < TILES:
                        weigh(t + 1)
                    act.wait_ge(s["f_sum"], t + 1)
                    nc.scalar.activation(junk[t % 2][:], x1[:, t, :], ACT.Square, accum_out=ssq[:, t:t + 1]).then_inc(s["f_sq"], 1)
                    act.wait_ge(s["f_sq"], t + 1)
                    nc.scalar.activation(rstd[:, t:t + 1], ssq[:, t:t + 1], ACT.Sqrt, bias=eps[:], scale=1.0 / D).then_inc(s["f_rt"], 1)

            @block.vector
            def _(dve):
                own = Tally(dve, s["f_dve_c"])
                tt, ts = nc.vector.tensor_tensor, nc.vector.tensor_scalar

                def finish(t):
                    dve.wait_ge(s["f_rt"], t + 1)
                    r, a, b = rstd[:, t:t + 1], nsq[:, t:t + 1], ntmp[:, t:t + 1]
                    own.step(ts(a, ssq[:, t:t + 1], 1.0 / D, EPS, ALU.mult, ALU.add))
                    own.step(nc.vector.reciprocal(r, r))
                    own.step(tt(b, r, r, ALU.mult))
                    own.step(tt(b, b, a, ALU.mult))
                    own.step(ts(b, b, -0.5, 1.5, ALU.mult, ALU.add))
                    own.step(tt(r, r, b, ALU.mult))
                    nc.vector.scalar_tensor_tensor(x1[:, t, :], x1[:, t, :], r, final_g[:], ALU.mult, ALU.mult).then_inc(s["f_normed"], 1)
                dve.wait_ge(s["f_final"], 16)
                for t in range(TILES):
                    dve.wait_ge(s["f_w1"], t + 1)
                    nc.vector.scalar_tensor_tensor(y2[t % 4][:], y2[t % 4][:], w_top[:, 1, t:t + 1], y1[t % 4][:], ALU.mult, ALU.add).then_inc(s["f_join"], 1)
                    dve.wait_ge(s["f_join"], t + 1)
                    tt(y2[t % 4][:], y2[t % 4][:], rowb[:, 4 + (t >= CTX_TILES), :], ALU.mult).then_inc(s["f_gated"], 1)
                    if t >= 2:
                        finish(t - 2)
                finish(TILES - 2)
                finish(TILES - 1)

            @block.sync
            def _(sp):
                sp.dma_start(final_g[:], io["final_g"].broadcast_to([P, D])).then_inc(s["f_final"], 16)
                for t in range(TILES):
                    sp.wait_ge(s["f_normed"], t + 1)
                    sp.dma_start(io["y"][t * P:(t + 1) * P, :], x1[:, t, :]).then_inc(s["f_st"], 16)
                sp.wait_ge(s["f_st"], 16 * TILES)
        return {}


ROUTE_TABLES = [("desc", EG), ("before", P), ("tile0", TILES), ("upto", NE * NE), ("slot0", SLOTS), ("slot", SLOTS), ("token", TILES),
                ("col", P), ("row", 1)]
ROUTE_W = sum(w for _, w in ROUTE_TABLES)


def route_tables():
    p, rep = np.arange(P), lambda v: np.broadcast_to(np.asarray(v).reshape(1, -1), (P, np.size(v)))
    tabs = {
        "desc": rep(np.arange(EG, 0, -1)),
        "before": p[:, None] < p[None, :],
        "tile0": rep(np.arange(TILES) * P),
        "upto": rep(np.arange(NE)[None, :] <= np.arange(NE)[:, None]),
        "slot0": rep(np.arange(SLOTS) * P), "slot": rep(np.arange(SLOTS)),
        "token": np.arange(TILES)[None, :] * P + p[:, None],
        "col": rep(p), "row": p[:, None],
    }
    return np.ascontiguousarray(np.concatenate([tabs[n].astype(np.float32) for n, _ in ROUTE_TABLES], axis=1))


def rope_tables():
    t = np.arange(LAT)
    nf = HD // 4
    freq = THETA ** (-np.arange(nf, dtype=np.float32) / np.float32(nf))
    pos = np.stack([t // GRID_W, t % GRID_W]).astype(np.float32)
    ang = (pos[:, None, :] * freq.astype(np.float32)[None, :, None]).astype(np.float32)
    c, s = np.cos(ang), np.sin(ang)
    cos = np.concatenate([c[0], c[0], c[1], c[1]]).astype(np.float32)
    sin = np.concatenate([s[0], -s[0], s[1], -s[1]]).astype(np.float32)
    return np.ascontiguousarray(cos), np.ascontiguousarray(sin)


def inverse_counts():
    out = np.zeros((4, TOK), np.float32)
    for g, w in enumerate((2, 4, 8, 16)):
        for o, l in STREAMS:
            t = np.arange(l)
            out[g, o:o + l] = 1.0 / (np.clip(t + w // 2, 0, l) - np.clip(t - w // 2, 0, l))
    return out


def layouts(a):
    c = np.ascontiguousarray
    pairs = lambda w: c(w.reshape(w.shape[0] // P, P, -1, PAIR).transpose(2, 1, 0, 3))
    cols = lambda v: v.reshape(-1, P).T
    order = [6, 7] + list(range(8, 16)) + [0, 1, 2, 3] + [4, 5]
    w_in = pairs(a["w_in"][0])[order]
    cos, sin = rope_tables()
    return {
        "x": c(np.concatenate([a["x_prompt"][0], a["x_sample"][0]]).reshape(TILES, P, D)),
        "cvec": c(np.stack([cols(a["c_ctx"]), cols(a["c"][0])], axis=2)),
        "vecs": c(np.concatenate([cols(a["b_ada"][0]), cols(a["norm1_g"][0]), cols(a["norm2_g"][0]), cols(a["q_norm_g"][0]),
                                  cols(a["k_norm_g"][0]), cols(a["pool_scale"][0])], axis=1)),
        "ident": np.eye(P, dtype=np.float32),
        "w_ada": pairs(a["w_ada"][0]), "w_in": c(w_in),
        "w_merge": pairs(np.concatenate([a["w_branch_a"][0], a["w_branch_b"][0]])), "w_out": pairs(a["w_out"][0]),
        "w_pool": c(a["w_pool"][0].transpose(1, 0, 2)),
        "icnt": inverse_counts(), "cos": cos, "sin": sin,
        "route": route_tables(),
        "w_route": c(np.concatenate([a["w_router_group"][0], a["w_router_expert"][0]], axis=1).reshape(KC, P, NR).transpose(1, 0, 2)),
        "w_gu": c(np.concatenate([a["w_exp_gate"][0], a["w_exp_up"][0]], axis=2).reshape(NE, KC, P, 2 * FE).transpose(0, 2, 1, 3).reshape(NE * P, -1)),
        "w_dn": c(a["w_exp_down"][0].reshape(NE, 2, P, D).transpose(0, 2, 1, 3).reshape(NE * P, -1)),
        "final_g": c(a["final_norm_g"][None, :]),
        "cache_k": c(a["cache_k"][0, 0].transpose(2, 1, 0)),
        "cache_v": c(a["cache_v"][0, 0].reshape(PAST // P, P, KV * HD).transpose(1, 0, 2)),
    }


def kernel(**inputs):
    import numpy as _np
    import concourse.bacc as _bacc
    from concourse import mybir as _mybir
    from concourse.bass_utils import run_bass_kernel_spmd as _run

    arrays = layouts({name: _np.asarray(a) for name, a in inputs.items()})
    nc = _bacc.Bacc("TRN2", target_bir_lowering=False, num_devices=1)
    f32 = _mybir.dt.float32
    io = {name: nc.dram_tensor("in_" + name, a.shape, f32, kind="ExternalInput").ap() for name, a in arrays.items()}
    for name, shape in (("y", (TOK, D)), ("out_k", (KV, HD, CTX)), ("out_v", (KV, HD, CTX))):
        io[name] = nc.dram_tensor(name, shape, f32, kind="ExternalOutput").ap()
    for name, shape in (("gates", (2 * KC, P, TOK)), ("poolT", (4, P, TOK)), ("h2d", (TOK, D)), ("ybuf", ((SLOTS - 1) * P, D))):
        io[name] = nc.dram_tensor(name, shape, f32).ap()
    build(nc, io)
    r = _run(nc, [{"in_" + name: a for name, a in arrays.items()}], core_ids=[0]).results[0]
    cache = [r[name].transpose(2, 0, 1).reshape(1, 1, CTX, KV, HD) for name in ("out_k", "out_v")]
    return r["y"][:CTX].reshape(1, CTX, D), r["y"][CTX:].reshape(1, LAT, D), cache[0], cache[1]
```

```python
from collections import namedtuple
from contextlib import ExitStack

import numpy as np

import concourse.bass as bass
from concourse import mybir

ALU = mybir.AluOpType
ACT = mybir.ActivationFunctionType
AX = mybir.AxisListType
F32 = mybir.dt.float32
F32R = mybir.dt.float32r
I32 = mybir.dt.int32

P = 128
D = 1024
CTX, LAT, PAST = 256, 1024, 512
TOK = CTX + LAT
TILES = TOK // P
CTX_TILES = CTX // P
KC = D // P
HEADS, KV, HD = 8, 2, 128
GRP = HEADS // KV
KEYS = TOK + PAST
KEY_TILES = KEYS // P
LAT_KEYS = LAT + PAST
EG, EPG, NE, FE = 4, 4, 16, 256
NR = EG + NE
EPS = 1e-6
GRID_W, THETA = 64, 10000.0
PAIR = 2 * P
N_ADA = 6 * D // PAIR
GROUPS = [(0, 512), (512, 512), (1024, 256)]
STREAMS = [(0, CTX), (CTX, LAT)]
PADW = 8
XPW = 4 * PADW + TOK
XSEG = [(PADW, 0, CTX), (3 * PADW + CTX, CTX, LAT)]
HALF = TILES // 2
HOME = 2
HOMES = HOME * NE
SPARE = max(min(k * -(-(TOK - HOME * P) // P), (2 * TOK - (HOME * P - P + 1) * k) // P) for k in range(1, NE + 1))
SLOTS = HOMES + SPARE


Unit = namedtuple("Unit", "u kv tok par keys key0")


class Tally:

    def __init__(self, eng, sem):
        self.eng, self.sem, self.n, self.extra = eng, sem, 0, 0

    def step(self, ins):
        ins.then_inc(self.sem, 1)
        self.n += 1
        self.eng.wait_ge(self.sem, self.extra + self.n)

    def enter(self, i, per):
        self.start, self.per, self.extra = self.n, per, i * per

    def leave(self, count):
        assert self.n - self.start == self.per, (self.n - self.start, self.per)
        self.n, self.extra = self.start + self.per * count, 0


def build(nc, io, last_block=99):
    with ExitStack() as ctx:
        base = (nc.sbuf_base + 31) // 32 * 32

        def at(name, shape, dt, off):
            return nc.alloc_sbuf_tensor_at(name, shape, dt, offset=base + off)

        early = []
        passed = nc.alloc_semaphore("passed")

        def sem(name):
            early.append(nc.alloc_semaphore(name))
            return early[-1]

        KB = 1024
        RA, RHL, RKV, RW, RS, RC = 0, 40 * KB, 120 * KB, 176 * KB, 200 * KB, 205 * KB
        psum = ctx.enter_context(nc.psum_tensor("psum", [P, 4096], F32))

        small_at = [RC]

        def small(name, shape):
            n = 4 * int(np.prod(shape[1:]))
            small_at[0] += (n + 31) // 32 * 32
            return at(name, shape, F32, small_at[0] - (n + 31) // 32 * 32)
        ident = small("ident", [P, P])
        ones = small("ones", [P, P])
        cc = small("cc", [P, KC, 2])
        cs = small("cs", [P, KC, 2])
        vecs = small("vecs", [P, 70])
        mods = small("mods", [P, 48, 2])
        m1 = small("m1", [P, KC, 2])
        m2 = small("m2", [P, KC, 2])
        eps = small("eps", [P, 1])
        ssq = small("ssq", [P, TILES])
        rstd = small("rstd", [P, TILES])
        rt = small("rt", [P, TILES])
        nsq = small("nsq", [P, TILES])
        ntmp = small("ntmp", [P, TILES])
        rmax = small("rmax", [P, 4])
        nmax = small("nmax", [P, 2, GRP])
        esum = small("esum", [P, 2, GRP])
        gate1 = small("gate1", [P, 4])
        einv = small("einv", [P, 2, GRP])
        short_max_, short_nmax, short_sum, short_inv = (small(n, [P, GRP]) for n in ("short_max", "short_nmax", "short_sum", "short_inv"))

        h_hi = at("h_hi", [P, KC, TOK], F32R, RHL)
        h_lo = at("h_lo", [P, KC, TOK], F32R, RHL + 40 * KB)
        xt = at("xt", [P, TILES, D], F32, RA)
        xnT = at("xnT", [P, KC, TOK], F32, RKV)
        ada = [at(f"ada{j}", [P, KC, PAIR], F32, RKV + (40 + 8 * j) * KB) for j in range(2)]
        ada_raw = ada + [at(f"ada_raw{j}", [P, KC, PAIR], F32, RHL + (40 + 8 * j) * KB) for j in range(4)]
        w_raw = at("w_raw", [P, KC, PAIR], F32, RW)
        w_hi = [at(f"w_hi{j}", [P, KC, P], F32R, RW + (8 + 8 * j) * KB) for j in range(2)]
        w_lo = [at(f"w_lo{j}", [P, KC, P], F32R, RW + (12 + 8 * j) * KB) for j in range(2)]
        stage = at("stage", [P, TOK], F32, RS)
        cs4 = at("cs4", [P, KC, P], F32R, RS)
        cs_full = at("cs_full", [P, KC, P], F32, RHL)
        sq_junk = at("sq_junk", [P, D], F32, RHL + 32 * KB)
        ada_hi = at("ada_hi", [P, KC, PAIR], F32R, RKV + 20 * KB)
        ada_lo = at("ada_lo", [P, KC, PAIR], F32R, RKV + 28 * KB)
        ada_rows = [at(f"ada_rows{j}", [P, PAIR], F32, o) for j, o in enumerate((RHL + 36 * KB, RHL + 37 * KB, RKV + 36 * KB, RKV + 37 * KB))]
        xpad = [at(f"xpad{j}", [P, XPW], F32, RA + 5376 * j) for j in range(2)]
        win = [at(f"win{j}", [P, XPW], F32, RA + 5376 * (2 + j)) for j in range(2)]
        icnt = at("icnt", [P, TOK], F32, RA + 5376 * 4)
        wpool = at("wpool", [P, 4, P], F32, RA + 27 * KB)
        gst = [at(f"gst{j}", [P, TOK], F32, RA + (30 + 5 * j) * KB) for j in range(2)]
        dpool = at("dpool", [P, 4, TOK], F32, RKV)
        qT = at("qT", [P, HEADS, TOK], F32, RA)
        cos = at("cos", [P, LAT], F32, RKV + 28 * KB)
        sin = at("sin", [P, LAT], F32, RKV + 32 * KB)
        rtmp = at("rtmp", [P, LAT], F32, RKV + 36 * KB)
        sq = [at(f"sq{j}", [P, TOK], F32, RKV + (40 + 5 * j) * KB) for j in range(2)]
        rsb = at("rsb", [P, TOK], F32, RKV + 50 * KB)
        kT_hi = at("kT_hi", [P, KV, KEYS], F32R, RKV)
        kT_lo = at("kT_lo", [P, KV, KEYS], F32R, RKV + 14 * KB)
        vals = at("vals", [P, KEY_TILES, KV * HD], F32, RKV + 28 * KB)
        kraw = [stage, at("kraw1", [P, TOK], F32, RKV + 40 * KB)]
        vraw = [stage, at("vraw1", [P, TOK], F32, RHL)]
        kc_raw = at("kc_raw", [P, KV, PAST], F32, RHL + 8 * KB)

        s = {}
        for n in ("eps_r x_ss rs_used consts rope wpool_in icnt_in x_sq x_scaled xT_ps xT_outa xT_outd c_in c_sig c_silu ada_mm0 ada_mm1 ada_lo_r0 ada_lo_r1 ada_rows0 ada_rows1 ada_turn mods_r0 mods_r1 ada_in0 ada_in1 "
                  "mods_b h_raw h_hi_r h_lo_p h_lo_d w_in0 w_hi0 w_hi1 w_lo0 w_lo1 mm0 mm1 ps_free0 ps_free1 pad0 xp_in xp_used "
                  "d_done gate_r0 gate_r1 gate_st0 gate_st1 py_ps py_out py_st sq_r0 sq_r1 ss_mm rt_sq rt_r rs_mm rs_out q_raw q_sin q_cos q_fin "
                  "k_fin k_hi k_lo kout v_raw vout v_ps v_out_a v_out_d cache_in cache_hi cache_lo dve_c").split():
            s[n] = sem("b1_" + n)
        x_in = [sem(f"x_in{t}") for t in range(TILES)]
        ada_first = [sem(f"ada_first{b}") for b in range(8)]

        XP_PAIRS, GATE_PAIRS, Q_PAIRS = 2, 8, 4
        G0, Q0, K0, V0 = 2, 10, 14, 15
        N_PAIRS = 16
        def pass_wait(pool):
            pool.sem_inc(passed, 1)
        par_sets = (0, 1536)
        AUX = (3072, 3584)
        rows_at = (3072, 2048, 3072, 3072)

        def v_chunk(n):
            j, (g, w) = n // 3, GROUPS[n % 3]
            return (vals[:, g // P:(g + w) // P, j * HD:(j + 1) * HD],
                    psum[:, AUX[n % 2]:AUX[n % 2] + w].rearrange("p (t d) -> p t d", d=P))

        with nc.Block() as block:
            @block.sync
            def _(sp):
                sp.dma_start(cc[:], io["cvec"]).then_inc(s["c_in"], 16)
                sp.dma_start(vecs[:], io["vecs"]).then_inc(s["consts"], 16)
                sp.dma_start(ident[:], io["ident"]).then_inc(s["consts"], 16)
                for t in range(TILES):
                    sp.dma_start(xt[:, t, :], io["x"][t]).then_inc(x_in[t], 16)
                for b in range(8):
                    if b >= 6:
                        sp.wait_ge(s[f"ada_mm{b % 2}"], 1)
                    sp.dma_start(ada_raw[b % 6][:], io["w_ada"][b]).then_inc(ada_first[b], 16)
                    if b == 4:
                        sp.dma_start(w_raw[:], io["w_in"][0]).then_inc(s["w_in0"], 16)

                def load_w(n):
                    sp.wait_ge(s["w_lo1"], n)
                    sp.dma_start(w_raw[:], io["w_in"][bass.ds(n, 1)].rearrange("o p k n -> p (o k) n")).then_inc(s["w_in0"], 16)
                def load_ada(n, j):
                    if isinstance(n, int):
                        sp.wait_ge(s[f"ada_mm{j}"], n)
                    else:
                        sp.wait_ge(s[f"ada_lo_r{j}"], n - 4)
                    sp.dma_start(ada[j][:], io["w_ada"][bass.ds(2 * n + j, 1)].rearrange("o p k n -> p (o k) n")).then_inc(s[f"ada_in{j}"], 16)

                load_w(1)
                load_ada(4, 0)
                load_ada(4, 1)
                sp.wait_ge(s["xT_ps"], TILES)
                sp.dma_start(wpool[:], io["w_pool"]).then_inc(s["wpool_in"], 16)
                for c in range(4):
                    if c:
                        sp.wait_ge(s["xp_used"], c)
                    sp.dma_start(icnt[:], io["icnt"][c:c + 1, :].broadcast_to([P, TOK])).then_inc(s["icnt_in"], 16)
                    if c == 1:
                        load_w(2)

                def store_gate(i, j):
                    sp.wait_ge(s[f"gate_r{j}"], i + 1)
                    sp.dma_start(io["gates"][bass.ds(2 * i + j, 1)].rearrange("o p n -> p (o n)"), gst[j][:]).then_inc(s[f"gate_st{j}"], 16)
                with sp.Fori(0, GATE_PAIRS - 1) as i:
                    load_w(i + G0 + 1)
                    load_ada(i + 5, 0)
                    store_gate(i, 0)
                    load_ada(i + 5, 1)
                    store_gate(i, 1)
                load_w(Q0)
                store_gate(GATE_PAIRS - 1, 0)
                store_gate(GATE_PAIRS - 1, 1)
                for c in range(4):
                    sp.wait_ge(s["py_out"], 3 * (c + 1))
                    sp.dma_start(io["poolT"][c], sq[c % 2][:]).then_inc(s["py_st"], 16)
                    sp.wait_ge(s["py_st"], 16 * (c + 1))
                    if c == 0:
                        sp.wait_ge(s["d_done"], 4)
                        sp.dma_start(cos[:], io["cos"]).then_inc(s["rope"], 16)
                        sp.dma_start(sin[:], io["sin"]).then_inc(s["rope"], 16)
                with sp.Fori(0, Q_PAIRS) as i:
                    load_w(i + Q0 + 1)
                load_w(V0)
                for j in range(2):
                    sp.wait_ge(s["q_raw"], HEADS + j + 1)
                    sp.dma_start(io["out_k"][j], kraw[j][:, 0:CTX]).then_inc(s["kout"], 16)
                for j in range(2):
                    sp.wait_ge(s["v_raw"], j + 1)
                    if j == 1:
                        sp.dma_start(kc_raw[:], io["cache_k"]).then_inc(s["cache_in"], 16)
                        sp.wait_ge(s["k_fin"], 2)
                        sp.dma_start(vals[:, TILES:KEY_TILES, :], io["cache_v"]).then_inc(s["cache_in"], 16)
                    sp.dma_start(io["out_v"][j], vraw[j][:, 0:CTX]).then_inc(s["vout"], 16)
                sp.wait_ge(s["kout"], 32)
                sp.wait_ge(s["vout"], 32)
                for j in range(2):
                    sp.wait_ge(s[f"gate_st{j}"], 16 * GATE_PAIRS)
                sp.wait_ge(s["cache_in"], 32)

            @block.tensor
            def _(pe):
                for t in range(TILES):
                    pe.wait_ge(s["x_scaled"], t + 1)
                    if t == 0:
                        pe.wait_ge(s["consts"], 32)
                    if t >= 2:
                        pe.wait_ge(s["xT_outa"], t - 1)
                        pe.wait_ge(s["xT_outd"], t - 1)
                    for k in range(KC):
                        o = (t % 2) * 1024 + k * P
                        mm = pe.transpose(psum[:, o:o + P], xt[:, t, k * P:(k + 1) * P], ident[:])
                    mm.then_inc(s["xT_ps"], 1)

                def ada_first_block(b):
                    pe.wait_ge(ada_first[b], 16)
                    pe.wait_ge(s[f"ada_rows{b % 2}"], b // 2)
                    for k in range(KC):
                        mm = pe.matmul(psum[:, rows_at[b % 2]:rows_at[b % 2] + PAIR], cs_full[:, k, :], ada_raw[b % 6][:, k, :],
                                       start=(k == 0), stop=(k == KC - 1))
                    mm.then_inc(s[f"ada_mm{b % 2}"], 1)

                def ada_block(n, j):
                    pe.wait_ge(s[f"ada_lo_r{j}"], n - 3)
                    pe.wait_ge(s[f"ada_rows{1 - j}"], n + j)
                    for part in (ada_hi, ada_lo):
                        for k in range(KC):
                            mm = pe.matmul(psum[:, rows_at[2]:rows_at[2] + PAIR], cs4[:, k, :], part[:, k, :],
                                           start=(k == 0 and part is ada_hi), stop=(k == KC - 1 and part is ada_lo))
                    mm.then_inc(s[f"ada_mm{j}"], 1)

                def ada_turn(n, j, buf):
                    pe.wait_ge(s[f"ada_rows{j}"], n + 1)
                    if j:
                        pe.wait_ge(s["mods_r0"], n + 1)
                    else:
                        pe.wait_ge(s["mods_r1"], n)
                    for m in range(2):
                        mm = pe.transpose(psum[:, AUX[1] + m * P:AUX[1] + (m + 1) * P], ada_rows[buf][:, m * P:(m + 1) * P], ident[:])
                    mm.then_inc(s["ada_turn"], 1)

                pe.wait_ge(s["c_silu"], 1)
                for b in range(9):
                    if b < 8:
                        ada_first_block(b)
                    if b:
                        ada_turn((b - 1) // 2, (b - 1) % 2, (b - 1) % 2)

                def project(n, j, first=False, hooks={}):
                    pe.wait_ge(s[f"w_hi{j}"], n + 1)
                    pe.wait_ge(s[f"w_lo{j}"], n + 1)
                    pe.wait_ge(s[f"ps_free{j}"], n)
                    for k in range(KC):
                        if first:
                            pe.wait_ge(s["h_hi_r"], k + 1)
                            pe.wait_ge(s["h_lo_p"] if k % 2 else s["h_lo_d"], k // 2 + 1)
                        for a, b in ((w_hi, h_hi), (w_hi, h_lo), (w_lo, h_hi)):
                            for g, w in GROUPS:
                                mm = pe.matmul(psum[:, par_sets[j] + g:par_sets[j] + g + w], a[j][:, k, :], b[:, k, g:g + w],
                                               start=(k == 0 and a is w_hi and b is h_hi), stop=(k == KC - 1 and a is w_lo))
                        if k in hooks:
                            hooks[k]()
                    mm.then_inc(s[f"mm{j}"], 1)

                pe.wait_ge(s["xT_outa"], TILES)
                pe.wait_ge(s["xT_outd"], TILES)
                for n in range(XP_PAIRS):
                    project(n, 0, first=(n == 0))
                    project(n, 1)
                with pe.Fori(0, GATE_PAIRS) as i:
                    for j in range(2):
                        project(i + G0, j, hooks={4: lambda: ada_block(i + 4, j), 7: lambda: ada_turn(i + 4, j, 2 + j)})
                pe.wait_ge(s["wpool_in"], 16)
                pe.wait_ge(s["d_done"], 4)
                pe.wait_ge(s["mods_b"], 1)

                def pooled(c):
                    for q, (g, w) in enumerate(GROUPS):
                        n = 3 * c + q
                        if n >= 2:
                            pe.wait_ge(s["py_out"], n - 1)
                        pe.matmul(psum[:, AUX[n % 2]:AUX[n % 2] + w], wpool[:, c, :], dpool[:, c, g:g + w],
                                  start=True, stop=True).then_inc(s["py_ps"], 1)
                project(Q0, 0, hooks={2 * c: lambda c=c: pooled(c) for c in range(4)})
                pe.wait_ge(s["py_out"], 12)

                def sums(n, j):
                    pe.wait_ge(s[f"sq_r{j}"], n + 1)
                    for t in range(TILES):
                        a = par_sets[j] + TOK + t
                        mm = pe.matmul(psum[:, a:a + 96], sq[j][:, t * P:(t + 1) * P], ones[:, 0:96], start=True, stop=True)
                    mm.then_inc(s["ss_mm"], 1)

                def spread(n, j):
                    pe.wait_ge(s["rt_r"], 2 * n + j + 1)
                    pe.wait_ge(s["rs_out"], 2 * (2 * n + j))
                    for t in range(TILES):
                        a = par_sets[j] + TOK + t * P if t < CTX_TILES else AUX[0] + (t - CTX_TILES) * P
                        mm = pe.transpose(psum[:, a:a + P], rt[:, t:t + 1].broadcast_to([P, P]), ident[:])
                    mm.then_inc(s["rs_mm"], 1)

                def hooks(n, j):
                    return {2: lambda: sums(n, j), 5: lambda: spread(n, j)}
                with pe.Fori(0, Q_PAIRS) as i:
                    project(i + Q0, 1, hooks=hooks(i, 0))
                    project(i + Q0 + 1, 0, hooks=hooks(i, 1))
                project(K0, 1, hooks=hooks(4, 0))
                project(V0, 0, hooks=hooks(4, 1))
                project(V0, 1)
                for j in range(2):
                    pe.wait_ge(s["v_raw"], j + 1)
                    for q, (g, w) in enumerate(GROUPS):
                        n = 3 * j + q
                        if n == 0:
                            pe.wait_ge(s["rs_out"], 20)
                        if n >= 2:
                            pe.wait_ge(s["v_out_d" if n % 2 else "v_out_a"], n // 2)
                        for r in range(w // P):
                            mm = pe.transpose(psum[:, AUX[n % 2] + r * P:AUX[n % 2] + (r + 1) * P],
                                              vraw[j][:, g + r * P:g + (r + 1) * P], ident[:])
                        mm.then_inc(s["v_ps"], 1)

            @block.scalar
            def _(act):
                def act_out(t):
                    act.wait_ge(s["xT_ps"], t + 1)
                    nc.scalar.copy(xnT[:, 0:4, t * P:(t + 1) * P],
                                   psum[:, (t % 2) * 1024:(t % 2) * 1024 + 512].rearrange("p (k n) -> p k n", n=P)).then_inc(s["xT_outa"], 1)

                act.wait_ge(s["c_in"], 16)
                act.wait_ge(s["eps_r"], 1)
                nc.scalar.activation(cs[:], cc[:], ACT.Sigmoid).then_inc(s["c_sig"], 1)
                for t in range(TILES):
                    act.wait_ge(x_in[t], 16)
                    if t:
                        act.wait_ge(s["x_ss"], t)
                    nc.scalar.activation(sq_junk[:], xt[:, t, :], ACT.Square, accum_out=ssq[:, t:t + 1]).then_inc(s["x_ss"], 1)
                    if t % HALF == HALF - 1:
                        act.wait_ge(s["x_ss"], t + 1)
                        h = slice(t + 1 - HALF, t + 1)
                        nc.scalar.activation(rstd[:, h], ssq[:, h], ACT.Sqrt, bias=eps[:], scale=1.0 / D).then_inc(s["x_sq"], 1)
                for t in range(TILES):
                    act_out(t)

                def split(n, j):
                    act.wait_ge(s["w_in0"], 16 * (n + 1))
                    act.wait_ge(s[f"mm{j}"], n)
                    nc.scalar.copy(w_hi[j][:], w_raw[:, :, j * P:(j + 1) * P]).then_inc(s[f"w_hi{j}"], 1)
                split(0, 0)
                split(0, 1)
                for k in range(KC):
                    act.wait_ge(s["h_raw"], k + 1)
                    nc.scalar.copy(h_hi[:, k, :], xnT[:, k, :]).then_inc(s["h_hi_r"], 1)
                for n in range(XP_PAIRS):
                    for j in range(2):
                        act.wait_ge(s[f"mm{j}"], n + 1)
                        act.wait_ge(s["pad0"], 6)
                        if n:
                            act.wait_ge(s["d_done"], j + 1)
                        for (o, g, w) in XSEG:
                            ins = nc.scalar.copy(xpad[j][:, o:o + w], psum[:, par_sets[j] + g:par_sets[j] + g + w])
                            ins.then_inc(s["xp_in"], 1)
                        act.wait_ge(s["xp_in"], 2 * (2 * n + j + 1))
                        act.sem_inc(s[f"ps_free{j}"], 1)
                        split(n + 1, j)
                with act.Fori(0, GATE_PAIRS) as i:
                    for j in range(2):
                        act.wait_ge(s[f"mm{j}"], i + G0 + 1)
                        act.wait_ge(s[f"gate_st{j}"], 16 * i)
                        nc.scalar.activation(gst[j][:], psum[:, par_sets[j]:par_sets[j] + TOK], ACT.Sigmoid).then_inc(s[f"gate_r{j}"], 1)
                        act.wait_ge(s[f"gate_r{j}"], i + 1)
                        act.sem_inc(s[f"ps_free{j}"], 1)
                        split(i + G0 + 1, j)
                for c in range(4):
                    for q, (g, w) in enumerate(GROUPS):
                        n = 3 * c + q
                        act.wait_ge(s["py_ps"], n + 1)
                        if c >= 2:
                            act.wait_ge(s["py_st"], 16 * (c - 1))
                        nc.scalar.mul(sq[c % 2][:, g:g + w], psum[:, AUX[n % 2]:AUX[n % 2] + w],
                                      vecs[:, 66 + c:67 + c]).then_inc(s["py_out"], 1)

                def square(n, j):
                    act.wait_ge(s[f"mm{j}"], n + Q0 + 1)
                    if j == 0:
                        act.wait_ge(s["ss_mm"], 2 * n)
                    else:
                        act.wait_ge(s["ss_mm"], 2 * n + 1)
                    nc.scalar.activation(sq[j][:], psum[:, par_sets[j]:par_sets[j] + TOK], ACT.Square).then_inc(s[f"sq_r{j}"], 1)

                def root(n, j):
                    act.wait_ge(s["ss_mm"], 2 * n + j + 1)
                    act.wait_ge(s["rs_mm"], 2 * n + j)
                    nc.scalar.activation(rt[:], psum[:, par_sets[j] + TOK:par_sets[j] + TOK + TILES], ACT.Sqrt,
                                         bias=eps[:], scale=1.0 / HD).then_inc(s["rt_sq"], 1)
                    act.wait_ge(s["rs_mm"], 2 * n + j + 1)
                    act.wait_ge(s["rs_used"], 2 * n + j)
                    nc.scalar.copy(rsb[:, 0:CTX], psum[:, par_sets[j] + TOK:par_sets[j] + TOK + CTX]).then_inc(s["rs_out"], 1)
                    nc.scalar.copy(rsb[:, CTX:TOK], psum[:, AUX[0]:AUX[0] + LAT]).then_inc(s["rs_out"], 1)
                act.wait_ge(s["py_st"], 64)
                with act.Fori(0, Q_PAIRS) as i:
                    for j in range(2):
                        square(i, j)
                        split(i + Q0 + 1, j)
                        root(i, j)
                for j in range(2):
                    square(4, j)
                    split(V0, j)
                    root(4, j)
                for j in range(2):
                    act.wait_ge(s["k_fin"], j + 1)
                    nc.scalar.copy(kT_hi[:, j, 0:TOK], kraw[j][:]).then_inc(s["k_hi"], 1)
                act.wait_ge(s["k_lo"], 2)
                act.wait_ge(s["kout"], 32)
                for j in range(2):
                    act.wait_ge(s[f"mm{j}"], V0 + 1)
                    if j == 1:
                        act.wait_ge(s["mm1"], V0 + 1)
                    nc.scalar.copy(vraw[j][:], psum[:, par_sets[j]:par_sets[j] + TOK]).then_inc(s["v_raw"], 1)
                act.wait_ge(s["q_fin"], HEADS)
                act.wait_ge(s["k_fin"], 2)
                for n in range(0, 6, 2):
                    act.wait_ge(s["v_ps"], n + 1)
                    nc.scalar.copy(*v_chunk(n)).then_inc(s["v_out_a"], 1)
                act.wait_ge(s["cache_in"], 32)
                nc.scalar.copy(kT_hi[:, :, TOK:KEYS], kc_raw[:]).then_inc(s["cache_hi"], 1)

            @block.gpsimd
            def _(pool):
                def split(n, j):
                    pool.wait_ge(s[f"w_hi{j}"], n + 1)
                    nc.gpsimd.tensor_tensor(w_lo[j][:], w_raw[:, :, j * P:(j + 1) * P], w_hi[j][:], ALU.subtract).then_inc(s[f"w_lo{j}"], 1)
                split(0, 0)
                split(0, 1)
                for k in range(1, KC, 2):
                    pool.wait_ge(s["h_hi_r"], k + 1)
                    nc.gpsimd.tensor_tensor(h_lo[:, k, :], xnT[:, k, :], h_hi[:, k, :], ALU.subtract).then_inc(s["h_lo_p"], 1)
                for n in range(1, G0 + 1):
                    split(n, 0)
                    split(n, 1)
                with pool.Fori(0, GATE_PAIRS) as i:
                    split(i + G0 + 1, 0)
                    split(i + G0 + 1, 1)
                with pool.Fori(0, Q_PAIRS) as i:
                    for j in range(2):
                        split(i + Q0 + 1, j)
                        pool.wait_ge(s["q_sin"], 2 * i + j + 1)
                        q_lat = qT[:, bass.ds(2 * i + j, 1), CTX:TOK].rearrange("p o n -> p (o n)")
                        nc.gpsimd.tensor_tensor(q_lat, q_lat, cos[:], ALU.mult).then_inc(s["q_cos"], 1)
                for j in range(2):
                    split(V0, j)
                    pool.wait_ge(s["q_sin"], HEADS + j + 1)
                    nc.gpsimd.tensor_tensor(kraw[j][:, CTX:TOK], kraw[j][:, CTX:TOK], cos[:], ALU.mult).then_inc(s["q_cos"], 1)
                for j in range(2):
                    pool.wait_ge(s["k_hi"], j + 1)
                    nc.gpsimd.tensor_tensor(kT_lo[:, j, 0:TOK], kraw[j][:], kT_hi[:, j, 0:TOK], ALU.subtract).then_inc(s["k_lo"], 1)
                pool.wait_ge(s["cache_hi"], 1)
                nc.gpsimd.tensor_tensor(kT_lo[:, :, TOK:KEYS], kc_raw[:], kT_hi[:, :, TOK:KEYS], ALU.subtract).then_inc(s["cache_lo"], 1)

            @block.vector
            def _(dve):
                own = Tally(dve, s["dve_c"])

                def inverse(r, a, t):
                    own.step(nc.vector.reciprocal(r, r))
                    own.step(nc.vector.tensor_tensor(t, r, r, ALU.mult))
                    own.step(nc.vector.tensor_tensor(t, t, a, ALU.mult))
                    own.step(nc.vector.tensor_scalar(t, t, -0.5, 1.5, ALU.mult, ALU.add))
                    own.step(nc.vector.tensor_tensor(r, r, t, ALU.mult))
                own.step(nc.vector.memset(eps[:], EPS))
                dve.sem_inc(s["eps_r"], 1)
                own.step(nc.vector.memset(ones[:], 1.0))
                dve.wait_ge(s["c_sig"], 1)
                own.step(nc.vector.tensor_tensor(cs[:], cs[:], cc[:], ALU.mult))
                parts = cs4[:].rearrange("p k (r q z) -> p k r q z", q=2, z=2)
                silu = cs[:].unsqueeze(2).broadcast_to([P, KC, P // 4, 2])
                own.step(nc.vector.tensor_copy(parts[:, :, :, 0, :], silu))
                own.step(nc.vector.tensor_tensor(parts[:, :, :, 1, :], silu, parts[:, :, :, 0, :], ALU.subtract))
                parts = cs_full[:].rearrange("p k (r q z) -> p k r q z", q=2, z=2)
                own.step(nc.vector.memset(parts[:, :, :, 1, :], 0.0))
                own.step(nc.vector.tensor_copy(parts[:, :, :, 0, :], silu))
                dve.sem_inc(s["c_silu"], 1)
                dve.wait_ge(s["consts"], 32)

                def dve_out(t):
                    dve.wait_ge(s["xT_ps"], t + 1)
                    nc.vector.tensor_copy(xnT[:, 4:8, t * P:(t + 1) * P],
                                          psum[:, (t % 2) * 1024 + 512:(t % 2) * 1024 + 1024].rearrange("p (k n) -> p k n", n=P)).then_inc(s["xT_outd"], 1)
                for t in range(TILES):
                    if t % HALF == 0:
                        h = slice(t, t + HALF)
                        dve.wait_ge(s["x_sq"], t // HALF + 1)
                        own.step(nc.vector.tensor_scalar(nsq[:, h], ssq[:, h], 1.0 / D, EPS, ALU.mult, ALU.add))
                        inverse(rstd[:, h], nsq[:, h], ntmp[:, h])
                    r = rstd[:, t:t + 1]
                    nc.vector.tensor_scalar(xt[:, t, :], xt[:, t, :], r, None, ALU.mult).then_inc(s["x_scaled"], 1)
                    if t:
                        dve_out(t - 1)
                dve_out(TILES - 1)

                def rows_out(n, j, buf):
                    dve.wait_ge(s[f"ada_mm{j}"], n + 1)
                    nc.vector.tensor_copy(ada_rows[buf][:], psum[:, rows_at[buf]:rows_at[buf] + PAIR]).then_inc(s[f"ada_rows{j}"], 1)

                def take_mods(n, j):
                    dve.wait_ge(s["ada_turn"], 2 * n + j + 1)
                    turned = psum[:, AUX[1]:AUX[1] + PAIR].rearrange("p (m r) -> p m r", m=2)
                    m = mods[:, bass.ds(4 * n + 2 * j, 2), :]
                    own.step(nc.vector.tensor_tensor(m, turned[:, :, 2:4], vecs[:, bass.ds(4 * n + 2 * j, 2)].unsqueeze(2).broadcast_to([P, 2, 2]), ALU.add))
                    own.step(nc.vector.tensor_tensor(m, m, turned[:, :, 0:2], ALU.add))
                    dve.sem_inc(s[f"mods_r{j}"], 1)

                def norm_gain(m, a, g):
                    own.step(nc.vector.tensor_scalar(m[:], mods[:, a:a + KC, :], 1.0, None, ALU.add))
                    own.step(nc.vector.tensor_tensor(m[:], m[:], vecs[:, g:g + KC].unsqueeze(2).broadcast_to([P, KC, 2]), ALU.mult))
                for b in range(10):
                    if 1 <= b < 9:
                        rows_out((b - 1) // 2, (b - 1) % 2, (b - 1) % 2)
                    if b >= 2:
                        take_mods((b - 2) // 2, b % 2)
                norm_gain(m1, KC, 48)
                dve.wait_ge(s["xT_outa"], TILES)
                dve.wait_ge(s["xT_outd"], TILES)
                for k in range(KC + 1):
                    if k < KC:
                        for q, (g, w) in enumerate(STREAMS):
                            v = xnT[:, k, g:g + w]
                            ins = nc.vector.tensor_scalar(v, v, m1[:, k, q:q + 1], mods[:, k, q:q + 1], ALU.mult, ALU.add)
                            if q == 0:
                                own.step(ins)
                        ins.then_inc(s["h_raw"], 1)
                    if k % 2:
                        dve.wait_ge(s["h_hi_r"], k)
                        nc.vector.tensor_tensor(h_lo[:, k - 1, :], xnT[:, k - 1, :], h_hi[:, k - 1, :], ALU.subtract).then_inc(s["h_lo_d"], 1)
                dve.wait_ge(s["xT_ps"], TILES)
                for j in range(2):
                    for a, b in ((0, PADW), (PADW + CTX, 3 * PADW + CTX), (XPW - PADW, XPW)):
                        nc.vector.memset(xpad[j][:, a:b], 0.0).then_inc(s["pad0"], 1)
                dve.wait_ge(s["pad0"], 6)
                dve.wait_ge(s["h_lo_p"], 4)

                def ada_split(n, j):
                    dve.wait_ge(s[f"ada_in{j}"], 16 * (n - 3))
                    dve.wait_ge(s[f"ada_mm{1 - j}"], n + j)
                    own.step(nc.vector.tensor_copy(ada_hi[:], ada[j][:]))
                    nc.vector.tensor_tensor(ada_lo[:], ada[j][:], ada_hi[:], ALU.subtract).then_inc(s[f"ada_lo_r{j}"], 1)
                ada_split(4, 0)
                for c in range(4):
                    j = c % 2
                    dve.wait_ge(s["xp_in"], 2 * (c + 1))
                    src = xpad[j]
                    lo, hi = 1, XPW
                    own.step(nc.vector.tensor_tensor(win[0][:, 1:XPW], src[:, 0:XPW - 1], src[:, 1:XPW], ALU.add))
                    src, sh = win[0], 1
                    for d in range(c):
                        dst = win[(d + 1) % 2]
                        lo, hi = lo + sh, hi - sh
                        own.step(nc.vector.tensor_tensor(dst[:, lo:hi], src[:, lo - sh:hi - sh], src[:, lo + sh:hi + sh], ALU.add))
                        src, sh = dst, 2 * sh
                    dve.wait_ge(s["icnt_in"], 16 * (c + 1))
                    for (o, g, w) in XSEG:
                        ins = nc.vector.tensor_tensor(dpool[:, c, g:g + w], src[:, o:o + w], icnt[:, g:g + w], ALU.mult)
                        ins.then_inc(own.sem, 1)
                        own.n += 1
                    dve.wait_ge(own.sem, own.n)
                    dve.sem_inc(s["xp_used"], 1)
                    for (o, g, w) in XSEG:
                        ins = nc.vector.tensor_tensor(dpool[:, c, g:g + w], dpool[:, c, g:g + w], xpad[j][:, o:o + w], ALU.subtract)
                        own.step(ins)
                    dve.sem_inc(s["d_done"], 1)
                with dve.Fori(0, GATE_PAIRS - 1) as i:
                    own.enter(i, 6)
                    for j in range(2):
                        rows_out(i + 4, j, 2 + j)
                        take_mods(i + 4, j)
                        ada_split(i + 4 + j, 1 - j)
                    own.leave(GATE_PAIRS - 1)
                rows_out(11, 0, 2)
                take_mods(11, 0)
                ada_split(11, 1)
                rows_out(11, 1, 3)
                take_mods(11, 1)
                norm_gain(m2, 4 * KC, 56)
                dve.sem_inc(s["mods_b"], 1)

                def norm_rope(n, j, dst_all, dst_parts):
                    dve.wait_ge(s["rt_sq"], 2 * n + j + 1)
                    own.step(nc.vector.tensor_scalar(nsq[:], psum[:, par_sets[j] + TOK:par_sets[j] + TOK + TILES], 1.0 / HD, EPS,
                                                     ALU.mult, ALU.add))
                    inverse(rt[:], nsq[:], ntmp[:])
                    dve.sem_inc(s["rt_r"], 1)
                    dve.wait_ge(s["rs_out"], 2 * (2 * n + j + 1))
                    is_k = isinstance(n, int)
                    own.step(nc.vector.scalar_tensor_tensor(out=dst_all, in0=psum[:, par_sets[j]:par_sets[j] + TOK],
                                                            scalar=vecs[:, 64 + int(is_k):65 + int(is_k)], in1=rsb[:], op0=ALU.mult, op1=ALU.mult))
                    dve.sem_inc(s[f"ps_free{j}"], 1)
                    dve.sem_inc(s["rs_used"], 1)
                    dve.sem_inc(s["q_raw"], 1)
                    for a in range(0, P, 32):
                        b = a ^ 32
                        own.step(nc.vector.tensor_tensor(rtmp[a:a + 32, :], dst_parts(b, b + 32), sin[b:b + 32, :], ALU.mult))
                    dve.sem_inc(s["q_sin"], 1)
                    dve.wait_ge(s["q_cos"], 2 * n + j + 1)
                    own.step(nc.vector.tensor_tensor(dst_parts(0, P), dst_parts(0, P), rtmp[:], ALU.add))

                dve.wait_ge(s["rope"], 32)
                dve.wait_ge(s["py_ps"], 12)
                for j in range(2):
                    dve.wait_ge(s[f"gate_st{j}"], 16 * GATE_PAIRS)
                with dve.Fori(0, Q_PAIRS) as i:
                    own.enter(i, 24)
                    for j in range(2):
                        h = bass.ds(2 * i + j, 1)
                        norm_rope(i, j, qT[:, h, :].rearrange("p o n -> p (o n)"),
                                  lambda a, b: qT[a:b, h, CTX:TOK].rearrange("p o n -> p (o n)"))
                        dve.sem_inc(s["q_fin"], 1)
                    own.leave(Q_PAIRS)
                for j in range(2):
                    norm_rope(4, j, kraw[j][:], lambda a, b: kraw[j][a:b, CTX:TOK])
                    dve.sem_inc(s["k_fin"], 1)
                for n in range(1, 6, 2):
                    dve.wait_ge(s["v_ps"], n + 1)
                    nc.vector.tensor_copy(*v_chunk(n)).then_inc(s["v_out_d"], 1)
        if last_block == 1:
            return dict(vals=vals, qT=qT, kT_hi=kT_hi, kT_lo=kT_lo, mods=mods)

        nc.clear_and_free_semaphores(early)
        nc.all_engine_barrier()

        pool_hi = at("pool_hi", [P, 4, TOK], F32R, RKV)
        pool_lo = at("pool_lo", [P, 4, TOK], F32R, RKV + 20 * KB)
        pool_raw = at("pool_raw", [P, 4, TOK], F32, RKV + 20 * KB)
        KM = KC + 4
        wm_hi = [at(f"wm_hi{j}", [P, KM, P], F32R, RKV + (42 + 12 * j) * KB) for j in range(2)]
        wm_lo = [at(f"wm_lo{j}", [P, KM, P], F32R, RKV + (48 + 12 * j) * KB) for j in range(2)]
        wm_raw = at("wm_raw", [P, KM, PAIR], F32, RW + 12 * KB)
        merged = at("merged", [P, KC, TOK], F32, RA)
        wo_raw = at("wo_raw", [P, KC, PAIR], F32, RW + 12 * KB)
        wo_hi = [at(f"wo_hi{j}", [P, KC, P], F32R, RKV + (42 + 8 * j) * KB) for j in range(2)]
        wo_lo = [at("wo_lo0", [P, KC, P], F32R, RKV + 46 * KB), at("wo_lo1", [P, KC, P], F32R, RW + 20 * KB)]
        ost = [stage, at("ost1", [P, TOK], F32, RKV)]
        x1 = at("x1", [P, TILES, D], F32, RA)
        for n in ("wm_in wm_hi0 wm_hi1 wm_lo0 wm_lo1 at_hi at_lo_d at_lo_p pl_in pl_hi pl_lo ga_in0 ga_in1 gb_in mmA mmB a_out b_out merged "
                  "mg_hi mg_lo_d mg_lo_p wo_in wo_hi0 wo_hi1 wo_lo0 wo_lo1 mmO0 mmO1 ost_r0 ost_r1 o_turn o_add "
                  "x_in dve_c act_c").split():
            s["m_" + n] = sem("b3_" + n)
        H_LO_POOL = (3, 7)
        lo_before = [sum(k not in H_LO_POOL for k in range(n)) for n in range(KC + 1)]

        prob = [at(f"prob{j}", [P, GRP, LAT_KEYS], F32, RHL + 24 * j * KB) for j in range(2)]
        probT = [[at(f"probT{b}_{j}", [P, GRP * P], F32, RHL + (48 + 4 * b + 2 * j) * KB) for j in range(2)] for b in range(3)]
        q_hi = [at(f"q_hi{j}", [P, GRP, P], F32R, RHL + (60 + 4 * j) * KB) for j in range(2)]
        q_lo = [at(f"q_lo{j}", [P, GRP, P], F32R, RHL + (62 + 4 * j) * KB) for j in range(2)]
        SC, TP, PV = 0, 1536, 3072
        SCALE = HD ** -0.5
        for n in ("q_hi_r q_lo_r scored neg_max exped normed turned0 turned1 turned2 t_out0 t_out1 t_out2 "
                  "pv0 pv1 pv2 pv_unit pv_out dve_c fill").split():
            s["a_" + n] = sem("b2_" + n)
        for n in "q_hi q_lo scored neg_max exped normed turned out_a out_d pv pv_out".split():
            s["c_" + n] = sem("b2_short_" + n)

        def latent(u, kv):
            qt = u - 8 * kv
            return Unit(u, kv, (qt + CTX_TILES) * P, None, LAT_KEYS, CTX)

        units = [latent(u, u // 8)._replace(par=u % 2) for u in range(16)]
        short = [Unit(z, z // 2, z % 2 * P, 0, CTX, 0) for z in range(4)]
        sq_hi = at("sq_hi", [P, GRP, P], F32R, RW)
        sq_lo = at("sq_lo", [P, GRP, P], F32R, RW + 2 * KB)
        sprob = at("sprob", [P, GRP, CTX], F32, RW + 4 * KB)
        sprobT = [at(f"sprobT{c}", [P, GRP * P], F32, RW + (8 + 2 * c) * KB) for c in range(2)]

        def uses(x, g):
            return 4 * x.u + g

        def banks_scored(x, g):
            return 12 * x.u + 3 * g

        def chunks(x, g):
            return range(3 * g, 3 * g + 3)

        def over_units(eng, head, block_, after, tail, own=None, per=0, short_score=lambda z: None, short_norm=lambda z: None,
                       short_turn=lambda z: None, short_value=lambda z: None):
            def step(w, x, n):
                for g in range(GRP):
                    block_(w, g)
                    after(x, g)
                    if g < GRP - 1:
                        head(x, g + 1)
                if n is not None:
                    head(n, 0)
                tail(w)

            for g in range(GRP + 1):
                head(units[g // GRP], g % GRP)
                if g:
                    short_turn(g - 1)
                if g < GRP:
                    short_score(g)
                    after(units[0], g)
                if g:
                    short_value(g - 1)
                if g < GRP:
                    short_norm(g)
            for kv in range(KV):
                with eng.Fori(0, 3) as i:
                    if own:
                        own.enter(i, per)
                    for r in (1, 2):
                        w, x, n = (latent(2 * i + 8 * kv + r + d, kv)._replace(par=(r + d) % 2) for d in (-1, 0, 1))
                        step(w, x, n)
                    if own:
                        own.leave(3)
                for u in ((7, 8) if kv == 0 else (15,)):
                    step(units[u - 1], units[u], units[u + 1] if u < 15 else None)
            for g in range(GRP):
                block_(units[15], g)
            tail(units[15])

        SS, TC, SV = 1536, (2560, 3072), 3584

        def turned_out(eng, copy, x, g, b, m):
            eng.wait_ge(s[f"a_turned{b}"], m + 1)
            copy(probT[b][g % 2][:], psum[:, TP + 512 * b:TP + 512 * b + 512]).then_inc(s[f"a_t_out{b}"], 1)

        with nc.Block() as block:
            @block.sync
            def _(sp):
                sp.dma_start(wm_raw[:], io["w_merge"][0]).then_inc(s["m_wm_in"], 16)
                x = io["x"].rearrange("t p d -> (t p) d")
                for first in range(HOMES * P, SLOTS * P, TOK):
                    n = min(TOK, SLOTS * P - first)
                    sp.dma_start(io["ybuf"][first:first + n, :], x[0:n, :]).then_inc(s["a_fill"], 16)
                    sp.wait_ge(s["a_fill"], 16 * ((first - HOMES * P) // TOK + 1))

            @block.tensor
            def _(pe):
                def head(x, g):
                    if g == 0:
                        pe.wait_ge(s["a_q_lo_r"], x.u + 1)
                    pe.wait_ge(s["a_exped"], 4 * x.u + g)
                    for b in range(3):
                        o = psum[:, SC + 512 * b:SC + 512 * (b + 1)]
                        k = slice(x.key0 + 512 * b, x.key0 + 512 * (b + 1))
                        pe.matmul(o, q_hi[x.par][:, g, :], kT_hi[:, x.kv, k], start=True, stop=False)
                        pe.matmul(o, q_hi[x.par][:, g, :], kT_lo[:, x.kv, k], start=False, stop=False)
                        pe.matmul(o, q_lo[x.par][:, g, :], kT_hi[:, x.kv, k], start=False, stop=True).then_inc(s["a_scored"], 1)

                def values(x, c):
                    b, g = c % 3, c // 3
                    m = uses(x, g)
                    pe.wait_ge(s[f"a_t_out{b}"], m + 1)
                    mm = pe.matmul(psum[:, PV + 512 * x.par:PV + 512 * x.par + 512], vals[:, x.key0 // P + c, x.kv * HD:(x.kv + 1) * HD],
                                   probT[b][g % 2][:], start=(c == 0), stop=(c == x.keys // P - 1))
                    mm.then_inc(s[f"a_pv{b}"], 1)
                    if c == x.keys // P - 1:
                        pe.wait_ge(s[f"a_pv{b}"], m + 1)
                        pe.sem_inc(s["a_pv_unit"], 1)

                def block_(x, g):
                    if g == 0:
                        pe.wait_ge(s["a_normed"], 4 * x.u + 4)
                    for c in chunks(x, g):
                        b = c % 3
                        pe.wait_ge(s[f"a_t_out{b}"], uses(x, g))
                        for h in range(GRP):
                            o = TP + 512 * b + h * P
                            mm = pe.transpose(psum[:, o:o + P], prob[x.par][:, h, c * P:(c + 1) * P], ident[:])
                        mm.then_inc(s[f"a_turned{b}"], 1)
                        if c >= 3:
                            values(x, c - 3)

                def tail(x):
                    for c in range(x.keys // P)[-3:]:
                        values(x, c)
                def short_score(z):
                    x = short[z]
                    pe.wait_ge(s["c_q_lo"], z + 1)
                    pe.wait_ge(s["c_exped"], GRP * z)
                    for g in range(GRP):
                        o = psum[:, SS + CTX * g:SS + CTX * (g + 1)]
                        pe.matmul(o, sq_hi[:, g, :], kT_hi[:, x.kv, 0:CTX], start=True, stop=False)
                        pe.matmul(o, sq_hi[:, g, :], kT_lo[:, x.kv, 0:CTX], start=False, stop=False)
                        mm = pe.matmul(o, sq_lo[:, g, :], kT_hi[:, x.kv, 0:CTX], start=False, stop=True)
                    mm.then_inc(s["c_scored"], 1)

                def short_turn(z):
                    pe.wait_ge(s["c_normed"], z + 1)
                    pe.wait_ge(s["c_out_a"], z)
                    pe.wait_ge(s["c_out_d"], z)
                    for c in range(2):
                        for h in range(GRP):
                            mm = pe.transpose(psum[:, TC[c] + h * P:TC[c] + (h + 1) * P], sprob[:, h, c * P:(c + 1) * P], ident[:])
                        mm.then_inc(s["c_turned"], 1)

                def short_value(z):
                    x = short[z]
                    pe.wait_ge(s["c_pv_out"], z)
                    for c, copied in enumerate(("c_out_a", "c_out_d")):
                        pe.wait_ge(s[copied], z + 1)
                        mm = pe.matmul(psum[:, SV:SV + 512], vals[:, c, x.kv * HD:(x.kv + 1) * HD], sprobT[c][:], start=(c == 0), stop=(c == 1))
                    mm.then_inc(s["c_pv"], 1)
                over_units(pe, head, block_, lambda x, g: None, tail, short_score=short_score, short_turn=short_turn, short_value=short_value)

            @block.scalar
            def _(act):
                def head(x, g):
                    act.wait_ge(s["a_neg_max"], 4 * x.u + g + 1)
                    if g == 0 and (not isinstance(x.u, int) or x.u > 1):
                        for b in range(3):
                            act.wait_ge(s[f"a_turned{b}"], 4 * x.u - 4)
                    nc.scalar.activation(prob[x.par][:, g, 0:x.keys], psum[:, SC:SC + x.keys], ACT.Exp, bias=nmax[:, x.par, g:g + 1],
                                         scale=SCALE, accum_out=esum[:, x.par, g:g + 1]).then_inc(s["a_exped"], 1)

                def block_(x, g):
                    for c in chunks(x, g):
                        b, m = c % 3, uses(x, g)
                        if b == 1:
                            continue
                        turned_out(act, nc.scalar.copy, x, g, b, m)

                def tail(x):
                    act.wait_ge(s["a_pv_unit"], x.u + 1)
                    nc.scalar.copy(qT[:, x.kv * GRP:(x.kv + 1) * GRP, bass.ds(x.tok, P)],
                                   psum[:, PV + 512 * x.par:PV + 512 * x.par + 512].rearrange("p (h n) -> p h n", n=P)).then_inc(s["a_pv_out"], 1)
                def short_score(z):
                    act.wait_ge(s["c_neg_max"], z + 1)
                    act.wait_ge(s["c_turned"], 2 * z)
                    for g in range(GRP):
                        nc.scalar.activation(sprob[:, g, :], psum[:, SS + CTX * g:SS + CTX * (g + 1)], ACT.Exp, bias=short_nmax[:, g:g + 1],
                                             scale=SCALE, accum_out=short_sum[:, g:g + 1]).then_inc(s["c_exped"], 1)

                def short_turn(z):
                    act.wait_ge(s["c_turned"], 2 * z + 1)
                    nc.scalar.copy(sprobT[0][:], psum[:, TC[0]:TC[0] + 512]).then_inc(s["c_out_a"], 1)

                def short_value(z):
                    x = short[z]
                    act.wait_ge(s["c_pv"], z + 1)
                    nc.scalar.copy(qT[:, x.kv * GRP:(x.kv + 1) * GRP, x.tok:x.tok + P],
                                   psum[:, SV:SV + 512].rearrange("p (h n) -> p h n", n=P)).then_inc(s["c_pv_out"], 1)
                over_units(act, head, block_, lambda x, g: None, tail, short_score=short_score, short_turn=short_turn, short_value=short_value)

            @block.gpsimd
            def _(pool):
                def split(x):
                    if not isinstance(x.u, int) or x.u > 1:
                        pool.wait_ge(s["a_scored"], 12 * x.u - 12)
                    q = qT[:, x.kv * GRP:(x.kv + 1) * GRP, bass.ds(x.tok, P)]
                    pass_wait(pool)
                    nc.gpsimd.tensor_copy(q_hi[x.par][:], q).then_inc(s["a_q_hi_r"], 1)
                    pool.wait_ge(s["a_q_hi_r"], x.u + 1)
                    pass_wait(pool)
                    nc.gpsimd.tensor_tensor(q_lo[x.par][:], q, q_hi[x.par][:], ALU.subtract).then_inc(s["a_q_lo_r"], 1)

                def head(x, g):
                    if g == 0:
                        split(x)

                def short_score(z):
                    x = short[z]
                    pool.wait_ge(s["c_scored"], z)
                    q = qT[:, x.kv * GRP:(x.kv + 1) * GRP, x.tok:x.tok + P]
                    nc.gpsimd.tensor_copy(sq_hi[:], q).then_inc(s["c_q_hi"], 1)
                    pool.wait_ge(s["c_q_hi"], z + 1)
                    nc.gpsimd.tensor_tensor(sq_lo[:], q, sq_hi[:], ALU.subtract).then_inc(s["c_q_lo"], 1)

                def short_value(z):
                    if z == len(short) - 1:
                        pool.wait_ge(s["m_wm_in"], 16)
                        nc.gpsimd.tensor_copy(wm_hi[0][:], wm_raw[:, :, 0:P]).then_inc(s["m_wm_hi0"], 1)
                        pool.wait_ge(s["m_wm_hi0"], 1)
                        nc.gpsimd.tensor_tensor(wm_lo[0][:], wm_raw[:, :, 0:P], wm_hi[0][:], ALU.subtract).then_inc(s["m_wm_lo0"], 1)
                over_units(pool, head, lambda x, g: None, lambda x, g: None, lambda x: None, short_score=short_score, short_value=short_value)

            @block.vector
            def _(dve):
                own = Tally(dve, s["a_dve_c"])

                def head(x, g):
                    for b in range(3):
                        dve.wait_ge(s["a_scored"], banks_scored(x, g) + b + 1)
                        ins = nc.vector.reduce_max(rmax[:, b:b + 1], psum[:, SC + 512 * b:SC + 512 * (b + 1)], AX.X)
                    own.step(ins)
                    own.step(nc.vector.reduce_max(rmax[:, 3:4], rmax[:, 0:3], AX.X))
                    nc.vector.tensor_scalar(nmax[:, x.par, g:g + 1], rmax[:, 3:4], -SCALE, None, ALU.mult).then_inc(s["a_neg_max"], 1)

                def block_(x, g):
                    for c in chunks(x, g):
                        if c % 3 == 1:
                            turned_out(dve, nc.vector.tensor_copy, x, g, 1, uses(x, g))

                def after(x, g):
                    dve.wait_ge(s["a_exped"], 4 * x.u + g + 1)
                    own.step(nc.vector.reciprocal(einv[:, x.par, g:g + 1], esum[:, x.par, g:g + 1]))
                    v = prob[x.par][:, g, 0:x.keys]
                    nc.vector.tensor_scalar(v, v, einv[:, x.par, g:g + 1], None, ALU.mult).then_inc(s["a_normed"], 1)
                def short_score(z):
                    dve.wait_ge(s["c_scored"], z + 1)
                    dve.wait_ge(s["c_neg_max"], z)
                    own.step(nc.vector.reduce_max(short_max_[:], psum[:, SS:SS + GRP * CTX].rearrange("p (g k) -> p g k", k=CTX), AX.X))
                    nc.vector.tensor_scalar(short_nmax[:], short_max_[:], -SCALE, None, ALU.mult).then_inc(s["c_neg_max"], 1)

                def short_norm(z):
                    dve.wait_ge(s["c_exped"], GRP * (z + 1))
                    dve.wait_ge(s["c_normed"], z)
                    own.step(nc.vector.reciprocal(short_inv[:], short_sum[:]))
                    nc.vector.tensor_tensor(sprob[:], sprob[:], short_inv[:].unsqueeze(2).broadcast_to([P, GRP, CTX]), ALU.mult).then_inc(s["c_normed"], 1)

                def short_turn(z):
                    dve.wait_ge(s["c_turned"], 2 * z + 2)
                    nc.vector.tensor_copy(sprobT[1][:], psum[:, TC[1]:TC[1] + 512]).then_inc(s["c_out_d"], 1)
                over_units(dve, head, block_, after, lambda x: None, own, 24, short_score, short_norm, short_turn)
        if last_block == 2:
            return dict(qT=qT)

        with nc.Block() as block:
            @block.sync
            def _(sp):
                def load_wm(n):
                    sp.wait_ge(s["m_wm_lo1"], n)
                    sp.dma_start(wm_raw[:], io["w_merge"][bass.ds(n, 1)].rearrange("o p k n -> p (o k) n")).then_inc(s["m_wm_in"], 16)

                def load_wo(n):
                    sp.wait_ge(s["m_wo_lo1"], n)
                    sp.dma_start(wo_raw[:], io["w_out"][bass.ds(n, 1)].rearrange("o p k n -> p (o k) n")).then_inc(s["m_wo_in"], 16)
                sp.dma_start(pool_raw[:], io["poolT"].rearrange("c p n -> p c n")).then_inc(s["m_pl_in"], 16)
                sp.wait_ge(s["m_at_hi"], KC)
                sp.wait_ge(s["m_at_lo_d"], KC - len(H_LO_POOL))
                sp.wait_ge(s["m_at_lo_p"], len(H_LO_POOL))

                def load_gates(n, j):
                    sp.dma_start(merged[:, bass.ds(2 * n + j, 1), :].rearrange("p o n -> p (o n)"),
                                 io["gates"][bass.ds(2 * n + j, 1)].rearrange("o p n -> p (o n)")).then_inc(s[f"m_ga_in{j}"], 16)
                    sp.wait_ge(s["m_merged"], 2 * n + j)
                    sp.dma_start(stage[:], io["gates"][bass.ds(2 * n + j + KC, 1)].rearrange("o p n -> p (o n)")).then_inc(s["m_gb_in"], 16)
                with sp.Fori(0, 3) as i:
                    load_gates(i, 0)
                    load_wm(i + 1)
                    load_gates(i, 1)
                load_gates(3, 0)
                sp.wait_ge(s["m_wm_lo1"], 4)
                load_wo(0)
                load_gates(3, 1)
                for k in range(KC):
                    if k in H_LO_POOL:
                        sp.wait_ge(s["m_mg_lo_p"], H_LO_POOL.index(k) + 1)
                    else:
                        sp.wait_ge(s["m_mg_lo_d"], lo_before[k] + 1)
                sp.dma_start(x1[:], io["x"].rearrange("t p d -> p t d")).then_inc(s["m_x_in"], 16)
                with sp.Fori(0, 3) as i:
                    load_wo(i + 1)

            @block.tensor
            def _(pe):
                def product(o, w_h, w_l, j, a_hi, a_lo, k0, k1, sem_, ready=None, hooks={}):
                    for k in range(k0, k1):
                        if ready:
                            ready(k - k0)
                        for a, b in ((w_h, a_hi), (w_h, a_lo), (w_l, a_hi)):
                            for g, w in GROUPS:
                                mm = pe.matmul(psum[:, o + g:o + g + w], a[j][:, k, :], b[:, k - k0, g:g + w],
                                               start=(k == k0 and a is w_h and b is a_hi), stop=(k == k1 - 1 and a is w_l))
                        if k in hooks:
                            hooks[k]()
                    mm.then_inc(sem_, 1)

                def attn_ready(k):
                    pe.wait_ge(s["m_at_hi"], k + 1)
                    pe.wait_ge(s["m_at_lo_p"], H_LO_POOL.index(k) + 1) if k in H_LO_POOL else pe.wait_ge(s["m_at_lo_d"], lo_before[k] + 1)

                def pool_ready(k):
                    pe.wait_ge(s["m_pl_hi"], k + 1)
                    pe.wait_ge(s["m_pl_lo"], k + 1)

                def branches(n, j, first=False):
                    pe.wait_ge(s[f"m_wm_hi{j}"], n + 1)
                    pe.wait_ge(s[f"m_wm_lo{j}"], n + 1)
                    pe.wait_ge(s["m_a_out"], 2 * n + j)
                    product(par_sets[0], wm_hi, wm_lo, j, h_hi, h_lo, 0, KC, s["m_mmA"], attn_ready if first else None)
                    pe.wait_ge(s["m_b_out"], 2 * n + j)
                    product(par_sets[1], wm_hi, wm_lo, j, pool_hi, pool_lo, KC, KM, s["m_mmB"], pool_ready if first else None)
                branches(0, 0, True)
                branches(0, 1)
                with pe.Fori(0, 3) as i:
                    branches(i + 1, 0)
                    branches(i + 1, 1)

                def merged_ready(k):
                    pe.wait_ge(s["m_mg_hi"], k + 1)
                    pe.wait_ge(s["m_mg_lo_p"], H_LO_POOL.index(k) + 1) if k in H_LO_POOL else pe.wait_ge(s["m_mg_lo_d"], lo_before[k] + 1)

                def turn(n, j):
                    pe.wait_ge(s[f"m_ost_r{j}"], 2 * n + 2)
                    for q, (g, w) in enumerate(GROUPS):
                        m = 6 * n + 3 * j + q
                        bank = AUX[(3 * j + q) % 2]
                        pe.wait_ge(s["m_o_add"], m - 1) if not isinstance(m, int) or m > 1 else None
                        for t in range(g // P, (g + w) // P):
                            mm = pe.transpose(psum[:, bank + t * P - g:bank + (t + 1) * P - g], ost[j][:, t * P:(t + 1) * P], ident[:])
                        mm.then_inc(s["m_o_turn"], 1)

                def out(n, j, ready=None, hooks={}):
                    pe.wait_ge(s[f"m_wo_hi{j}"], n + 1)
                    pe.wait_ge(s[f"m_wo_lo{j}"], n + 1)
                    pe.wait_ge(s[f"m_ost_r{j}"], 2 * n)
                    product(par_sets[j], wo_hi, wo_lo, j, h_hi, h_lo, 0, KC, s[f"m_mmO{j}"], ready, hooks)
                pe.wait_ge(s["m_a_out"], KC)
                out(0, 0, merged_ready)
                pe.wait_ge(s["m_b_out"], KC)
                out(0, 1, hooks={3: lambda: turn(0, 0)})
                with pe.Fori(0, 3) as i:
                    out(i + 1, 0, hooks={3: lambda: turn(i, 1)})
                    out(i + 1, 1, hooks={3: lambda: turn(i + 1, 0)})
                turn(3, 1)

            @block.scalar
            def _(act):
                def split_wm(n, j):
                    act.wait_ge(s["m_wm_in"], 16 * (n + 1))
                    act.wait_ge(s["m_mmB"], 2 * n - 1 + j) if not isinstance(n, int) or n else None
                    nc.scalar.copy(wm_hi[j][:], wm_raw[:, :, j * P:(j + 1) * P]).then_inc(s[f"m_wm_hi{j}"], 1)
                for k in range(KC):
                    nc.scalar.copy(h_hi[:, k, :], qT[:, k, :]).then_inc(s["m_at_hi"], 1)
                act.wait_ge(s["m_pl_in"], 16)
                for k in range(4):
                    nc.scalar.copy(pool_hi[:, k, :], pool_raw[:, k, :]).then_inc(s["m_pl_hi"], 1)
                split_wm(0, 1)
                with act.Fori(0, 3) as i:
                    split_wm(i + 1, 0)
                    split_wm(i + 1, 1)

                def split_wo(n, j):
                    act.wait_ge(s["m_wo_in"], 16 * (n + 1))
                    act.wait_ge(s[f"m_mmO{j}"], n)
                    nc.scalar.copy(wo_hi[j][:], wo_raw[:, :, j * P:(j + 1) * P]).then_inc(s[f"m_wo_hi{j}"], 1)
                act.wait_ge(s["m_mmB"], KC - 1)
                split_wo(0, 0)
                split_wo(0, 1)
                act.wait_ge(s["m_mmA"], KC)
                for k in range(KC):
                    act.wait_ge(s["m_merged"], k + 1)
                    nc.scalar.copy(h_hi[:, k, :], merged[:, k, :]).then_inc(s["m_mg_hi"], 1)

                def out(n, j, more=True):
                    act.wait_ge(s[f"m_mmO{j}"], n + 1)
                    for q, (g, w) in enumerate(STREAMS):
                        nc.scalar.mul(ost[j][:, g:g + w], psum[:, par_sets[j] + g:par_sets[j] + g + w],
                                      gate1[:, 2 * j + q:2 * j + q + 1]).then_inc(s[f"m_ost_r{j}"], 1)
                    if more:
                        split_wo(n + 1, j)
                own = Tally(act, s["m_act_c"])
                with act.Fori(0, 3) as i:
                    own.enter(i, 1)
                    for j in range(2):
                        act.wait_ge(s[f"m_ost_r{j}"], 2 * i)
                    own.step(nc.scalar.copy(gate1[:], mods[:, bass.ds(2 * i + 2 * KC, 2), :].rearrange("p m q -> p (m q)")))
                    out(i, 0)
                    out(i, 1)
                    own.leave(3)
                for j in range(2):
                    act.wait_ge(s[f"m_ost_r{j}"], 6)
                own.step(nc.scalar.copy(gate1[:], mods[:, 3 * KC - 2:3 * KC, :].rearrange("p m q -> p (m q)")))
                out(3, 0, False)
                out(3, 1, False)

            @block.gpsimd
            def _(pool):
                def split_wm(n, j):
                    pool.wait_ge(s[f"m_wm_hi{j}"], n + 1)
                    nc.gpsimd.tensor_tensor(wm_lo[j][:], wm_raw[:, :, j * P:(j + 1) * P], wm_hi[j][:], ALU.subtract).then_inc(s[f"m_wm_lo{j}"], 1)
                for k in H_LO_POOL:
                    pool.wait_ge(s["m_at_hi"], k + 1)
                    nc.gpsimd.tensor_tensor(h_lo[:, k, :], qT[:, k, :], h_hi[:, k, :], ALU.subtract).then_inc(s["m_at_lo_p"], 1)
                split_wm(0, 1)
                with pool.Fori(0, 3) as i:
                    split_wm(i + 1, 0)
                    split_wm(i + 1, 1)

                def split_wo(n, j):
                    pool.wait_ge(s[f"m_wo_hi{j}"], n + 1)
                    nc.gpsimd.tensor_tensor(wo_lo[j][:], wo_raw[:, :, j * P:(j + 1) * P], wo_hi[j][:], ALU.subtract).then_inc(s[f"m_wo_lo{j}"], 1)
                split_wo(0, 0)
                split_wo(0, 1)
                for k in H_LO_POOL:
                    pool.wait_ge(s["m_mg_hi"], k + 1)
                    nc.gpsimd.tensor_tensor(h_lo[:, k, :], merged[:, k, :], h_hi[:, k, :], ALU.subtract).then_inc(s["m_mg_lo_p"], 1)
                with pool.Fori(0, 3) as i:
                    split_wo(i + 1, 0)
                    split_wo(i + 1, 1)

            @block.vector
            def _(dve):
                own = Tally(dve, s["m_dve_c"])
                for k in range(KC):
                    if k not in H_LO_POOL:
                        dve.wait_ge(s["m_at_hi"], k + 1)
                        nc.vector.tensor_tensor(h_lo[:, k, :], qT[:, k, :], h_hi[:, k, :], ALU.subtract).then_inc(s["m_at_lo_d"], 1)
                for k in range(4):
                    dve.wait_ge(s["m_pl_hi"], k + 1)
                    nc.vector.tensor_tensor(pool_lo[:, k, :], pool_raw[:, k, :], pool_hi[:, k, :], ALU.subtract).then_inc(s["m_pl_lo"], 1)
                with dve.Fori(0, 4) as i:
                    own.enter(i, 6)
                    for j in range(2):
                        v = merged[:, bass.ds(2 * i + j, 1), :].rearrange("p o n -> p (o n)")
                        dve.wait_ge(s[f"m_ga_in{j}"], 16 * (i + 1))
                        dve.wait_ge(s["m_mmA"], 2 * i + j + 1)
                        own.step(nc.vector.tensor_tensor(v, v, psum[:, par_sets[0]:par_sets[0] + TOK], ALU.mult))
                        dve.sem_inc(s["m_a_out"], 1)
                        dve.wait_ge(s["m_gb_in"], 32 * i + 16 * (j + 1))
                        dve.wait_ge(s["m_mmB"], 2 * i + j + 1)
                        own.step(nc.vector.tensor_tensor(stage[:], stage[:], psum[:, par_sets[1]:par_sets[1] + TOK], ALU.mult))
                        dve.sem_inc(s["m_b_out"], 1)
                        own.step(nc.vector.tensor_tensor(v, v, stage[:], ALU.add))
                        dve.sem_inc(s["m_merged"], 1)
                    own.leave(4)
                for k in range(KC):
                    if k not in H_LO_POOL:
                        dve.wait_ge(s["m_mg_hi"], k + 1)
                        nc.vector.tensor_tensor(h_lo[:, k, :], merged[:, k, :], h_hi[:, k, :], ALU.subtract).then_inc(s["m_mg_lo_d"], 1)
                dve.wait_ge(s["m_x_in"], 16)
                with dve.Fori(0, 4) as i:
                    for j in range(2):
                        for q, (g, w) in enumerate(GROUPS):
                            dve.wait_ge(s["m_o_turn"], 6 * i + 3 * j + q + 1)
                            bank = AUX[(3 * j + q) % 2]
                            v = x1[:, g // P:(g + w) // P, bass.ds((2 * i + j) * P, P)]
                            nc.vector.tensor_tensor(v, v, psum[:, bank:bank + w].rearrange("p (t n) -> p t n", n=P), ALU.add).then_inc(s["m_o_add"], 1)
        if last_block == 3:
            return dict(x1=x1)

        h2 = at("h2", [P, TILES, D], F32, RHL)
        h2T = [at(f"h2T{j}", [P, KC, P], F32, RHL + (40 + 4 * j) * KB) for j in range(2)]
        rowb = at("rowb", [P, 6, D], F32, RHL + 48 * KB)
        route = at("route", [P, ROUTE_W], F32, RHL + 72 * KB)
        r_at = [RKV + 48 * KB]

        def routed(name, shape, dt=F32):
            r_at[0] += (4 * int(np.prod(shape[1:])) + 31) // 32 * 32
            return at(name, shape, dt, r_at[0] - (4 * int(np.prod(shape[1:])) + 31) // 32 * 32)
        w_route = routed("w_route", [P, KC, NR])
        logits_T = routed("logits_T", [P, TOK])
        logits = routed("logits", [P, TILES, NR])
        gmax, psel, v1, v2, wexp = (routed(n, [P, TILES]) for n in ("gmax", "psel", "v1", "v2", "wexp"))
        rsub, geq, gsel = (routed(n, [P, TILES, EG]) for n in ("rsub", "geq", "gsel"))
        e_in, eeq, rest = (routed(n, [P, TILES, EPG]) for n in ("e_in", "eeq", "rest"))
        pick = [routed(f"pick{c}", [P, TILES, EPG]) for c in range(2)]
        by_expert = routed("by_expert", [P, TILES, EG, EPG])
        chosen = [routed(f"chosen{c}", [P, TILES, EG, EPG]) for c in range(2)]
        either = routed("either", [P, TILES, NE], F32R)
        before_r = routed("before_r", [P, P], F32R)
        ones_r = routed("ones_r", [P, P], F32R)
        place = routed("place", [P, TILES, NE])
        rsum = routed("rsum", [P, TILES])
        count = routed("count", [P, NE])
        fills = routed("fills", [P, NE, TILES])
        n_tiles, ends, starts = (routed(n, [P, NE]) for n in ("n_tiles", "ends", "starts"))
        sums = routed("sums", [P, NE, NE])
        past = routed("past", [P, SPARE, NE])
        owner = routed("owner", [P, SPARE])
        beyond = routed("beyond", [P, TILES, NE])
        pos = routed("pos", [P, 2, TILES])
        posA, posB = (routed(n, [P, 2 * TILES]) for n in ("posA", "posB"))
        above = routed("above", [P, 2 * TILES, SLOTS])
        hotB = routed("hotB", [P, 2 * TILES, P], F32R)
        hotA = routed("hotA", [P, 2 * TILES, SLOTS], F32R)
        assert r_at[0] <= RC
        k_at = [RHL + 75 * KB]

        def kept(name, shape, dt):
            k_at[0] += (4 * int(np.prod(shape[1:])) + 31) // 32 * 32
            return at(name, shape, dt, k_at[0] - (4 * int(np.prod(shape[1:])) + 31) // 32 * 32)
        ids = kept("ids", [P, SLOTS], I32)
        wrow = kept("wrow", [P, SPARE], I32)
        n_spare = kept("n_spare", [P, 1], I32)
        place_i = kept("place_i", [P, 2, TILES], I32)
        w_top = kept("w_top", [P, 2, TILES], F32)
        assert k_at[0] <= RKV
        o = 0
        tabs = {}
        for n, w in ROUTE_TABLES:
            tabs[n] = route[:, o:o + w]
            o += w
        for n in "tabs sq_d lg_out lg_turned sq rt rows rows_out consts wr h2_a h2_d h2_st turned out logit g_max e_sum e_dif e_w mask ranks onehot ids_ps dve_c".split():
            s["r_" + n] = sem("b4_" + n)
        gu_raw = [at(f"gu_raw{q}", [P, KC, 2 * FE], F32, RKV + 16 * q * KB) for q in range(2)]
        gu_lo = [at(f"gu_lo{q}", [P, KC, 2 * FE], F32R, RKV + 16 * q * KB) for q in range(2)]
        gu_hi = [at(f"gu_hi{q}", [P, KC, 2 * FE], F32R, RKV + (32 + 16 * q) * KB) for q in range(2)]
        dn_hi = [at(f"dn_hi{q}", [P, 2, D], F32R, RKV + (64 + 8 * q) * KB) for q in range(2)]
        dn_raw = [at(f"dn_raw{q}", [P, 2, D], F32, RHL + 8 * q * KB) for q in range(2)]
        dn_lo = [at(f"dn_lo{q}", [P, 2, D], F32R, RHL + 8 * q * KB) for q in range(2)]
        xg = [at(f"xg{j}", [P, D], F32, RHL + (16 + 4 * j) * KB) for j in range(2)]
        x_hi = [at(f"x_hi{j}", [P, KC, P], F32R, RHL + (24 + 4 * j) * KB) for j in range(2)]
        x_lo = [at(f"x_lo{j}", [P, KC, P], F32R, RHL + (32 + 4 * j) * KB) for j in range(2)]
        xT = at("xT", [P, KC, P], F32, RHL + 24 * KB)
        yst = [at(f"yst{j}", [P, D], F32, RHL + (40 + 4 * j) * KB) for j in range(2)]
        sig = [at(f"sig{j}", [P, FE], F32, RHL + (48 + j) * KB) for j in range(2)]
        hid = [at(f"hid{j}", [P, FE], F32, RHL + (50 + j) * KB) for j in range(2)]
        hid_hi = [at(f"hid_hi{j}", [P, 2, P], F32R, RHL + (52 + j) * KB) for j in range(2)]
        hid_lo = [at(f"hid_lo{j}", [P, 2, P], F32R, RHL + (54 + j) * KB) for j in range(2)]
        hidT = at("hidT", [P, 2, P], F32, RHL + 56 * KB)
        x_row = [kept(f"x_row{j}", [P, 1], I32) for j in range(2)]
        w_gu = io["w_gu"].rearrange("(e p) (k n) -> e p k n", p=P, n=2 * FE)
        w_dn = io["w_dn"].rearrange("(e p) (k n) -> e p k n", p=P, n=D)
        XT_PS, GU_PS, HT_PS, Y_PS = 0, (1024, 1536), 2048, 3072
        GU_DVE = 6
        for n in ("pool_c xg0 xg1 turned x_hi x_lo gu_in0 gu_in1 dn_in0 dn_in1 gu_hi0 gu_hi1 gu_lo0 gu_lo1 gu_lp0 gu_lp1 dn_hi0 dn_hi1 "
                  "dn_lo0 dn_lo1 gu sig hid_s hid hid_turned hid_hi hid_lo down y_a y_d y_st0 y_st1").split():
            s["e_" + n] = sem("b5_" + n)
        for n in "pool_c in turned xT gu sig hid_s hid hid_turned hidT down y y_st".split():
            s["o_" + n] = sem("b5b_" + n)

        def over_steps(eng, step):
            with eng.Fori(0, NE // 2 - 1) as i:
                for r in range(4):
                    step(i, r)
            for r, more in enumerate((2, 2, 1, 0)):
                step(NE // 2 - 1, r, more)

        SQ_DVE = 3
        ROWS = [(m2, 0, 0), (m2, 0, 1), (mods, 3 * KC, 0), (mods, 3 * KC, 1), (mods, 5 * KC, 0), (mods, 5 * KC, 1)]
        LG_T, LG, RANKS, COUNTS, IDS = 2048, 3584, 0, 512, 1024

        with nc.Block() as block:
            @block.sync
            def _(sp):
                sp.dma_start(route[:], io["route"]).then_inc(s["r_consts"], 16)
                sp.dma_start(w_route[:], io["w_route"]).then_inc(s["r_wr"], 16)
                for e in range(2):
                    sp.dma_start(gu_raw[e][:], w_gu[e:e + 1].rearrange("o p k n -> p (o k) n")).then_inc(s[f"e_gu_in{e}"], 16)
                for t in range(TILES):
                    sp.wait_ge(s["r_h2_a"], t + 1)
                    sp.dma_start(io["h2d"][t * P:(t + 1) * P, :], h2[:, t, :]).then_inc(s["r_h2_st"], 16)
                sp.wait_ge(s["r_h2_st"], 16 * TILES)

            @block.tensor
            def _(pe):
                def rows(rs, banks):
                    for n, r in enumerate(rs):
                        v, c, q = ROWS[r]
                        for k in range(KC):
                            o = n % banks * 1024 + k * P
                            mm = pe.matmul(psum[:, o:o + P], v[:, c + k, q:q + 1].broadcast_to([P, P]), ident[:], start=True, stop=True)
                        mm.then_inc(s["r_rows"], 1)
                rows(range(4), 4)
                pe.wait_ge(s["r_rows_out"], 4)

                def logit(t):
                    pe.wait_ge(s["r_out"], t + 1)
                    for k in range(KC):
                        mm = pe.matmul(psum[0:NR, LG_T + t * P:LG_T + (t + 1) * P], w_route[:, k, :], h2T[t % 2][:, k, :],
                                       start=(k == 0), stop=(k == KC - 1))
                    mm.then_inc(s["r_logit"], 1)
                pe.wait_ge(s["r_wr"], 16)
                for t in range(TILES):
                    pe.wait_ge(s["r_h2_a"], t + 1)
                    if t >= 2:
                        pe.wait_ge(s["r_out"], t - 1)
                    for k in range(KC):
                        o = (t % 2) * 1024 + k * P
                        mm = pe.transpose(psum[:, o:o + P], h2[:, t, k * P:(k + 1) * P], ident[:])
                    mm.then_inc(s["r_turned"], 1)
                    if t:
                        logit(t - 1)
                logit(TILES - 1)
                pe.wait_ge(s["r_lg_out"], 1)
                for t in range(TILES):
                    mm = pe.transpose(psum[:, LG + t * NR:LG + (t + 1) * NR], logits_T[0:NR, t * P:(t + 1) * P], ident[0:NR, 0:NR])
                mm.then_inc(s["r_lg_turned"], 1)
                rows(range(4, 6), 2)

                pe.wait_ge(s["r_rows_out"], 6)
                pe.wait_ge(s["r_mask"], 1)
                pe.wait_ge(s["r_tabs"], 2)
                n = TILES * NE
                m = either[:].rearrange("p t e -> p (t e)")
                pe.matmul(psum[:, RANKS:RANKS + n], before_r[:], m, start=True, stop=False)
                for d in range(1, TILES):
                    mm = pe.matmul(psum[:, RANKS + d * NE:RANKS + n], ones_r[:], m[:, 0:n - d * NE], start=False, stop=(d == TILES - 1))
                for t in range(TILES):
                    mm = pe.matmul(psum[:, COUNTS:COUNTS + NE], ones_r[:], either[:, t, :], start=(t == 0), stop=(t == TILES - 1))
                mm.then_inc(s["r_ranks"], 1)
                pe.wait_ge(s["r_onehot"], 1)
                for c in range(2 * TILES):
                    mm = pe.matmul(psum[:, IDS:IDS + SLOTS], hotB[:, c, :], hotA[:, c, :], start=(c == 0), stop=(c == 2 * TILES - 1))
                mm.then_inc(s["r_ids_ps"], 1)

            @block.scalar
            def _(act):
                nc.scalar.activation(rt[:, 0:1], eps[:], ACT.Sqrt)
                for t in range(SQ_DVE, TILES):
                    nc.scalar.activation(h2[:, t, :], x1[:, t, :], ACT.Square, accum_out=ssq[:, t:t + 1]).then_inc(s["r_sq"], 1)
                act.wait_ge(s["r_sq"], TILES - SQ_DVE)
                act.wait_ge(s["r_sq_d"], SQ_DVE)
                nc.scalar.activation(rstd[:], ssq[:], ACT.Sqrt, bias=eps[:], scale=1.0 / D).then_inc(s["r_rt"], 1)
                for t in range(TILES):
                    act.wait_ge(s["r_turned"], t + 1)
                    if t >= 2:
                        act.wait_ge(s["r_logit"], t - 1)
                    nc.scalar.copy(h2T[t % 2][:].rearrange("p k n -> p (k n)"), psum[:, (t % 2) * 1024:(t % 2) * 1024 + 1024]).then_inc(s["r_out"], 1)
                act.wait_ge(s["r_logit"], TILES)
                nc.scalar.copy(logits_T[0:NR, :], psum[0:NR, LG_T:LG_T + TOK]).then_inc(s["r_lg_out"], 1)
                act.wait_ge(s["r_g_max"], 1)
                nc.scalar.activation(rsub[:], rsub[:], ACT.Exp).then_inc(s["r_e_sum"], 1)
                act.wait_ge(s["r_e_dif"], 1)
                nc.scalar.activation(wexp[:], v2[:], ACT.Exp).then_inc(s["r_e_w"], 1)
                act.wait_ge(s["e_gu_in0"], 16)
                nc.scalar.copy(gu_hi[0][:], gu_raw[0][:]).then_inc(s["e_gu_hi0"], 1)

            @block.gpsimd
            def _(pool):
                pool.wait_ge(s["r_consts"], 16)
                nc.gpsimd.tensor_copy(before_r[:], tabs["before"]).then_inc(s["r_tabs"], 1)
                nc.gpsimd.tensor_copy(ones_r[:], ones[:]).then_inc(s["r_tabs"], 1)
                pool.wait_ge(s["r_rows_out"], 4)
                for t in range(TILES):
                    pool.wait_ge(s["r_h2_d"], t + 1)
                    nc.gpsimd.tensor_tensor(h2[:, t, :], h2[:, t, :], rowb[:, 2 + (t >= CTX_TILES), :], ALU.add).then_inc(s["r_h2_a"], 1)
                pool.wait_ge(s["e_gu_hi0"], 1)
                nc.gpsimd.tensor_tensor(gu_lo[0][:], gu_raw[0][:], gu_hi[0][:], ALU.subtract).then_inc(s["e_gu_lp0"], 1)

            @block.vector
            def _(dve):
                own = Tally(dve, s["r_dve_c"])
                tt, ts = nc.vector.tensor_tensor, nc.vector.tensor_scalar
                def row_out(r):
                    dve.wait_ge(s["r_rows"], r + 1)
                    nc.vector.tensor_copy(rowb[:, r, :], psum[:, r % 4 * 1024:r % 4 * 1024 + 1024]).then_inc(s["r_rows_out"], 1)
                for t in range(SQ_DVE):
                    nc.vector.scalar_tensor_tensor(h2[:, t, :], x1[:, t, :], 1.0, x1[:, t, :], ALU.mult, ALU.mult,
                                                   accum_out=ssq[:, t:t + 1]).then_inc(s["r_sq_d"], 1)
                for r in range(4):
                    row_out(r)
                dve.wait_ge(s["r_rows_out"], 4)
                dve.wait_ge(s["r_rt"], 1)
                own.step(ts(nsq[:], ssq[:], 1.0 / D, EPS, ALU.mult, ALU.add))
                own.step(nc.vector.reciprocal(rstd[:], rstd[:]))
                own.step(tt(ntmp[:], rstd[:], rstd[:], ALU.mult))
                own.step(tt(ntmp[:], ntmp[:], nsq[:], ALU.mult))
                own.step(ts(ntmp[:], ntmp[:], -0.5, 1.5, ALU.mult, ALU.add))
                own.step(tt(rstd[:], rstd[:], ntmp[:], ALU.mult))
                for t in range(TILES):
                    nc.vector.scalar_tensor_tensor(h2[:, t, :], x1[:, t, :], rstd[:, t:t + 1], rowb[:, int(t >= CTX_TILES), :],
                                                   ALU.mult, ALU.mult).then_inc(s["r_h2_d"], 1)
                dve.wait_ge(s["r_lg_turned"], 1)
                own.step(nc.vector.tensor_copy(logits[:], psum[:, LG:LG + TILES * NR].rearrange("p (t n) -> p t n", n=NR)))
                dve.wait_ge(s["r_consts"], 16)
                g4 = [P, TILES, EG]
                desc = tabs["desc"].unsqueeze(1).broadcast_to(g4)

                def first_max(hot, eq, x, top):
                    own.step(nc.vector.reduce_max(top, x, AX.X))
                    own.step(tt(eq[:], x, top.unsqueeze(2).broadcast_to(g4), ALU.is_equal))
                    own.step(tt(eq[:], eq[:], desc, ALU.mult))
                    own.step(nc.vector.reduce_max(rsum[:], eq[:], AX.X))
                    own.step(tt(hot[:], eq[:], rsum[:].unsqueeze(2).broadcast_to(g4), ALU.is_equal))
                gl = logits[:, :, 0:EG]
                first_max(gsel, geq, gl, gmax[:])
                own.step(tt(rsub[:], gl, gmax[:].unsqueeze(2).broadcast_to(g4), ALU.subtract))
                dve.sem_inc(s["r_g_max"], 1)
                el = logits[:, :, EG:NR].rearrange("p t (g e) -> p t g e", e=EPG)
                g44 = [P, TILES, EG, EPG]
                own.step(tt(by_expert[:], el, gsel[:].unsqueeze(3).broadcast_to(g44), ALU.mult))
                own.step(nc.vector.reduce_sum(e_in[:], by_expert[:].rearrange("p t g e -> p t e g"), AX.X))
                first_max(pick[0], eeq, e_in[:], v1[:])
                own.step(ts(rest[:], pick[0][:], -1.0, 1.0, ALU.mult, ALU.add))
                own.step(tt(rest[:], rest[:], e_in[:], ALU.mult))
                own.step(ts(e_in[:], pick[0][:], -3.0e38, None, ALU.mult))
                own.step(tt(rest[:], rest[:], e_in[:], ALU.add))
                first_max(pick[1], eeq, rest[:], v2[:])
                own.step(tt(v2[:], v2[:], v1[:], ALU.subtract))
                dve.sem_inc(s["r_e_dif"], 1)
                for c in range(2):
                    own.step(tt(chosen[c][:], gsel[:].unsqueeze(3).broadcast_to(g44), pick[c][:].unsqueeze(2).broadcast_to(g44), ALU.mult))
                own.step(tt(either[:], chosen[0][:].rearrange("p t g e -> p t (g e)"), chosen[1][:].rearrange("p t g e -> p t (g e)"), ALU.add))
                dve.sem_inc(s["r_mask"], 1)
                for r in range(4, 6):
                    row_out(r)
                dve.wait_ge(s["r_e_sum"], 1)
                own.step(nc.vector.reduce_sum(psel[:], rsub[:], AX.X))
                own.step(nc.vector.reciprocal(psel[:], psel[:]))
                dve.wait_ge(s["r_e_w"], 1)
                own.step(ts(v1[:], wexp[:], 1.0, None, ALU.add))
                own.step(nc.vector.reciprocal(v1[:], v1[:]))
                own.step(tt(w_top[:, 0, :], v1[:], psel[:], ALU.mult))
                own.step(tt(w_top[:, 1, :], w_top[:, 0, :], wexp[:], ALU.mult))
                dve.wait_ge(s["r_ranks"], 1)
                own.step(nc.vector.tensor_copy(count[:], psum[:, COUNTS:COUNTS + NE]))
                own.step(tt(fills[:], count[:].unsqueeze(2).broadcast_to([P, NE, TILES]),
                            tabs["tile0"].unsqueeze(1).broadcast_to([P, NE, TILES]), ALU.is_gt))
                own.step(nc.vector.reduce_sum(n_tiles[:], fills[:], AX.X))
                own.step(tt(sums[:], tabs["upto"].rearrange("p (e f) -> p e f", f=NE), n_tiles[:].unsqueeze(1).broadcast_to([P, NE, NE]), ALU.mult))
                own.step(nc.vector.reduce_sum(ends[:], sums[:], AX.X))
                own.step(tt(starts[:], ends[:], n_tiles[:], ALU.subtract))
                te = [P, TILES, NE]
                rank = psum[:, RANKS:RANKS + TILES * NE].rearrange("p (t e) -> p t e", e=NE)
                own.step(ts(starts[:], starts[:], float(P), float(P * (HOMES - HOME)), ALU.mult, ALU.add))
                own.step(tt(starts[:], starts[:], tabs["home"], ALU.subtract))
                own.step(ts(beyond[:], rank, float(HOME * P), None, ALU.is_ge))
                own.step(tt(beyond[:], beyond[:], starts[:].unsqueeze(1).broadcast_to(te), ALU.mult))
                own.step(tt(place[:], rank, tabs["home"].unsqueeze(1).broadcast_to(te), ALU.add))
                own.step(tt(place[:], place[:], beyond[:], ALU.add))
                for c in range(2):
                    x = by_expert[:].rearrange("p t g e -> p t (g e)")
                    own.step(tt(x, place[:], chosen[c][:].rearrange("p t g e -> p t (g e)"), ALU.mult))
                    own.step(nc.vector.reduce_sum(pos[:, c, :], x, AX.X))
                flat = pos[:].rearrange("p c t -> p (c t)")
                ab = [P, 2 * TILES, SLOTS]
                own.step(tt(above[:], flat.unsqueeze(2).broadcast_to(ab), tabs["slot0"].unsqueeze(1).broadcast_to(ab), ALU.is_ge))
                own.step(nc.vector.reduce_sum(posA[:], above[:], AX.X))
                own.step(ts(posA[:], posA[:], -1.0, None, ALU.add))
                own.step(ts(posB[:], posA[:], -float(P), None, ALU.mult))
                own.step(tt(posB[:], posB[:], flat, ALU.add))
                own.step(tt(hotA[:], posA[:].unsqueeze(2).broadcast_to(ab), tabs["slot"].unsqueeze(1).broadcast_to(ab), ALU.is_equal))
                for c in range(2):
                    v = hotA[:, c * TILES:(c + 1) * TILES, :]
                    own.step(tt(v, v, tabs["token"].unsqueeze(2).broadcast_to([P, TILES, SLOTS]), ALU.mult))
                bb = [P, 2 * TILES, P]
                own.step(tt(hotB[:], posB[:].unsqueeze(2).broadcast_to(bb), tabs["col"].unsqueeze(1).broadcast_to(bb), ALU.is_equal))
                dve.sem_inc(s["r_onehot"], 1)
                own.step(tt(past[:], tabs["slot"][:, 0:SPARE].unsqueeze(2).broadcast_to([P, SPARE, NE]),
                            ends[:].unsqueeze(1).broadcast_to([P, SPARE, NE]), ALU.is_ge))
                own.step(nc.vector.reduce_sum(owner[:], past[:], AX.X))
                own.step(ts(owner[:], owner[:], float(NE - 1), float(P), ALU.min, ALU.mult))
                own.step(tt(owner[:], owner[:], tabs["row"].broadcast_to([P, SPARE]), ALU.add))
                own.step(nc.vector.tensor_copy(wrow[:], owner[:]))
                own.step(nc.vector.tensor_copy(n_spare[:], ends[:, NE - 1:NE]))
                own.step(nc.vector.tensor_copy(place_i[:], pos[:]))
                dve.wait_ge(s["r_ids_ps"], 1)
                own.step(nc.vector.tensor_copy(ids[:], psum[:, IDS:IDS + SLOTS]))
        if last_block == 4:
            return dict(h2=h2, logits=logits, ids=ids, wrow=wrow, place_i=place_i, w_top=w_top, rowb=rowb)

        with nc.Block() as block:
            @block.sync
            def _(sp):
                def load_gu(i, q):
                    sp.wait_ge(s["e_gu"], 4 * i + 2 * q - 2)
                    sp.dma_start(gu_raw[q][:], w_gu[bass.ds(2 * i + q, 1)].rearrange("o p k n -> p (o k) n")).then_inc(s[f"e_gu_in{q}"], 16)

                def load_dn(i, q):
                    sp.wait_ge(s["e_down"], 4 * i + 2 * q - 2)
                    sp.dma_start(dn_raw[q][:], w_dn[bass.ds(2 * i + q, 1)].rearrange("o p k n -> p (o k) n")).then_inc(s[f"e_dn_in{q}"], 16)

                def store(i, r):
                    a = 4 * i + r
                    sp.wait_ge(s["e_y_a"], a + 1)
                    sp.wait_ge(s["e_y_d"], a + 1)
                    sp.dma_start(io["ybuf"][bass.ds(a * P, P), :], yst[r % 2][:]).then_inc(s[f"e_y_st{r % 2}"], 16)
                sp.wait_ge(s["e_xg1"], 16)
                for q in range(2):
                    sp.dma_start(dn_raw[q][:], w_dn[q:q + 1].rearrange("o p k n -> p (o k) n")).then_inc(s[f"e_dn_in{q}"], 16)
                with sp.Fori(0, NE // 2 - 1) as i:
                    for q in range(2):
                        load_gu(i + 1, q)
                        store(i, 2 * q)
                        load_dn(i + 1, q)
                        store(i, 2 * q + 1)
                for r in range(4):
                    store(NE // 2 - 1, r)
                for j in range(2):
                    sp.wait_ge(s[f"e_y_st{j}"], 16 * NE)

            @block.gpsimd
            def _(pool):
                own = Tally(pool, s["e_pool_c"])

                def load_x(a, j):
                    pass_wait(pool)
                    own.step(nc.gpsimd.tensor_copy(x_row[j][:], ids[:, bass.ds(a, 1)]))
                    pass_wait(pool)
                    nc.gpsimd.indirect_dma_start(xg[j][:], None, io["h2d"], bass.IndirectOffsetOnAxis(x_row[j][:], 0)).then_inc(s[f"e_xg{j}"], 16)

                def gu_low(i, q):
                    pool.wait_ge(s[f"e_gu_hi{q}"], i + 1)
                    nc.gpsimd.tensor_tensor(gu_lo[q][:, GU_DVE:KC, :], gu_raw[q][:, GU_DVE:KC, :], gu_hi[q][:, GU_DVE:KC, :], ALU.subtract).then_inc(s[f"e_gu_lp{q}"], 1)
                load_x(0, 0)
                load_x(1, 1)
                for a in range(2):
                    pool.wait_ge(s["e_turned"], a + 1)
                    load_x(a + 2, a)
                gu_low(0, 1)
                with pool.Fori(0, NE // 2 - 1) as i:
                    own.enter(i, 4)
                    for r in range(4):
                        pool.wait_ge(s["e_turned"], 4 * i + r + 3)
                        load_x(4 * i + r + 4, r % 2)
                        if r % 2:
                            gu_low(i + 1, r // 2)
                    own.leave(NE // 2 - 1)

            @block.tensor
            def _(pe):
                def turn(i, r):
                    a, j = 4 * i + r, r % 2
                    pe.wait_ge(s[f"e_xg{j}"], 32 * i + 16 * (r // 2) + 16)
                    pe.wait_ge(s["e_x_lo"], a)
                    for k in range(KC):
                        mm = pe.transpose(psum[:, XT_PS + k * P:XT_PS + (k + 1) * P], xg[j][:, k * P:(k + 1) * P], ident[:])
                    mm.then_inc(s["e_turned"], 1)

                def gate_up(i, r):
                    i, r = i + r // 4, r % 4
                    a, j, q = 4 * i + r, r % 2, r // 2
                    o = psum[:, GU_PS[j]:GU_PS[j] + 2 * FE]
                    pe.wait_ge(s[f"e_gu_hi{q}"], i + 1)
                    pe.wait_ge(s["e_x_hi"], a + 1)
                    if not isinstance(i, int) or a >= 2:
                        pe.wait_ge(s["e_hid"], a - 1)
                    for k in range(KC):
                        pe.matmul(o, x_hi[j][:, k, :], gu_hi[q][:, k, :], start=(k == 0), stop=False)
                    pe.wait_ge(s["e_x_lo"], a + 1)
                    for k in range(KC):
                        pe.matmul(o, x_lo[j][:, k, :], gu_hi[q][:, k, :], start=False, stop=False)
                    pe.wait_ge(s[f"e_gu_lo{q}"], i + 1)
                    pe.wait_ge(s[f"e_gu_lp{q}"], i + 1)
                    for k in range(KC):
                        mm = pe.matmul(o, x_hi[j][:, k, :], gu_lo[q][:, k, :], start=False, stop=(k == KC - 1))
                    mm.then_inc(s["e_gu"], 1)

                def turn_hidden(i, r):
                    a, j = 4 * i + r, r % 2
                    pe.wait_ge(s["e_hid"], a + 1)
                    pe.wait_ge(s["e_hid_lo"], a)
                    for c in range(2):
                        mm = pe.transpose(psum[:, HT_PS + c * P:HT_PS + (c + 1) * P], hid[j][:, c * P:(c + 1) * P], ident[:])
                    mm.then_inc(s["e_hid_turned"], 1)

                def down(i, r):
                    a, j, q = 4 * i + r, r % 2, r // 2
                    pe.wait_ge(s[f"e_dn_hi{q}"], i + 1)
                    pe.wait_ge(s[f"e_dn_lo{q}"], i + 1)
                    pe.wait_ge(s["e_hid_hi"], a + 1)
                    pe.wait_ge(s["e_y_a"], a)
                    pe.wait_ge(s["e_y_d"], a)
                    for n, (x, w) in enumerate(((hid_hi, dn_hi), (hid_hi, dn_lo), (hid_lo, dn_hi))):
                        if n == 2:
                            pe.wait_ge(s["e_hid_lo"], a + 1)
                        for h in range(2):
                            for c in range(2):
                                mm = pe.matmul(psum[:, Y_PS + 512 * h:Y_PS + 512 * (h + 1)], x[j][:, c, :], w[q][:, c, 512 * h:512 * (h + 1)],
                                               start=(n == 0 and c == 0), stop=(n == 2 and c == 1))
                    mm.then_inc(s["e_down"], 1)

                def step(i, r, more=2):
                    if more > 0:
                        gate_up(i, r + 1)
                    turn_hidden(i, r)
                    if more > 1:
                        turn(i + (r + 2) // 4, (r + 2) % 4)
                    down(i, r)
                turn(0, 0)
                turn(0, 1)
                gate_up(0, 0)
                over_steps(pe, step)

            @block.scalar
            def _(act):
                def x_high(i, r):
                    a = 4 * i + r
                    act.wait_ge(s["e_turned"], a + 1)
                    if not isinstance(i, int) or a >= 2:
                        act.wait_ge(s["e_gu"], a - 1)
                    nc.scalar.copy(x_hi[r % 2][:].rearrange("p k n -> p (k n)"), psum[:, XT_PS:XT_PS + D]).then_inc(s["e_x_hi"], 1)

                def sigmoid(i, r):
                    i, r = i + r // 4, r % 4
                    a, j = 4 * i + r, r % 2
                    act.wait_ge(s["e_gu"], a + 1)
                    if not isinstance(i, int) or a >= 2:
                        act.wait_ge(s["e_hid"], a - 1)
                    nc.scalar.activation(sig[j][:], psum[:, GU_PS[j]:GU_PS[j] + FE], ACT.Sigmoid).then_inc(s["e_sig"], 1)

                def hidden_high(i, r):
                    act.wait_ge(s["e_hid_turned"], 4 * i + r + 1)
                    nc.scalar.copy(hid_hi[r % 2][:].rearrange("p c n -> p (c n)"), psum[:, HT_PS:HT_PS + FE]).then_inc(s["e_hid_hi"], 1)

                def y_out(i, r):
                    act.wait_ge(s["e_down"], 4 * i + r + 1)
                    act.wait_ge(s[f"e_y_st{r % 2}"], 32 * i + 16 * (r // 2))
                    nc.scalar.copy(yst[r % 2][:, 0:512], psum[:, Y_PS:Y_PS + 512]).then_inc(s["e_y_a"], 1)

                def gu_high(i, q):
                    act.wait_ge(s[f"e_gu_in{q}"], 16 * (i + 1))
                    nc.scalar.copy(gu_hi[q][:], gu_raw[q][:]).then_inc(s[f"e_gu_hi{q}"], 1)

                def dn_high(i, q):
                    act.wait_ge(s[f"e_dn_in{q}"], 16 * (i + 1))
                    nc.scalar.copy(dn_hi[q][:], dn_raw[q][:]).then_inc(s[f"e_dn_hi{q}"], 1)

                def step(i, r, more=2):
                    hidden_high(i, r)
                    if more > 1:
                        x_high(i + (r + 2) // 4, (r + 2) % 4)
                    if more > 0:
                        sigmoid(i, r + 1)
                    y_out(i, r)
                    if r % 2 and not isinstance(i, int):
                        gu_high(i + 1, r // 2)
                    if r % 2 == 0 and more > 1:
                        dn_high(i + (r + 2) // 4, (r + 2) // 2 % 2)
                x_high(0, 0)
                x_high(0, 1)
                dn_high(0, 0)
                gu_high(0, 1)
                sigmoid(0, 0)
                over_steps(act, step)

            @block.vector
            def _(dve):
                tt = nc.vector.tensor_tensor

                def x_low(i, r):
                    dve.wait_ge(s["e_x_hi"], 4 * i + r + 1)
                    v = "p k n -> p (k n)"
                    tt(x_lo[r % 2][:].rearrange(v), psum[:, XT_PS:XT_PS + D], x_hi[r % 2][:].rearrange(v), ALU.subtract).then_inc(s["e_x_lo"], 1)

                def hidden(i, r):
                    i, r = i + r // 4, r % 4
                    a, j = 4 * i + r, r % 2
                    dve.wait_ge(s["e_sig"], a + 1)
                    tt(sig[j][:], sig[j][:], psum[:, GU_PS[j]:GU_PS[j] + FE], ALU.mult).then_inc(s["e_hid_s"], 1)
                    dve.wait_ge(s["e_hid_s"], a + 1)
                    if not isinstance(i, int) or a >= 2:
                        dve.wait_ge(s["e_hid_turned"], a - 1)
                    tt(hid[j][:], sig[j][:], psum[:, GU_PS[j] + FE:GU_PS[j] + 2 * FE], ALU.mult).then_inc(s["e_hid"], 1)

                def hidden_low(i, r):
                    dve.wait_ge(s["e_hid_hi"], 4 * i + r + 1)
                    v = "p c n -> p (c n)"
                    tt(hid_lo[r % 2][:].rearrange(v), psum[:, HT_PS:HT_PS + FE], hid_hi[r % 2][:].rearrange(v), ALU.subtract).then_inc(s["e_hid_lo"], 1)

                def y_out(i, r):
                    dve.wait_ge(s["e_down"], 4 * i + r + 1)
                    dve.wait_ge(s[f"e_y_st{r % 2}"], 32 * i + 16 * (r // 2))
                    nc.vector.tensor_copy(yst[r % 2][:, 512:1024], psum[:, Y_PS + 512:Y_PS + 1024]).then_inc(s["e_y_d"], 1)

                def gu_low(i, q):
                    dve.wait_ge(s[f"e_gu_hi{q}"], i + 1)
                    tt(gu_lo[q][:, 0:GU_DVE, :], gu_raw[q][:, 0:GU_DVE, :], gu_hi[q][:, 0:GU_DVE, :], ALU.subtract).then_inc(s[f"e_gu_lo{q}"], 1)

                def dn_low(i, q):
                    dve.wait_ge(s[f"e_dn_hi{q}"], i + 1)
                    tt(dn_lo[q][:], dn_raw[q][:], dn_hi[q][:], ALU.subtract).then_inc(s[f"e_dn_lo{q}"], 1)

                def step(i, r, more=2):
                    hidden_low(i, r)
                    if more > 1:
                        x_low(i + (r + 2) // 4, (r + 2) % 4)
                    if more > 0:
                        hidden(i, r + 1)
                    y_out(i, r)
                    if r % 2 and not isinstance(i, int):
                        gu_low(i + 1, r // 2)
                    if r % 2 == 0 and more > 1:
                        dn_low(i + (r + 2) // 4, (r + 2) // 2 % 2)
                dve.sem_inc(s["e_gu_lo0"], 1)
                x_low(0, 0)
                x_low(0, 1)
                dn_low(0, 0)
                gu_low(0, 1)
                hidden(0, 0)
                over_steps(dve, step)

        def if_spare(eng, body):
            n = eng.value_load(n_spare[0:1, 0:1], min_val=0, max_val=SPARE)
            with eng.If(n > 0):
                body()

        with nc.Block() as block:
            @block.gpsimd
            def _(pool):
                own = Tally(pool, s["o_pool_c"])

                def body():
                    with pool.Fori(0, SPARE) as i:
                        own.enter(i, 2)
                        pool.wait_ge(s["o_y"], i)
                        pass_wait(pool)
                        own.step(nc.gpsimd.tensor_copy(x_row[0][:], ids[:, bass.ds(i + HOMES, 1)]))
                        own.step(nc.gpsimd.tensor_copy(x_row[1][:], wrow[:, bass.ds(i, 1)]))
                        for dst, rows, index in ((xg[0][:], io["h2d"], x_row[0]), (gu_raw[0][:].rearrange("p k n -> p (k n)"), io["w_gu"], x_row[1]),
                                                 (dn_raw[0][:].rearrange("p k n -> p (k n)"), io["w_dn"], x_row[1])):
                            pass_wait(pool)
                            nc.gpsimd.indirect_dma_start(dst, None, rows, bass.IndirectOffsetOnAxis(index[:], 0)).then_inc(s["o_in"], 16)
                        own.leave(SPARE)
                if_spare(pool, body)

            @block.tensor
            def _(pe):
                def body():
                    with pe.Fori(0, SPARE) as i:
                        pe.wait_ge(s["o_in"], 48 * i + 48)
                        for k in range(KC):
                            mm = pe.transpose(psum[:, XT_PS + k * P:XT_PS + (k + 1) * P], xg[0][:, k * P:(k + 1) * P], ident[:])
                        mm.then_inc(s["o_turned"], 1)
                        pe.wait_ge(s["o_xT"], i + 1)
                        for k in range(KC):
                            mm = pe.matmul(psum[:, GU_PS[0]:GU_PS[0] + 2 * FE], xT[:, k, :], gu_raw[0][:, k, :], start=(k == 0), stop=(k == KC - 1))
                        mm.then_inc(s["o_gu"], 1)
                        pe.wait_ge(s["o_hid"], i + 1)
                        for c in range(2):
                            mm = pe.transpose(psum[:, HT_PS + c * P:HT_PS + (c + 1) * P], hid[0][:, c * P:(c + 1) * P], ident[:])
                        mm.then_inc(s["o_hid_turned"], 1)
                        pe.wait_ge(s["o_hidT"], i + 1)
                        for h in range(2):
                            for c in range(2):
                                mm = pe.matmul(psum[:, Y_PS + 512 * h:Y_PS + 512 * (h + 1)], hidT[:, c, :], dn_raw[0][:, c, 512 * h:512 * (h + 1)],
                                               start=(c == 0), stop=(c == 1))
                        mm.then_inc(s["o_down"], 1)
                if_spare(pe, body)

            @block.scalar
            def _(act):
                def body():
                    with act.Fori(0, SPARE) as i:
                        act.wait_ge(s["o_turned"], i + 1)
                        nc.scalar.copy(xT[:].rearrange("p k n -> p (k n)"), psum[:, XT_PS:XT_PS + D]).then_inc(s["o_xT"], 1)
                        act.wait_ge(s["o_gu"], i + 1)
                        nc.scalar.activation(sig[0][:], psum[:, GU_PS[0]:GU_PS[0] + FE], ACT.Sigmoid).then_inc(s["o_sig"], 1)
                        act.wait_ge(s["o_hid_turned"], i + 1)
                        nc.scalar.copy(hidT[:].rearrange("p c n -> p (c n)"), psum[:, HT_PS:HT_PS + FE]).then_inc(s["o_hidT"], 1)
                        act.wait_ge(s["o_down"], i + 1)
                        act.wait_ge(s["o_y_st"], 16 * i)
                        nc.scalar.copy(yst[0][:], psum[:, Y_PS:Y_PS + D]).then_inc(s["o_y"], 1)
                if_spare(act, body)

            @block.vector
            def _(dve):
                def body():
                    with dve.Fori(0, SPARE) as i:
                        dve.wait_ge(s["o_sig"], i + 1)
                        nc.vector.tensor_tensor(sig[0][:], sig[0][:], psum[:, GU_PS[0]:GU_PS[0] + FE], ALU.mult).then_inc(s["o_hid_s"], 1)
                        dve.wait_ge(s["o_hid_s"], i + 1)
                        nc.vector.tensor_tensor(hid[0][:], sig[0][:], psum[:, GU_PS[0] + FE:GU_PS[0] + 2 * FE], ALU.mult).then_inc(s["o_hid"], 1)
                if_spare(dve, body)

            @block.sync
            def _(sp):
                def body():
                    with sp.Fori(0, SPARE) as i:
                        sp.wait_ge(s["o_y"], i + 1)
                        sp.dma_start(io["ybuf"][bass.ds(i * P + HOMES * P, P), :], yst[0][:]).then_inc(s["o_y_st"], 16)
                    sp.wait_ge(s["o_y_st"], 16 * SPARE)
                if_spare(sp, body)
        if last_block == 5:
            return dict(x1=x1)

        y1 = [at(f"y1_{t}", [P, D], F32, RKV + 4 * t * KB) for t in range(TILES)]
        y2 = [at(f"y2_{t}", [P, D], F32, RKV + (40 + 4 * t) * KB) for t in range(TILES)]
        final_g = at("final_g", [P, D], F32, RHL)
        junk = [at(f"junk{j}", [P, D], F32, RHL + (4 + 4 * j) * KB) for j in range(2)]
        AHEAD, HALF_D = 4, 3 * D // 4
        g_in = [sem(f"b6_g{t}") for t in range(AHEAD)]
        for n in "final w1 join gated sum_p sum_d sq rt normed st dve_c".split():
            s["f_" + n] = sem("b6_" + n)
        with nc.Block() as block:
            @block.gpsimd
            def _(pool):
                def gather(t):
                    for c, buf in enumerate((y1, y2)):
                        nc.gpsimd.indirect_dma_start(buf[t][:], None, io["ybuf"], bass.IndirectOffsetOnAxis(place_i[:, c, t:t + 1], 0)).then_inc(g_in[t % AHEAD], 16)
                for t in range(AHEAD):
                    gather(t)
                for t in range(TILES):
                    pool.wait_ge(s["f_gated"], t + 1)
                    v = x1[:, t, 0:HALF_D]
                    nc.gpsimd.tensor_tensor(v, v, y2[t][:, 0:HALF_D], ALU.add).then_inc(s["f_sum_p"], 1)
                    if t + AHEAD < TILES:
                        gather(t + AHEAD)

            @block.scalar
            def _(act):
                def weigh(t):
                    act.wait_ge(g_in[t % AHEAD], 32 * (t // AHEAD + 1))
                    nc.scalar.mul(y1[t][:], y1[t][:], w_top[:, 0, t:t + 1]).then_inc(s["f_w1"], 1)
                for t in range(2):
                    weigh(t)
                for t in range(TILES):
                    if t + 2 < TILES:
                        weigh(t + 2)
                    act.wait_ge(s["f_sum_p"], t + 1)
                    act.wait_ge(s["f_sum_d"], t + 1)
                    nc.scalar.activation(junk[t % 2][:], x1[:, t, :], ACT.Square, accum_out=ssq[:, t:t + 1]).then_inc(s["f_sq"], 1)
                    act.wait_ge(s["f_sq"], t + 1)
                    nc.scalar.activation(rstd[:, t:t + 1], ssq[:, t:t + 1], ACT.Sqrt, bias=eps[:], scale=1.0 / D).then_inc(s["f_rt"], 1)

            @block.vector
            def _(dve):
                own = Tally(dve, s["f_dve_c"])
                tt, ts = nc.vector.tensor_tensor, nc.vector.tensor_scalar

                def join(t):
                    dve.wait_ge(s["f_w1"], t + 1)
                    nc.vector.scalar_tensor_tensor(y2[t][:], y2[t][:], w_top[:, 1, t:t + 1], y1[t][:], ALU.mult, ALU.add).then_inc(s["f_join"], 1)
                    dve.wait_ge(s["f_join"], t + 1)
                    tt(y2[t][:], y2[t][:], rowb[:, 4 + (t >= CTX_TILES), :], ALU.mult).then_inc(s["f_gated"], 1)
                    dve.wait_ge(s["f_gated"], t + 1)
                    v = x1[:, t, HALF_D:D]
                    tt(v, v, y2[t][:, HALF_D:D], ALU.add).then_inc(s["f_sum_d"], 1)

                def finish(t):
                    dve.wait_ge(s["f_rt"], t + 2)
                    r, a, b = rstd[:, t:t + 2], nsq[:, t:t + 2], ntmp[:, t:t + 2]
                    own.step(ts(a, ssq[:, t:t + 2], 1.0 / D, EPS, ALU.mult, ALU.add))
                    own.step(nc.vector.reciprocal(r, r))
                    own.step(tt(b, r, r, ALU.mult))
                    own.step(tt(b, b, a, ALU.mult))
                    own.step(ts(b, b, -0.5, 1.5, ALU.mult, ALU.add))
                    own.step(tt(r, r, b, ALU.mult))
                    for u in (t, t + 1):
                        nc.vector.scalar_tensor_tensor(x1[:, u, :], x1[:, u, :], rstd[:, u:u + 1], final_g[:], ALU.mult, ALU.mult).then_inc(s["f_normed"], 1)
                dve.wait_ge(s["f_final"], 16)
                for t in range(TILES):
                    join(t)
                    if t >= 3 and t % 2:
                        finish(t - 3)
                finish(TILES - 2)

            @block.sync
            def _(sp):
                sp.dma_start(final_g[:], io["final_g"].broadcast_to([P, D])).then_inc(s["f_final"], 16)
                for t in range(TILES):
                    sp.wait_ge(s["f_normed"], t + 1)
                    sp.dma_start(io["y"][t * P:(t + 1) * P, :], x1[:, t, :]).then_inc(s["f_st"], 16)
                sp.wait_ge(s["f_st"], 16 * TILES)
        return {}


ROUTE_TABLES = [("desc", EG), ("before", P), ("tile0", TILES), ("upto", NE * NE), ("home", NE), ("slot0", SLOTS), ("slot", SLOTS), ("token", TILES),
                ("col", P), ("row", 1)]
ROUTE_W = sum(w for _, w in ROUTE_TABLES)


def route_tables():
    p, rep = np.arange(P), lambda v: np.broadcast_to(np.asarray(v).reshape(1, -1), (P, np.size(v)))
    tabs = {
        "desc": rep(np.arange(EG, 0, -1)),
        "before": p[:, None] < p[None, :],
        "tile0": rep(np.where(np.arange(TILES) < HOME, 2 * TOK, np.arange(TILES) * P)),
        "home": rep(np.arange(NE) * HOME * P),
        "upto": rep(np.arange(NE)[None, :] <= np.arange(NE)[:, None]),
        "slot0": rep(np.arange(SLOTS) * P), "slot": rep(np.arange(SLOTS)),
        "token": np.arange(TILES)[None, :] * P + p[:, None],
        "col": rep(p), "row": p[:, None],
    }
    return np.ascontiguousarray(np.concatenate([tabs[n].astype(np.float32) for n, _ in ROUTE_TABLES], axis=1))


def rope_tables():
    t = np.arange(LAT)
    nf = HD // 4
    freq = THETA ** (-np.arange(nf, dtype=np.float32) / np.float32(nf))
    pos = np.stack([t // GRID_W, t % GRID_W]).astype(np.float32)
    ang = (pos[:, None, :] * freq.astype(np.float32)[None, :, None]).astype(np.float32)
    c, s = np.cos(ang), np.sin(ang)
    cos = np.concatenate([c[0], c[0], c[1], c[1]]).astype(np.float32)
    sin = np.concatenate([s[0], -s[0], s[1], -s[1]]).astype(np.float32)
    return np.ascontiguousarray(cos), np.ascontiguousarray(sin)


def inverse_counts():
    out = np.zeros((4, TOK), np.float32)
    for g, w in enumerate((2, 4, 8, 16)):
        for o, l in STREAMS:
            t = np.arange(l)
            out[g, o:o + l] = 1.0 / (np.clip(t + w // 2, 0, l) - np.clip(t - w // 2, 0, l))
    return out


def layouts(a):
    c = np.ascontiguousarray
    pairs = lambda w: c(w.reshape(w.shape[0] // P, P, -1, PAIR).transpose(2, 1, 0, 3))
    cols = lambda v: v.reshape(-1, P).T
    order = [6, 7] + list(range(8, 16)) + [0, 1, 2, 3] + [4, 5]
    w_in = pairs(a["w_in"][0])[order]
    cos, sin = rope_tables()
    return {
        "x": c(np.concatenate([a["x_prompt"][0], a["x_sample"][0]]).reshape(TILES, P, D)),
        "cvec": c(np.stack([cols(a["c_ctx"]), cols(a["c"][0])], axis=2)),
        "vecs": c(np.concatenate([cols(a["b_ada"][0]), cols(a["norm1_g"][0]), cols(a["norm2_g"][0]), cols(a["q_norm_g"][0]),
                                  cols(a["k_norm_g"][0]), cols(a["pool_scale"][0])], axis=1)),
        "ident": np.eye(P, dtype=np.float32),
        "w_ada": pairs(a["w_ada"][0]), "w_in": c(w_in),
        "w_merge": pairs(np.concatenate([a["w_branch_a"][0], a["w_branch_b"][0]])), "w_out": pairs(a["w_out"][0]),
        "w_pool": c(a["w_pool"][0].transpose(1, 0, 2)),
        "icnt": inverse_counts(), "cos": cos, "sin": sin,
        "route": route_tables(),
        "w_route": c(np.concatenate([a["w_router_group"][0], a["w_router_expert"][0]], axis=1).reshape(KC, P, NR).transpose(1, 0, 2)),
        "w_gu": c(np.concatenate([a["w_exp_gate"][0], a["w_exp_up"][0]], axis=2).reshape(NE, KC, P, 2 * FE).transpose(0, 2, 1, 3).reshape(NE * P, -1)),
        "w_dn": c(a["w_exp_down"][0].reshape(NE, 2, P, D).transpose(0, 2, 1, 3).reshape(NE * P, -1)),
        "final_g": c(a["final_norm_g"][None, :]),
        "cache_k": c(a["cache_k"][0, 0].transpose(2, 1, 0)),
        "cache_v": c(a["cache_v"][0, 0].reshape(PAST // P, P, KV * HD).transpose(1, 0, 2)),
    }


def kernel(**inputs):
    import numpy as _np
    import concourse.bacc as _bacc
    from concourse import mybir as _mybir
    from concourse.bass_utils import run_bass_kernel_spmd as _run

    arrays = layouts({name: _np.asarray(a) for name, a in inputs.items()})
    nc = _bacc.Bacc("TRN2", target_bir_lowering=False, num_devices=1)
    f32 = _mybir.dt.float32
    io = {name: nc.dram_tensor("in_" + name, a.shape, f32, kind="ExternalInput").ap() for name, a in arrays.items()}
    for name, shape in (("y", (TOK, D)), ("out_k", (KV, HD, CTX)), ("out_v", (KV, HD, CTX))):
        io[name] = nc.dram_tensor(name, shape, f32, kind="ExternalOutput").ap()
    for name, shape in (("gates", (2 * KC, P, TOK)), ("poolT", (4, P, TOK)), ("h2d", (TOK, D)), ("ybuf", (SLOTS * P, D))):
        io[name] = nc.dram_tensor(name, shape, f32).ap()
    build(nc, io)
    r = _run(nc, [{"in_" + name: a for name, a in arrays.items()}], core_ids=[0]).results[0]
    cache = [r[name].transpose(2, 0, 1).reshape(1, 1, CTX, KV, HD) for name in ("out_k", "out_v")]
    return r["y"][:CTX].reshape(1, CTX, D), r["y"][CTX:].reshape(1, LAT, D), cache[0], cache[1]
```
